# Optimizing a Trainium2 kernel written in Bass

```python
import jax, jax.numpy as jnp
from jax import lax
import numpy as np
import math

D_MODEL = 2048
BATCH = 1
SEQ = 256
DEPTH = 1

N_HEADS_ATTN = 8
HEAD_DIM = 128
N_IDX_HEADS = 16
IDX_DIM = 64
TOPK_MAX = 256
Q_BLOCK = 128
N_RET_HEADS = 8
RET_QK_DIM = 128
RET_V_DIM = 256
RET_CHUNK = 128
N_MEM = 256
N_MEM_HEADS = 4
MEM_HEAD_DIM = 256
D_FF = -(-8 * D_MODEL // (3 * 256)) * 256
ROPE_THETA = 10000.0
EPS = 1e-6
N_BRANCHES = 3

A_WIDTH = N_HEADS_ATTN * HEAD_DIM
IDX_Q_WIDTH = N_IDX_HEADS * IDX_DIM
RET_QK_WIDTH = N_RET_HEADS * RET_QK_DIM
RET_V_WIDTH = N_RET_HEADS * RET_V_DIM
MEM_WIDTH = N_MEM_HEADS * MEM_HEAD_DIM
COL_SIZES = (A_WIDTH, A_WIDTH, A_WIDTH, IDX_Q_WIDTH, IDX_DIM, N_IDX_HEADS,
             RET_QK_WIDTH, RET_QK_WIDTH, RET_V_WIDTH, RET_V_WIDTH, MEM_WIDTH, N_BRANCHES * D_MODEL)
COL_SPLITS = tuple(sum(COL_SIZES[:i + 1]) for i in range(len(COL_SIZES) - 1))
IN_COLS = sum(COL_SIZES)


def rms_norm(x, g):
    xf = x.astype(jnp.float32)
    y = xf * lax.rsqrt(jnp.mean(xf * xf, axis=-1, keepdims=True) + EPS)
    return (y * g.astype(jnp.float32)).astype(x.dtype)

def rope(x, pos):
    d = x.shape[-1]
    freqs = ROPE_THETA ** (-jnp.arange(0, d, 2, dtype=jnp.float32) / d)
    ang = pos.astype(jnp.float32)[..., None] * freqs
    cos = jnp.cos(ang)[:, :, None, :]
    sin = jnp.sin(ang)[:, :, None, :]
    xf = x.astype(jnp.float32)
    x1, x2 = xf[..., : d // 2], xf[..., d // 2:]
    return jnp.concatenate([x1 * cos - x2 * sin, x2 * cos + x1 * sin], axis=-1).astype(x.dtype)

def dsa_attention(q, k, v, q_idx, k_idx, w_idx):
    B, S, H, dh = q.shape
    k_top = min(TOPK_MAX, S // 4)
    nb = S // Q_BLOCK

    def to_blocks(a):
        return jnp.moveaxis(a.reshape(B, nb, Q_BLOCK, *a.shape[2:]), 1, 0)

    t_blk = jnp.arange(S, dtype=jnp.int32).reshape(nb, Q_BLOCK)
    key_pos = jnp.arange(S, dtype=jnp.int32)
    gather = jax.vmap(lambda a, i: a[i])

    def block(args):
        qb, qib, wb, tb = args
        rel = jax.nn.relu(jnp.einsum('bqhd,bsd->bqhs', qib, k_idx))
        score = jnp.einsum('bqhs,bqh->bqs', rel, wb).astype(jnp.float32)
        causal = key_pos[None, None, :] <= tb[None, :, None]
        score = jnp.where(causal, score, -jnp.inf)
        _, idx = lax.top_k(score, k_top)
        valid = idx <= tb[None, :, None]
        ks = gather(k, idx)
        vs = gather(v, idx)
        logits = jnp.einsum('bqhd,bqkhd->bqhk', qb, ks).astype(jnp.float32)
        logits = jnp.where(valid[:, :, None, :], logits, -jnp.inf)
        p = jax.nn.softmax(logits, axis=-1).astype(v.dtype)
        return jnp.einsum('bqhk,bqkhd->bqhd', p, vs)

    out = lax.map(block, (to_blocks(q), to_blocks(q_idx), to_blocks(w_idx), t_blk))
    return jnp.moveaxis(out, 0, 1).reshape(B, S, H * dh)

def retention(q, k, v, g):
    B, S, H, dk = q.shape
    dv = v.shape[-1]
    C = RET_CHUNK
    n = S // C
    dt = v.dtype
    log_gamma = jnp.log1p(-jnp.exp2(-5.0 - jnp.arange(H, dtype=jnp.float32)))
    i = jnp.arange(C, dtype=jnp.float32)
    diff = i[:, None] - i[None, :]
    inner_decay = jnp.where(diff[None] >= 0,
                            jnp.exp(jnp.maximum(diff, 0.0)[None] * log_gamma[:, None, None]), 0.0)
    k_decay = jnp.exp((C - 1 - i)[None, :] * log_gamma[:, None])
    q_decay = jnp.exp((i + 1)[None, :] * log_gamma[:, None])
    chunk_decay = jnp.exp(C * log_gamma)

    qc = q.reshape(B, n, C, H, dk)
    kc = (k * dk ** -0.5).reshape(B, n, C, H, dk)
    vc = v.reshape(B, n, C, H, dv)

    scores = jnp.einsum('bnihd,bnjhd->bnhij', qc, kc) * inner_decay.astype(dt)
    inner = jnp.einsum('bnhij,bnjhe->bnihe', scores, vc)
    kv = jnp.einsum('bnjhd,bnjhe,hj->nbhde', kc, vc, k_decay.astype(dt)).astype(jnp.float32)

    def step(state, kv_n):
        return state * chunk_decay[None, :, None, None] + kv_n, state

    _, prev = lax.scan(step, jnp.zeros((B, H, dk, dv), jnp.float32), kv)
    cross = jnp.einsum('bnihd,nbhde->bnihe', qc, prev.astype(dt)) * \
        jnp.transpose(q_decay)[None, None, :, :, None].astype(dt)
    y = (inner + cross).reshape(B, S, H, dv).astype(jnp.float32)
    mu = jnp.mean(y, axis=-1, keepdims=True)
    var = jnp.mean(jnp.square(y - mu), axis=-1, keepdims=True)
    yn = ((y - mu) * lax.rsqrt(var + EPS)).astype(dt).reshape(B, S, H * dv)
    return jax.nn.silu(g) * yn

def memory_attention(q, k, v):
    B, S, H, d = q.shape
    logits = jnp.einsum('bshd,bmhd->bhsm', q, k).astype(jnp.float32)
    p = jax.nn.softmax(logits, axis=-1).astype(v.dtype)
    return jnp.einsum('bhsm,bmhd->bshd', p, v).reshape(B, S, H * d)

def first_inputs(seed: int = 0) -> dict:
    key = jax.random.key(seed)
    ks = jax.random.split(key, 16)

    def w(k, fan_in, fan_out):
        return jax.random.normal(k, (DEPTH, fan_in, fan_out), jnp.float32) * fan_in ** -0.5

    def gain(k):
        return 1.0 + 0.05 * jax.random.normal(k, (DEPTH, D_MODEL), jnp.float32)

    return {
        "x": jax.random.normal(ks[0], (BATCH, SEQ, D_MODEL), jnp.float32),
        "mem": jax.random.normal(ks[1], (BATCH, N_MEM, D_MODEL), jnp.float32),
        "positions": jnp.broadcast_to(jnp.arange(SEQ, dtype=jnp.int32), (BATCH, SEQ)),
        "g_pre_mix": gain(ks[2]),
        "g_mem": gain(ks[3]),
        "w_in": w(ks[4], D_MODEL, IN_COLS),
        "w_mem_kv": w(ks[5], D_MODEL, 2 * MEM_WIDTH),
        "w_branch_a": w(ks[6], A_WIDTH, D_MODEL),
        "w_branch_b": w(ks[7], RET_V_WIDTH, D_MODEL),
        "w_branch_c": w(ks[8], MEM_WIDTH, D_MODEL),
        "w_out": w(ks[9], D_MODEL, D_MODEL),
        "g_post_mix": gain(ks[10]),
        "g_pre_ffn": gain(ks[11]),
        "w_ffn_in": w(ks[12], D_MODEL, 2 * D_FF),
        "w_ffn_out": w(ks[13], D_FF, D_MODEL),
        "g_post_ffn": gain(ks[14]),
    }

def first_block(x, mem, positions, g_pre_mix, g_mem, w_in, w_mem_kv, w_branch_a, w_branch_b,
              w_branch_c, w_out, g_post_mix, g_pre_ffn, w_ffn_in, w_ffn_out, g_post_ffn):
    B, S, D = x.shape
    M = mem.shape[1]
    for l in range(DEPTH):
        h = rms_norm(x, g_pre_mix[l])
        proj = h @ w_in[l]
        (a_q, a_k, a_v, i_q, i_k, i_w, r_q, r_k, r_v, r_g, m_q, gate_logits) = \
            jnp.split(proj, COL_SPLITS, axis=-1)

        a_q = rope(a_q.reshape(B, S, N_HEADS_ATTN, HEAD_DIM), positions) * HEAD_DIM ** -0.5
        a_k = rope(a_k.reshape(B, S, N_HEADS_ATTN, HEAD_DIM), positions)
        a_v = a_v.reshape(B, S, N_HEADS_ATTN, HEAD_DIM)
        i_q = rope(i_q.reshape(B, S, N_IDX_HEADS, IDX_DIM), positions) * IDX_DIM ** -0.5
        i_k = rope(i_k.reshape(B, S, 1, IDX_DIM), positions)[:, :, 0, :]
        i_w = i_w * N_IDX_HEADS ** -0.5
        o_a = dsa_attention(a_q, a_k, a_v, i_q, i_k, i_w)

        r_q = rope(r_q.reshape(B, S, N_RET_HEADS, RET_QK_DIM), positions)
        r_k = rope(r_k.reshape(B, S, N_RET_HEADS, RET_QK_DIM), positions)
        r_v = r_v.reshape(B, S, N_RET_HEADS, RET_V_DIM)
        o_b = retention(r_q, r_k, r_v, r_g)

        mem_kv = rms_norm(mem, g_mem[l]) @ w_mem_kv[l]
        m_k, m_v = jnp.split(mem_kv, 2, axis=-1)
        m_k = m_k.reshape(B, M, N_MEM_HEADS, MEM_HEAD_DIM)
        m_v = m_v.reshape(B, M, N_MEM_HEADS, MEM_HEAD_DIM)
        m_q = m_q.reshape(B, S, N_MEM_HEADS, MEM_HEAD_DIM) * MEM_HEAD_DIM ** -0.5
        o_c = memory_attention(m_q, m_k, m_v)

        gates = jax.nn.sigmoid(gate_logits).reshape(B, S, N_BRANCHES, D)
        mixed = (gates[:, :, 0] * (o_a @ w_branch_a[l])
                 + gates[:, :, 1] * (o_b @ w_branch_b[l])
                 + gates[:, :, 2] * (o_c @ w_branch_c[l]))
        x = x + rms_norm(mixed @ w_out[l], g_post_mix[l])

        h2 = rms_norm(x, g_pre_ffn[l])
        f_gate, f_up = jnp.split(h2 @ w_ffn_in[l], 2, axis=-1)
        y2 = (jax.nn.silu(f_gate) * f_up) @ w_ffn_out[l]
        x = x + rms_norm(y2, g_post_ffn[l])
    return x


DEPTH_2 = 2

N_A = DEPTH_2 // 2
N_B = DEPTH_2 - N_A
SSM_WIDTH = D_MODEL
SSM_GROUP = 16
SSM_GROUPS = SSM_WIDTH // SSM_GROUP
SSM_STATE = 64
N_HEADS = 16
N_KV = 4
HPG = N_HEADS // N_KV
HEAD_DIM_2 = D_MODEL // N_HEADS
ATT_WIDTH = N_HEADS * HEAD_DIM_2
N_BRANCH = 3
CMP_LEN = 32
CMP_STRIDE = 16
SEL_LEN = 64
SEL_TOPK = 16
WINDOW = 512
WIN_QBLOCK = 128
SEL_QCHUNK = 32
SEL_BONUS = 1e3
NEG = -1e30


def rmsnorm(x, g):
    xf = x.astype(jnp.float32)
    y = xf * lax.rsqrt(jnp.mean(xf * xf, axis=-1, keepdims=True) + EPS)
    return (y * g.astype(jnp.float32)).astype(x.dtype)

def modulate(h, shift, scale):
    return h * (1.0 + scale[:, None, :]) + shift[:, None, :]

def masked_softmax(s, mask):
    s = jnp.where(mask, s.astype(jnp.float32), NEG)
    p = jax.nn.softmax(s, axis=-1)
    return jnp.where(mask, p, 0.0)

def s5_discretize(lam_re, lam_im, log_step, b_re, b_im):
    dt = jnp.exp(log_step.astype(jnp.float32))[:, None]
    lr, li = lam_re.astype(jnp.float32), lam_im.astype(jnp.float32)
    mag = jnp.exp(lr * dt)
    a_re, a_im = mag * jnp.cos(li * dt), mag * jnp.sin(li * dt)
    den = lr * lr + li * li
    coef_re = ((a_re - 1.0) * lr + a_im * li) / den
    coef_im = (a_im * lr - (a_re - 1.0) * li) / den
    br, bi = b_re.astype(jnp.float32), b_im.astype(jnp.float32)
    bb_re = coef_re[..., None] * br - coef_im[..., None] * bi
    bb_im = coef_re[..., None] * bi + coef_im[..., None] * br
    return a_re, a_im, bb_re, bb_im

def _ssm_combine(left, right):
    ar_i, ai_i, br_i, bi_i = left
    ar_j, ai_j, br_j, bi_j = right
    return (ar_j * ar_i - ai_j * ai_i,
            ar_j * ai_i + ai_j * ar_i,
            ar_j * br_i - ai_j * bi_i + br_j,
            ar_j * bi_i + ai_j * br_i + bi_j)

def _scan_one(a_re, a_im, bu_re, bu_im):
    out = lax.associative_scan(_ssm_combine, (a_re, a_im, bu_re, bu_im), axis=0)
    return out[2], out[3]

def s5_mixer(h, w_in, lam_re, lam_im, log_step, b_re, b_im, c_re, c_im, d_skip, w_glu, b_glu, w_out):
    B_, L, _ = h.shape
    u, z = jnp.split(h @ w_in, 2, axis=-1)
    ug = u.reshape(B_, L, SSM_GROUPS, SSM_GROUP).astype(jnp.float32)
    a_re, a_im, bb_re, bb_im = s5_discretize(lam_re, lam_im, log_step, b_re, b_im)
    bu_re = jnp.einsum('blgc,gnc->blgn', ug, bb_re)
    bu_im = jnp.einsum('blgc,gnc->blgn', ug, bb_im)
    shp = (L, SSM_GROUPS, SSM_STATE)
    x_re, x_im = jax.vmap(_scan_one, in_axes=(None, None, 0, 0))(
        jnp.broadcast_to(a_re, shp), jnp.broadcast_to(a_im, shp), bu_re, bu_im)
    y = (jnp.einsum('blgn,gcn->blgc', x_re, c_re.astype(jnp.float32))
         - jnp.einsum('blgn,gcn->blgc', x_im, c_im.astype(jnp.float32)))
    y = y + d_skip.astype(jnp.float32).reshape(SSM_GROUPS, SSM_GROUP) * ug
    y = jax.nn.gelu(y.reshape(B_, L, SSM_WIDTH).astype(h.dtype))
    y = y * jax.nn.sigmoid(y @ w_glu + b_glu)
    return (y * jax.nn.silu(z)) @ w_out

def compress_blocks(t, blk_idx, pe, w1, b1, w2, b2):
    blocks = t[:, blk_idx] + pe[None, None, :, None, :]
    B_, n = blocks.shape[:2]
    flat = jnp.moveaxis(blocks, 3, 2).reshape(B_, n, N_KV, CMP_LEN * HEAD_DIM_2)
    return jax.nn.gelu(flat @ w1 + b1) @ w2 + b2

def nsa_shared_kv(h_kv, w_kv, cmp_pe, cmp_w1, cmp_b1, cmp_w2, cmp_b2):
    B_, L, _ = h_kv.shape
    kv = (h_kv @ w_kv).reshape(B_, L, 2 * N_BRANCH, N_KV, HEAD_DIM_2)
    n_cmp = (L - CMP_LEN) // CMP_STRIDE + 1
    blk_idx = np.arange(n_cmp)[:, None] * CMP_STRIDE + np.arange(CMP_LEN)[None, :]
    kc = compress_blocks(kv[:, :, 0], blk_idx, cmp_pe[0], cmp_w1[0], cmp_b1[0], cmp_w2[0], cmp_b2[0])
    vc = compress_blocks(kv[:, :, 1], blk_idx, cmp_pe[1], cmp_w1[1], cmp_b1[1], cmp_w2[1], cmp_b2[1])
    return kc, vc, kv[:, :, 2], kv[:, :, 3], kv[:, :, 4], kv[:, :, 5]

def cmp_attention(q, kc, vc, pos):
    n_cmp = kc.shape[1]
    s = jnp.einsum('blghd,bngd->bghln', q, kc)
    blk_end = jnp.arange(n_cmp) * CMP_STRIDE + CMP_LEN - 1
    mask = blk_end[None, :] <= pos[:, None]
    p = masked_softmax(s, mask)
    o = jnp.einsum('bghln,bngd->blghd', p.astype(vc.dtype), vc)
    return o, p.sum(axis=2)

def selection_overlap(n_cmp, n_slc):
    c0 = np.arange(n_cmp)[:, None] * CMP_STRIDE
    s0 = np.arange(n_slc)[None, :] * SEL_LEN
    ov = np.clip(np.minimum(c0 + CMP_LEN, s0 + SEL_LEN) - np.maximum(c0, s0), 0, None)
    return (ov / CMP_STRIDE).astype(np.float32)

def select_blocks(p_cmp, pos):
    n_cmp = p_cmp.shape[-1]
    n_slc = pos.shape[0] // SEL_LEN
    p_slc = jnp.einsum('bgln,ns->bgls', p_cmp, jnp.asarray(selection_overlap(n_cmp, n_slc)))
    blk = jnp.arange(n_slc)[None, :]
    cur = (pos // SEL_LEN)[:, None]
    valid = blk <= cur
    forced = ((blk == 0) | (blk == cur) | (blk == cur - 1)).astype(jnp.float32)
    score = jnp.where(valid, p_slc + SEL_BONUS * forced, -SEL_BONUS)
    top, idx = lax.top_k(score, min(SEL_TOPK, n_slc))
    return idx, top > -0.5 * SEL_BONUS

def selected_attention(q, ks, vs, idx, ok):
    B_, L = q.shape[:2]
    n_slc = L // SEL_LEN
    n_ch = L // SEL_QCHUNK
    kb = jnp.moveaxis(ks.reshape(B_, n_slc, SEL_LEN, N_KV, HEAD_DIM_2), 3, 1)
    vb = jnp.moveaxis(vs.reshape(B_, n_slc, SEL_LEN, N_KV, HEAD_DIM_2), 3, 1)
    q_ch = jnp.moveaxis(q.reshape(B_, n_ch, SEL_QCHUNK, N_KV, HPG, HEAD_DIM_2), 1, 0)
    idx_ch = jnp.moveaxis(idx.reshape(B_, N_KV, n_ch, SEL_QCHUNK, -1), 2, 0)
    ok_ch = jnp.moveaxis(ok.reshape(B_, N_KV, n_ch, SEL_QCHUNK, -1), 2, 0)
    gather = jax.vmap(jax.vmap(lambda blocks, ix: blocks[ix]))
    offs = jnp.arange(SEL_LEN)

    def chunk(args):
        ci, qc, ic, oc = args
        t = ci * SEL_QCHUNK + jnp.arange(SEL_QCHUNK)
        kg = gather(kb, ic)
        vg = gather(vb, ic)
        s = jnp.einsum('bqghd,bgqksd->bgqhks', qc, kg)
        kpos = ic[..., None] * SEL_LEN + offs
        mask = (oc[..., None] & (kpos <= t[None, None, :, None, None]))[:, :, :, None]
        p = masked_softmax(s.reshape(*s.shape[:4], -1), mask.reshape(*mask.shape[:4], -1))
        p = p.reshape(s.shape).astype(vg.dtype)
        return jnp.einsum('bgqhks,bgqksd->bqghd', p, vg)

    o = lax.map(chunk, (jnp.arange(n_ch), q_ch, idx_ch, ok_ch))
    return jnp.moveaxis(o, 0, 1).reshape(B_, L, N_KV, HPG, HEAD_DIM_2)

def window_attention(q, kw, vw):
    B_, L = q.shape[:2]
    nb = L // WIN_QBLOCK
    span = WIN_QBLOCK + WINDOW
    pad = ((0, 0), (WINDOW, 0), (0, 0), (0, 0))
    kp, vp = jnp.pad(kw, pad), jnp.pad(vw, pad)
    q_blk = jnp.moveaxis(q.reshape(B_, nb, WIN_QBLOCK, N_KV, HPG, HEAD_DIM_2), 1, 0)
    koff = np.arange(span) - WINDOW
    rel = np.arange(WIN_QBLOCK)[:, None] - koff[None, :]
    band = (rel >= 0) & (rel < WINDOW)

    def block(args):
        bi, qb = args
        start = bi * WIN_QBLOCK
        kb = lax.dynamic_slice_in_dim(kp, start, span, axis=1)
        vb = lax.dynamic_slice_in_dim(vp, start, span, axis=1)
        mask = band & ((start + koff) >= 0)[None, :]
        s = jnp.einsum('bqghd,bkgd->bghqk', qb, kb)
        p = masked_softmax(s, mask).astype(vb.dtype)
        return jnp.einsum('bghqk,bkgd->bqghd', p, vb)

    o = lax.map(block, (jnp.arange(nb), q_blk))
    return jnp.moveaxis(o, 0, 1).reshape(B_, L, N_KV, HPG, HEAD_DIM_2)

def nsa_mixer(h, w_qg, w_o, kc, vc, ks, vs, kw, vw):
    B_, L, _ = h.shape
    proj = h @ w_qg
    q = proj[..., :ATT_WIDTH].reshape(B_, L, N_KV, HPG, HEAD_DIM_2) * (HEAD_DIM_2 ** -0.5)
    g_end = ATT_WIDTH + N_BRANCH * N_HEADS
    gates = jax.nn.sigmoid(proj[..., ATT_WIDTH:g_end].astype(jnp.float32)).astype(h.dtype)
    gates = gates.reshape(B_, L, N_BRANCH, N_KV, HPG, 1)
    z = proj[..., g_end:].reshape(B_, L, N_BRANCH, N_KV, HPG, HEAD_DIM_2)
    pos = jnp.arange(L)
    o_cmp, p_cmp = cmp_attention(q, kc, vc, pos)
    idx, ok = select_blocks(p_cmp, pos)
    o_sel = selected_attention(q, ks, vs, idx, ok)
    o_win = window_attention(q, kw, vw)
    o_br = jnp.stack([o_cmp, o_sel, o_win], axis=2)
    o = jnp.sum(gates * jax.nn.silu(z) * o_br, axis=2)
    return o.reshape(B_, L, ATT_WIDTH) @ w_o

def second_inputs(seed: int = 0) -> dict:
    key = jax.random.key(seed)
    keys = list(jax.random.split(key, 40))

    def nrm(shape, s):
        return s * jax.random.normal(keys.pop(), shape, jnp.float32)

    D, E, G, N = D_MODEL, SSM_WIDTH, SSM_GROUPS, SSM_STATE
    qg_cols = ATT_WIDTH + N_BRANCH * N_HEADS + N_BRANCH * ATT_WIDTH
    lam_im0 = jnp.pi * jnp.arange(N, dtype=jnp.float32)
    return {
        "x": nrm((BATCH, SEQ, D), 1.0),
        "c": nrm((BATCH, D), 1.0),
        "norm_g": 1.0 + nrm((DEPTH_2, D), 0.02),
        "mod_w": nrm((DEPTH_2, D, 3 * D), 0.5 * D ** -0.5),
        "mod_b": nrm((DEPTH_2, 3 * D), 0.01),
        "ssm_w_in": nrm((N_A, D, 2 * E), D ** -0.5),
        "ssm_lam_re": -0.5 + nrm((N_A, G, N), 0.01),
        "ssm_lam_im": lam_im0 + nrm((N_A, G, N), 0.01),
        "ssm_log_step": jax.random.uniform(keys.pop(), (N_A, G), jnp.float32, math.log(1e-3), math.log(1e-1)),
        "ssm_b_re": nrm((N_A, G, N, SSM_GROUP), (2 * SSM_GROUP) ** -0.5),
        "ssm_b_im": nrm((N_A, G, N, SSM_GROUP), (2 * SSM_GROUP) ** -0.5),
        "ssm_c_re": nrm((N_A, G, SSM_GROUP, N), 0.5),
        "ssm_c_im": nrm((N_A, G, SSM_GROUP, N), 0.5),
        "ssm_d": nrm((N_A, E), 1.0),
        "ssm_w_glu": nrm((N_A, E, E), E ** -0.5),
        "ssm_b_glu": nrm((N_A, E), 0.01),
        "ssm_w_out": nrm((N_A, E, D), E ** -0.5),
        "kv_norm_g": 1.0 + nrm((D,), 0.02),
        "kv_mod_w": nrm((D, 2 * D), 0.5 * D ** -0.5),
        "kv_mod_b": nrm((2 * D,), 0.01),
        "w_kv": nrm((D, 2 * N_BRANCH * N_KV * HEAD_DIM_2), D ** -0.5),
        "cmp_pe": nrm((2, CMP_LEN, HEAD_DIM_2), 0.02),
        "cmp_w1": nrm((2, CMP_LEN * HEAD_DIM_2, HEAD_DIM_2), (CMP_LEN * HEAD_DIM_2) ** -0.5),
        "cmp_b1": nrm((2, HEAD_DIM_2), 0.01),
        "cmp_w2": nrm((2, HEAD_DIM_2, HEAD_DIM_2), HEAD_DIM_2 ** -0.5),
        "cmp_b2": nrm((2, HEAD_DIM_2), 0.01),
        "nsa_w_qg": nrm((N_B, D, qg_cols), D ** -0.5),
        "nsa_w_o": nrm((N_B, ATT_WIDTH, D), ATT_WIDTH ** -0.5),
        "final_norm_g": 1.0 + nrm((D,), 0.02),
    }

def second_block(x, c, norm_g, mod_w, mod_b, ssm_w_in, ssm_lam_re, ssm_lam_im, ssm_log_step,
              ssm_b_re, ssm_b_im, ssm_c_re, ssm_c_im, ssm_d, ssm_w_glu, ssm_b_glu, ssm_w_out,
              kv_norm_g, kv_mod_w, kv_mod_b, w_kv, cmp_pe, cmp_w1, cmp_b1, cmp_w2, cmp_b2,
              nsa_w_qg, nsa_w_o, final_norm_g):
    c_act = jax.nn.silu(c)
    shared = None
    for layer in range(DEPTH_2):
        if layer == N_A:
            kv_shift, kv_scale = jnp.split(c_act @ kv_mod_w + kv_mod_b, 2, axis=-1)
            h_kv = modulate(rmsnorm(x, kv_norm_g), kv_shift, kv_scale)
            shared = nsa_shared_kv(h_kv, w_kv, cmp_pe, cmp_w1, cmp_b1, cmp_w2, cmp_b2)
        shift, scale, gate = jnp.split(c_act @ mod_w[layer] + mod_b[layer], 3, axis=-1)
        h = modulate(rmsnorm(x, norm_g[layer]), shift, scale)
        if layer < N_A:
            out = s5_mixer(h, ssm_w_in[layer], ssm_lam_re[layer], ssm_lam_im[layer],
                           ssm_log_step[layer], ssm_b_re[layer], ssm_b_im[layer],
                           ssm_c_re[layer], ssm_c_im[layer], ssm_d[layer],
                           ssm_w_glu[layer], ssm_b_glu[layer], ssm_w_out[layer])
        else:
            j = layer - N_A
            out = nsa_mixer(h, nsa_w_qg[j], nsa_w_o[j], *shared)
        x = x + gate[:, None, :] * out
    return rmsnorm(x, final_norm_g)


def setup_inputs(seed=0):
    out = dict(first_inputs(seed))
    for name, value in second_inputs(seed + 1).items():
        if name != "x":
            out[name + "_2"] = value
    return out


def reference(
    x, mem, positions, g_pre_mix, g_mem, w_in, w_mem_kv, w_branch_a, w_branch_b, w_branch_c,
    w_out, g_post_mix, g_pre_ffn, w_ffn_in, w_ffn_out, g_post_ffn, c_2, norm_g_2, mod_w_2,
    mod_b_2, ssm_w_in_2, ssm_lam_re_2, ssm_lam_im_2, ssm_log_step_2, ssm_b_re_2, ssm_b_im_2,
    ssm_c_re_2, ssm_c_im_2, ssm_d_2, ssm_w_glu_2, ssm_b_glu_2, ssm_w_out_2, kv_norm_g_2,
    kv_mod_w_2, kv_mod_b_2, w_kv_2, cmp_pe_2, cmp_w1_2, cmp_b1_2, cmp_w2_2, cmp_b2_2,
    nsa_w_qg_2, nsa_w_o_2, final_norm_g_2,
):
    x = first_block(
        x, mem, positions, g_pre_mix, g_mem, w_in, w_mem_kv, w_branch_a, w_branch_b, w_branch_c,
        w_out, g_post_mix, g_pre_ffn, w_ffn_in, w_ffn_out, g_post_ffn,
    )
    return second_block(
        x, c_2, norm_g_2, mod_w_2, mod_b_2, ssm_w_in_2, ssm_lam_re_2, ssm_lam_im_2,
        ssm_log_step_2, ssm_b_re_2, ssm_b_im_2, ssm_c_re_2, ssm_c_im_2, ssm_d_2, ssm_w_glu_2,
        ssm_b_glu_2, ssm_w_out_2, kv_norm_g_2, kv_mod_w_2, kv_mod_b_2, w_kv_2, cmp_pe_2,
        cmp_w1_2, cmp_b1_2, cmp_w2_2, cmp_b2_2, nsa_w_qg_2, nsa_w_o_2, final_norm_g_2,
    )


_drawn_inputs = setup_inputs


def setup_inputs(seed=0):
    import zlib

    import numpy as np

    out = dict(_drawn_inputs(seed))
    spreads = {}
    factors = {'g_mem': 6.442,
     'norm_g_2': 8.0,
     'mod_b_2': 8.0,
     'ssm_lam_re_2': 64.0,
     'ssm_lam_im_2': 3.712,
     'ssm_log_step_2': 4.01,
     'ssm_b_re_2': 5.117,
     'ssm_b_im_2': 4.981,
     'ssm_c_re_2': 5.218,
     'ssm_c_im_2': 5.082,
     'ssm_w_glu_2': 3.71,
     'ssm_b_glu_2': 8.0,
     'kv_norm_g_2': 8.0,
     'kv_mod_b_2': 8.0,
     'cmp_pe_2': 8.0,
     'cmp_w1_2': 2.725,
     'cmp_b1_2': 34.723,
     'cmp_b2_2': 64.0,
     'final_norm_g_2': 8.162}
    for name, (base, spread) in spreads.items():
        noise = np.random.default_rng([zlib.crc32(name.encode()), seed]).standard_normal(out[name].shape)
        drawn = base * np.exp(spread * noise) if base else spread * noise
        out[name] = __import__('jax').numpy.asarray(drawn.astype(out[name].dtype))
    for name, factor in factors.items():
        out[name] = (out[name] * factor).astype(out[name].dtype)
    return out
```

```python
from contextlib import ExitStack

import concourse.bass as bass
import numpy as np
from concourse import mybir

F32 = mybir.dt.float32
I32 = mybir.dt.int32
ALU = mybir.AluOpType
ACT = mybir.ActivationFunctionType
AX = mybir.AxisListType.X

P = 128
S = 256
D = 2048
TT = S // P
KT = D // P
EPS = 1e-6
NEG = -1e30
TAKEN = -3e38
N_ATT, N_IDX, N_RET, N_MEM = 8, 16, 8, 4
TOPK = min(256, S // 4)
FF_T = 5632 // P
NQ, NKV, HPG, HD = 16, 4, 4, 128
CMP_STRIDE, CMP_LEN = 16, 32
N_CMP = (S - CMP_LEN) // CMP_STRIDE + 1
ROUND = 1.5 * 2.0 ** 23
TURN = 2 * np.pi
TURN_HI = 6.28125
TURN_LO = float(np.float32(TURN - 6.28125))
PI = 3.1415925
RING, UNIT = 8, 2048
CHUNK = 512
KG = 4

PHASES = [
    ("m0", 16, 8), ("mk", 8, 4), ("mv", 8, 4), ("mq", 8, 4), ("ik", 1, 1), ("iq", 8, 4), ("aq", 8, 4), ("av", 8, 4),
    ("ak", 8, 4), ("rq", 8, 4), ("rk", 8, 4), ("rv", 16, 8), ("rg", 16, 8), ("mix", 80, 48), ("wo", 16, 8),
    ("m1", 16, 8), ("ff", 88, 44), ("fo", 44, 8), ("m2", 16, 8), ("su", 16, 8), ("sz", 16, 8),
    ("ms", 64, 32), ("glu", 16, 8), ("so", 16, 8), ("m7", 16, 8),
    ("kvt", 16, 8), ("cw", 4, 0), ("kvn", 8, 4), ("nq", 16, 8), ("nz", 48, 24), ("no", 16, 8),
]
U0, B0, NB = {}, {}, {}
UNITS = BANKS = 0
for _name, _units, _banks in PHASES:
    U0[_name], B0[_name], NB[_name] = UNITS, BANKS, _banks
    UNITS += _units
    BANKS += _banks
STREAM_UNITS = -(-UNITS // RING) * RING
T_PHASES = ("mk", "mq", "iq", "aq", "ak", "rq", "rk", "ff", "su", "sz", "glu", "kvt", "nq")

PIECES = ["s5_scale", "s5_shift", "kv_shift", "s5_gate", "kv_scale", "nsa_shift", "nsa_scale", "nsa_gate"]
PIECE_PHASE = {0: "m0", 1: "m1", 2: "m2", 3: "ms", 7: "m7"}
SSM_PIECE0 = 3

VECS = ["g_pre_mix", "g_mem", "g_pre_ffn", "norm0", "norm1", "kv_norm", "c", "b_glu", "d_skip"] + PIECES
V = {n: i for i, n in enumerate(VECS)}

SSM_CHUNKS, PAIRS = D // P, 4
SSM_BODY = 4
SSM_B, SSM_C = PAIRS * 2 * P, 2 * P
SSM_COLS = SSM_B + SSM_C


CONSTS_MADE = 6
LATE = 1533
SSM_Y0 = 1
SSM_GELU0 = 1
TURN_F = 6.283185
MIX_UNITS = (4, 10, 18, 24, 30, 38)
MIX_ENDS = (6, 14, 20, 26, 34, 40)
CMP_PAD = 32
RETV = 256
SSM_BACK = (2, 3, 0, 1)
S5_PAIRS = (SSM_CHUNKS + 1) * PAIRS
EARLY, CST = 2560, 898 + len(VECS) * KT
O_ADDS = NKV * TT + 2 * NQ


def heads_in_turn(name, n, first=0):
    out = []
    for h in range(n + 2):
        out += [(name + "_logits", first + h)] * (h < n)
        out += [(name + "_turn", first + h - 1)] * (1 <= h <= n)
        out += [(name + "_values", first + h - 2)] * (h >= 2)
    return out


def spread(phase, n, tasks=()):
    out, done = [], 0
    for u in range(n):
        want = -(-len(tasks) * (u + 1) // n)
        out += [("unit", phase, u), *tasks[done:want]]
        done = want
    return out


def with_ropes(steps):
    out, due = [], []
    for s in steps:
        out += [s]
        if s[0] == "unit":
            out += due
            due = [("rope", s[1], s[2] // 2)] if s[2] % 2 or s[1] == "ik" else []
    return out + due


def mixer_steps():
    att = heads_in_turn("att", N_ATT)
    ret = [x for h in range(N_RET + 1) for x in [("ret_scores", h)] * (h < N_RET) + [("ret_values", h - 1)] * (h > 0)]
    s = [("mod_units", 0)] + [("norm", "mem", j) for j in range(KT // 2)] + [("mod_turn", 0)] + [("norm", "x", j) for j in range(KT // 2)]
    s += spread("mk", 8) + spread("mv", 8) + spread("mq", 8)
    s += with_ropes(spread("ik", 1) + spread("iq", 8, heads_in_turn("mem", N_MEM)))
    s += with_ropes(spread("aq", 8, [("idx_w", 0)] + [("idx", h) for h in range(N_IDX)]))
    s += spread("av", 8) + with_ropes(spread("ak", 8)) + with_ropes(spread("rq", 8))
    s += with_ropes(spread("rk", 8, att[:8])) + spread("rv", 16, att[8:])
    s += spread("rg", 16, ret) + [("turn_y", j) for j in range(KT // 2)]
    return s


def nsa_steps():
    s = [("mod_units", 7)] + [("norm", "x3", j) for j in range(KT // 2)] + [("mod_turn", 7)] + spread("kvt", 16)
    s += [("cmp_hidden", 0), ("cmp_hidden", 1)] + spread("kvn", 8, [("cmp_out", 0), ("cmp_out", 1)])
    s += spread("nq", 16) + [("ngate", 0)]
    for g in range(NKV):
        for br, name in enumerate(("cmp", "sel", "win")):
            if br == 0:
                tasks = [("cmp_logits", g), ("cmp_turn", g), ("cmp_values", g, 0), ("cmp_values", g, 1)]
            else:
                tasks = heads_in_turn(name, HPG, HPG * g)
            s += [("unit", "nz", 4 * (3 * g + br) + u) for u in range(4)] + tasks
    return s + [("turn_o", j) for j in range(KT // 2)]


MIXER, NSA = mixer_steps(), nsa_steps()
AFTER_MIX = [("turn_mix", j) for j in range(KT // 2)]
BEFORE_FFN = [("mod_units", 1)] + [("norm", "x1", j) for j in range(KT // 2)] + [("mod_turn", 1)]
BEFORE_S5 = [("mod_units", 2)] + [("norm", "x2", j) for j in range(KT // 2)] + [("mod_turn", 2)]
BEFORE_S5_OUT = [("gate", "s5", j) for j in range(D // CHUNK)]
BEFORE_NSA_OUT = [("gate", "nsa", j) for j in range(D // CHUNK)]

SIDE = {}
_n = 0
for _steps in (MIXER, AFTER_MIX, BEFORE_FFN, BEFORE_S5, None, BEFORE_S5_OUT, NSA, BEFORE_NSA_OUT):
    if _steps is None:
        SSM_SIDE0 = _n
        _n += SSM_CHUNKS * (PAIRS + 1)
        continue
    for _s in _steps:
        if _s[0] not in ("unit", "mod_units", "mod_turn"):
            SIDE[_s] = _n
            _n += 1
GATES = {s: n for n, s in enumerate(BEFORE_S5_OUT + BEFORE_NSA_OUT)}
ROPE = {s: n for n, s in enumerate(x for x in MIXER if x[0] == "rope")}
_attn = [x for x in MIXER + NSA if x[0].endswith("_logits")]
TURNS = [(x[0][:3] + "_turn", x[1]) for x in _attn]
VALUES = [(x[0][:3] + "_values", x[1]) + ((1,) if x[0][:3] == "cmp" else ()) for x in _attn]
MASKED = {n: n - N_MEM for n in range(len(_attn))}
O_INDEX = {s: n for n, s in enumerate(x for x in NSA if x[0] in ("cmp_values", "sel_values", "win_values"))}
O_AFTER = [sum(1 for s in O_INDEX if (3 * s[1] if s[0] == "cmp_values" else 3 * (s[1] // HPG) + (1 if s[0][:3] == "sel" else 2)) <= c)
           for c in range(3 * NKV)]
HEADS = {s[:2]: n for n, s in enumerate(x for x in MIXER + NSA if x[0].endswith("_logits"))}
NORMS = {"mem": 0, "x": 1, "x1": 2, "x2": 3, "x3": 4, "out": 5}


class Steps:

    def __init__(self, eng, sem):
        self.eng, self.sem, self.n, self.i, self.stride = eng, sem, 0, None, 0

    def __call__(self, ins):
        ins.then_inc(self.sem, 1)
        self.n += 1

    def wait(self):
        self.eng.wait_ge(self.sem, self.n if self.i is None else self.i * self.stride + self.n)

    def enter(self, i, stride):
        self.i, self.stride, self.n0 = i, stride, self.n

    def leave(self, count):
        assert self.n - self.n0 == self.stride, (self.n - self.n0, self.stride)
        self.n, self.i = self.n0 + self.stride * count, None


def program(nc, A, out):
    with ExitStack() as ctx:
        def sb(name, shape):
            return ctx.enter_context(nc.sbuf_tensor(name, shape, F32))

        def sem(name):
            return ctx.enter_context(nc.semaphore(name))

        ring = sb("ring", [P, RING, UNIT])
        mod_row = sb("mod_row", [1, D])
        v_blocks = sb("v_blocks", [P, NKV, CHUNK])
        junk = sb("junk", [P, D])
        arena = sb("arena", [P, 88 * 256])
        work = sb("work", [P, 7, CHUNK])
        early = sb("early", [P, EARLY])
        perms = early[:, 0:2 * P].rearrange("p (k m) -> p k m", k=2)
        w_iw = early[:, 256:512].rearrange("p (k n) -> p k n", k=KT)
        ropes = early[:, 512:1536].rearrange("p (k t) -> p k t", k=4)
        selbias = early[:, 1536:2048].rearrange("p (t s) -> p t s", t=TT)
        ikT = early[:, 2048:2560].rearrange("p (h s) -> p h s", h=2)
        w_ng = early[:, 0:768].rearrange("p (k n) -> p k n", k=KT)
        cmp_w2 = early[:, 768:1024].rearrange("p (j n) -> p j n", j=2)
        b1_rows = early[:, 1024:1280].rearrange("p (j n) -> p j n", j=2)
        b2_row = early[:, 1280:1408]
        cmp_pe = early[:, 1408:1472].rearrange("p (j l) -> p j l", j=2)
        cmp_add = early[:, 1472:1502].rearrange("p (t n) -> p t n", t=TT)
        cmp_keep = early[:, 1502:1532].rearrange("p (t n) -> p t n", t=TT)
        b2_col = early[:, 1532:1533]
        hid = early[:, 1536:1656].rearrange("p (j n) -> p j n", j=2)
        kcT = early[:, 1656:1716]
        gates = early[:, 1720:1816].rearrange("p (t n) -> p t n", t=TT)
        v_tmp = early[:, 2048:2560].rearrange("p (g n) -> p g n", g=NKV)
        cst = sb("cst", [P, CST])
        ident = cst[:, 0:128]
        causal = cst[:, 128:640].rearrange("p (t s) -> p t s", t=TT)
        time_row = cst[:, 640:896]
        vecs = cst[:, 896:896 + len(VECS) * KT].rearrange("p (v c) -> p v c", c=KT)
        freq = cst[:, CST - 2:CST]
        ones = sb("ones", [P, P])
        modv = sb("modv", [P, len(PIECES), KT])
        gains = sb("gains", [P, 3, KT])
        c_act = sb("c_act", [P, KT])
        iw = sb("iw", [P, TT, N_IDX])
        stat = sb("stat", [P, 64])
        bn = sb("bn", [P, TT, 6])
        s5 = sb("s5", [P, 5, S5_PAIRS])
        half_pi = sb("half_pi", [P, 1])
        round_up, round_back = sb("round_up", [P, 1]), sb("round_back", [P, 1])
        bn_all = sb("bn_all", [P, TT * N_RET, 2])
        psum = ctx.enter_context(nc.psum_tensor("psum", [P, 8, CHUNK], F32))

        def area(kb, n):
            return arena[:, kb * 256:kb * 256 + n]

        def tokens(kb, n=D):
            return area(kb, TT * n).rearrange("p (t n) -> p t n", t=TT)

        def feats(kb, n=KT):
            return area(kb, n * S).rearrange("p (c t) -> p c t", c=n)

        hT, memT, x_in, mem_in = feats(0), feats(64), tokens(16), tokens(32)
        mkT, mv, mqT, o_cT = feats(32, 8), tokens(40, 1024), feats(48, 8), feats(24, 8)
        iqT, aqT, akT, av, o_aT = feats(64, 8), feats(48, 8), feats(56, 8), tokens(80, 1024), feats(16, 8)
        score, top = tokens(72, S), tokens(74, S)
        rqT, rkT, rv, rg = feats(32, 8), feats(40, 8), tokens(64), tokens(48)
        decay = area(80, N_RET * S).rearrange("p (h t) -> p h t", h=N_RET)
        o_bT, mixed, mixT = feats(32), tokens(48), feats(0)
        xr, y, row = tokens(64), tokens(16), area(80, D)
        xn, h2T, actT, y2 = tokens(16), feats(0), feats(16, FF_T), tokens(0)
        h3T, uT, zT = feats(0), feats(16), feats(32)
        ssm_in = area(48, 2 * SSM_COLS).rearrange("p (b n) -> p b n", b=2)
        ssm_c = area(58, 2 * 3 * P).rearrange("p (b k q c) -> p b k q c", b=2, k=3, q=PAIRS)
        hkvT, hnT, qT, ksT, kwT = feats(0), feats(48), feats(0), feats(32, NKV), feats(36, NKV)
        vs, vw, o_tok, oT = tokens(40, 512), tokens(44, 512), tokens(16), feats(0)
        cin = area(16, 4 * NKV * S).rearrange("p (j h g t) -> p j h g t", j=2, h=2, g=NKV)
        zs = area(80, 2 * TT * CHUNK).rearrange("p (b t n) -> p b t n", b=2, t=TT)
        y_out = tokens(32)

        def halves(i):
            return work[:, i, :].rearrange("p (t s) -> p t s", t=2)

        prob, probT = (0, 1), (2, 3)
        TMP = (4, 5, 6)

        def halves_of(ap):
            return ap.rearrange("p (t s) -> p t s", t=2)

        pos_i = area(80, S).bitcast(I32)
        rope_pos, rope_ang, rope_k, rope_abs = area(81, S), [area(82, S), area(83, S)], area(84, S), area(85, S)
        s5_raw = area(56, 3 * 64).rearrange("p (k n) -> p k n", k=3)
        s5_dt, s5_thr, s5_sin, s5_sin2 = (area(57, 256)[:, 64 * k:64 * k + 64] for k in range(4))
        s5_tmp = [area(58, 320)[:, 64 * k:64 * k + 64] for k in range(5)]
        ret_stat = bn_all[:, :, :]
        final_row = area(48, D)
        whole_t = work[:, TMP[1]:TMP[2] + 1, :].rearrange("p b n -> p (b n)")

        def stream_bank(b):
            return psum[:, b % 4, :]

        def side_bank(n):
            return psum[:, 4 + n % 4, :]

        landed = [sem(f"ring_slot{s}_landed") for s in range(RING)]
        units_done = sem("units_done")
        evacuated = [sem(f"stream_bank{b}_evacuated") for b in range(4)]
        side_done = sem("side_done")
        side_read = [sem(f"side_bank{b}_read") for b in range(4)]
        consts_landed, mem_landed, x_landed = sem("consts_landed"), sem("mem_landed"), sem("x_landed")
        decay_landed, rows_landed = sem("decay_landed"), sem("rows_landed")
        mod_turned = sem("mod_turned")
        norm_squares, norm_mean, norm_root, norm_scaled = (sem("norm_" + n) for n in ("squares", "mean", "root", "scaled"))
        roped, idx_added = sem("roped"), sem("idx_added")
        head_max, head_exp, head_prob = sem("head_max"), sem("head_exp"), sem("head_prob")
        ret_var, ret_root, ret_gated = sem("ret_var"), sem("ret_root"), sem("ret_gated")
        mix_done = sem("mix_done")
        res_mean, res_root, res_added = sem("res_mean"), sem("res_root"), sem("res_added")
        act_ready, trig_done, s5_ready = sem("c_act_ready"), sem("trig_done"), sem("s5_ready")
        act_steps, dve_steps, pool_steps = sem("act_steps"), sem("dve_steps"), sem("pool_steps")
        ang_ready, rope_ready, const_made = sem("ang_ready"), sem("rope_ready"), sem("const_made")
        diag_ready, mod_gain = sem("diag_ready"), sem("mod_gain")
        ssm_landed = [sem(f"ssm_in{b}_landed") for b in range(2)]
        ssm_cmul, ssm_turns, ssm_whole, ssm_frac, ssm_trig = (
            sem("ssm_" + n) for n in ("cmul", "turns", "whole", "frac", "trig"))
        ssm_prod, ssm_rot, ssm_state, ssm_back, ssm_y, ssm_skip = (
            sem("ssm_" + n) for n in ("prod", "rot", "state", "back", "y", "skip"))
        cmp_key, cmp_vblock, v_zero, silu_z, o_added = sem("cmp_key"), sem("cmp_vblock"), sem("v_zero"), sem("silu_z"), sem("o_added")
        gates_made, out_ready, out_stored = sem("gates_made"), sem("out_ready"), sem("out_stored")
        glu_in, late_landed = sem("glu_in"), sem("late_landed")
        s5_raw_landed, x_again_landed, final_row_landed = sem("s5_raw_landed"), sem("x_again_landed"), sem("final_row_landed")
        consts_made, ff_gate, res_squares = sem("consts_made"), sem("ff_gate"), sem("res_squares")
        glu_gate, iw_ready, sel_ready, cin_part = sem("glu_gate"), sem("iw_ready"), sem("sel_ready"), sem("cin_part")
        pos_landed, s5_params, mix_part, ssm_gelu = sem("pos_landed"), sem("s5_params"), sem("mix_part"), sem("ssm_gelu")
        p_cmp = work[:, TMP[0], 0:2 * P]
        SSM_USES = SSM_CHUNKS * (PAIRS + 1)

        def written(n):
            return side_done, n + 1 - (SSM_CHUNKS if n >= SSM_SIDE0 + SSM_USES else 0)

        def read(n):
            return side_read[n % 4], n // 4 + 1

        def multiplied(phase, u):
            return units_done, U0[phase] + u + 1

        def emptied(b):
            return evacuated[b % 4], b // 4 + 1

        def last_banks(phase):
            return [emptied(B0[phase] + NB[phase] - 1 - i) for i in range(min(4, NB[phase]))]

        def last_reads(uses):
            return [read(n) for n in uses[-4:]]

        def norm_uses(tag):
            return [SIDE[("norm", tag, j)] for j in range(KT // 2)]

        cos_t = [area(0, 1024), area(4, 1024)]
        sin_t = [area(8, 1024), area(12, 1024)]
        frac_t, abs_t = area(80, 1024), area(84, 1024)
        S_MAG, S_TURN, S_KRE, S_KIM, S_NKIM = 0, 1, 2, 3, 4

        block = ctx.enter_context(nc.Block())

        @block.sync
        def _(sp):
            for s in range(RING):
                sp.dma_start(ring[:, s, :], A["stream"][s]).then_inc(landed[s], 16)
            with sp.Fori(1, STREAM_UNITS // RING) as turn:
                for s in range(RING):
                    sp.wait_ge(units_done, turn * RING + (s + 1 - RING))
                    sp.dma_start(ring[:, s, :], A["stream"][bass.ds(turn * RING + s, 1)]
                                 .rearrange("a p n -> p (a n)")).then_inc(landed[s], 16)
            sp.wait_ge(out_ready, 2)
            for t in range(TT):
                sp.dma_start(out[t * P:(t + 1) * P, :], y_out[:, t, :]).then_inc(out_stored, 16)
            sp.wait_ge(out_stored, 16 * TT)

        @block.tensor
        def _(pe):
            def slot_of(phase, u, i=None, turns=0):
                n = U0[phase] + u
                value = 16 * (n // RING + 1)
                pe.wait_ge(landed[n % RING], value if i is None else i * (16 * turns) + value)
                return n % RING

            def free_bank(b, i=None, uses=0):
                if b >= 4:
                    pe.wait_ge(evacuated[b % 4], b // 4 if i is None else i * uses + b // 4)
                return stream_bank(b)

            def free_side(n):
                if n >= 4:
                    pe.wait_ge(*read(n - 4))
                return side_bank(n)

            def t_unit(phase, u, rhs, i=None, turns=0, uses=0):
                slot = slot_of(phase, u, i, turns)
                b = B0[phase] + u // 2
                bank = free_bank(b, i, uses) if u % 2 == 0 or phase == "ik" else stream_bank(b)
                half = (u % 2) * S
                for k in range(KT):
                    mm = pe.matmul(bank[:, half:half + S], ring[:, slot, k * P:(k + 1) * P], rhs[:, k, :],
                                   start=(k == 0), stop=(k == KT - 1))
                mm.then_inc(units_done, 1)

            def n_unit(phase, u, lhsT, kg, groups, b, i=None, turns=0, uses=0):
                slot = slot_of(phase, u, i, turns)
                if kg == 0:
                    free_bank(b, i, uses)
                    free_bank(b + 1, i, uses)
                for kk in range(KG):
                    for t in range(TT):
                        mm = pe.matmul(stream_bank(b + t), lhsT[:, kg * KG + kk, t * P:(t + 1) * P],
                                       ring[:, slot, kk * CHUNK:(kk + 1) * CHUNK],
                                       start=(kg == 0 and kk == 0), stop=(kg == groups - 1 and kk == KG - 1))
                mm.then_inc(units_done, 1)

            def turn_tokens(src, j, n):
                bank = free_side(n)
                for c in range(2):
                    for t in range(TT):
                        mm = pe.transpose(bank[:, c * S + t * P:c * S + (t + 1) * P],
                                          src[:, t, (2 * j + c) * P:(2 * j + c + 1) * P], ident[:, :])
                mm.then_inc(side_done, 1)

            T_RHS = {"mk": memT, "mq": hT, "ik": hT, "iq": hT, "aq": hT, "ak": hT, "rq": hT, "rk": hT,
                     "su": h3T, "sz": h3T, "glu": uT, "kvt": hkvT, "nq": hnT}
            N_LHS = {"mv": memT, "av": hT, "rv": hT, "rg": hT, "wo": mixT, "so": zT, "kvn": hkvT, "nz": hnT, "no": oT}

            def mod_units(piece, units, i=None):
                phase = PIECE_PHASE[piece]
                for u in units:
                    slot = slot_of(phase, u, i, 2)
                    for c in range(4):
                        b = B0[phase] + c
                        bank = free_bank(b, i, 2) if u == 0 else stream_bank(b)
                        mm = pe.matmul(bank[0:1, :], c_act[:, u:u + 1], ring[:, slot, c * CHUNK:(c + 1) * CHUNK],
                                       start=(u == 0), stop=(u == KT - 1))
                    mm.then_inc(units_done, 1)

            def mod_turn(piece, i=None):
                for c in range(4):
                    bank = free_bank(B0[PIECE_PHASE[piece]] + 4 + c, i, 2)
                    for k in range(4):
                        at = c * CHUNK + k * P
                        mm = pe.matmul(bank[:, k:k + 1], mod_row[0:1, at:at + P], ones[0:1, 0:1], start=True, stop=True)
                    mm.then_inc(mod_turned, 1)

            def plain_unit(phase, u):
                if phase in T_RHS:
                    t_unit(phase, u, T_RHS[phase])
                else:
                    n_unit(phase, u, N_LHS[phase], u % 4, 4, B0[phase] + u // 4 * 2)

            def logits(n, q, k, h, hk):
                bank = free_side(n)
                for t in range(TT):
                    mm = pe.matmul(bank[:, t * S:(t + 1) * S], q[:, h, t * P:(t + 1) * P], k[:, hk, :],
                                   start=True, stop=True)
                mm.then_inc(side_done, 1)

            def turn_probs(n, a):
                bank = free_side(n)
                pe.wait_ge(head_prob, a + 1)
                for blk in range(2):
                    for t in range(TT):
                        mm = pe.transpose(bank[:, blk * S + t * P:blk * S + (t + 1) * P],
                                          halves(prob[a % 2])[:, t, blk * P:(blk + 1) * P], ident[:, :])
                mm.then_inc(side_done, 1)

            def side(step):
                kind, n = step[0], SIDE[step]
                if kind == "norm":
                    tag, j = step[1:]
                    if j == 0:
                        pe.wait_ge(norm_scaled, TT * (NORMS[tag] + 1))
                    turn_tokens({"mem": mem_in, "x": x_in}.get(tag, xn), j, n)
                elif kind == "rope":
                    r = ROPE[step]
                    bank = free_side(n)
                    pe.wait_ge(*emptied(B0[step[1]] + step[2]))
                    width = S if step[1] == "ik" else 2 * S
                    pe.matmul(bank[:, 0:width], perms[:, 1 if step[1] in ("ik", "iq") else 0, :],
                              work[:, TMP[r % 2], 0:width], start=True, stop=True).then_inc(side_done, 1)
                elif kind in ("idx_w", "ngate"):
                    src, w, m = (hT, w_iw, N_IDX) if kind == "idx_w" else (hnT, w_ng, 3 * NQ)
                    bank = free_side(n)
                    for t in range(TT):
                        for k in range(KT):
                            mm = pe.matmul(bank[:, t * m:(t + 1) * m], src[:, k, t * P:(t + 1) * P], w[:, k, :],
                                           start=(k == 0), stop=(k == KT - 1))
                    mm.then_inc(side_done, 1)
                elif kind == "idx":
                    h = step[1]
                    if h == 0:
                        pe.wait_ge(roped, ROPE[("rope", "iq", 3)] + 1)
                    logits(n, iqT, ikT, h // 2, h % 2)
                elif kind == "mem_logits":
                    h = step[1]
                    bank = free_side(n)
                    if h == 0:
                        for w in last_banks("mk") + last_banks("mq"):
                            pe.wait_ge(*w)
                    for t in range(TT):
                        for kk in range(2):
                            mm = pe.matmul(bank[:, t * S:(t + 1) * S], mqT[:, 2 * h + kk, t * P:(t + 1) * P],
                                           mkT[:, 2 * h + kk, :], start=(kk == 0), stop=(kk == 1))
                    mm.then_inc(side_done, 1)
                elif kind == "att_logits":
                    if step[1] == 0:
                        pe.wait_ge(roped, ROPE[("rope", "ak", 3)] + 1)
                    logits(n, aqT, akT, step[1], step[1])
                elif kind in ("sel_logits", "win_logits"):
                    logits(n, qT, ksT if kind == "sel_logits" else kwT, step[1], step[1] // HPG)
                elif kind.endswith("_turn") and kind != "cmp_turn":
                    turn_probs(n, HEADS[(kind[:3] + "_logits", step[1])])
                elif kind == "mem_values":
                    h = step[1]
                    a = HEADS[("mem_logits", h)]
                    bank = free_side(n)
                    pe.wait_ge(*read(SIDE[("mem_turn", h)]))
                    if h == 0:
                        for w in last_banks("mv"):
                            pe.wait_ge(*w)
                    for e in range(2):
                        for blk in range(2):
                            at = (2 * h + e) * P
                            mm = pe.matmul(bank[:, e * S:(e + 1) * S], mv[:, blk, at:at + P],
                                           halves(probT[a % 2])[:, blk, :], start=(blk == 0), stop=(blk == 1))
                    mm.then_inc(side_done, 1)
                elif kind == "att_values":
                    h = step[1]
                    a = HEADS[("att_logits", h)]
                    bank = free_side(n)
                    pe.wait_ge(*read(SIDE[("att_turn", h)]))
                    if h == 0:
                        for w in last_banks("av"):
                            pe.wait_ge(*w)
                    for blk in range(2):
                        mm = pe.matmul(bank[:, 0:S], av[:, blk, h * P:(h + 1) * P], halves(probT[a % 2])[:, blk, :],
                                       start=(blk == 0), stop=(blk == 1))
                    mm.then_inc(side_done, 1)
                elif kind in ("sel_values", "win_values"):
                    h = step[1]
                    a = HEADS[(kind[:3] + "_logits", h)]
                    v, g = (vs if kind == "sel_values" else vw), h // HPG
                    bank = free_side(n)
                    pe.wait_ge(*read(SIDE[(kind[:3] + "_turn", h)]))
                    for t in range(TT):
                        for blk in range(2):
                            mm = pe.matmul(bank[:, t * P:(t + 1) * P], halves(probT[a % 2])[:, blk, t * P:(t + 1) * P],
                                           v[:, blk, g * P:(g + 1) * P], start=(blk == 0), stop=(blk == 1))
                    mm.then_inc(side_done, 1)
                elif kind == "ret_scores":
                    h = step[1]
                    bank = free_side(n)
                    if h == 0:
                        pe.wait_ge(roped, ROPE[("rope", "rk", 3)] + 1)
                    pe.matmul(bank[:, 0:S], rkT[:, h, 0:P], rqT[:, h, :], start=True, stop=True)
                    pe.matmul(bank[:, S:S + P], rkT[:, h, P:S], rqT[:, h, P:S], start=True,
                              stop=True).then_inc(side_done, 1)
                elif kind == "ret_values":
                    h = step[1]
                    bank = free_side(n)
                    pe.wait_ge(*read(SIDE[("ret_scores", h)]))
                    if h == 0:
                        for w in last_banks("rv"):
                            pe.wait_ge(*w)
                    sd, at = work[:, prob[h % 2], :], h * RETV
                    pe.matmul(bank[:, 0:RETV], sd[:, 0:P], rv[:, 0, at:at + RETV], start=True, stop=True)
                    pe.matmul(bank[:, RETV:2 * RETV], sd[:, P:S], rv[:, 0, at:at + RETV], start=True, stop=False)
                    pe.matmul(bank[:, RETV:2 * RETV], sd[:, S:S + P], rv[:, 1, at:at + RETV], start=False,
                              stop=True).then_inc(side_done, 1)
                elif kind in ("turn_y", "turn_mix", "turn_o"):
                    src, done, value = {"turn_y": (rv, ret_gated, 1), "turn_mix": (mixed, mix_done, 1),
                                        "turn_o": (o_tok, o_added, O_ADDS)}[kind]
                    if step[1] == 0:
                        pe.wait_ge(done, value)
                    turn_tokens(src, step[1], n)
                elif kind == "gate":
                    tag, j = step[1:]
                    bank = free_side(n)
                    pe.wait_ge(diag_ready, GATES[step] + 1)
                    for c in range(4):
                        mm = pe.matmul(bank[:, c * P:(c + 1) * P], ones[:, :], work[:, TMP[j % 2], c * P:(c + 1) * P],
                                       start=True, stop=True)
                    mm.then_inc(side_done, 1)
                elif kind == "cmp_hidden":
                    j = step[1]
                    bank = free_side(n)
                    for b in range(2):
                        pe.wait_ge(*emptied(B0["kvt"] + 2 * j + b))
                    for half in range(2):
                        slot = slot_of("cw", 2 * j + half)
                        for r in range(CMP_STRIDE):
                            blocks = cin[:, j, half, :, :].rearrange("p g (n r) -> p g n r", r=CMP_STRIDE)
                            mm = pe.matmul(bank[:, 0:NKV * N_CMP], ring[:, slot, r * P:(r + 1) * P],
                                           blocks[:, :, half:half + N_CMP, r], start=(half == 0 and r == 0), stop=False)
                        mm.then_inc(units_done, 1)
                    pe.matmul(bank[:, 0:NKV * N_CMP], b1_rows[0:1, j, :], ones[0:1, 0:NKV * N_CMP], start=False,
                              stop=True).then_inc(side_done, 1)
                elif kind == "cmp_out":
                    j = step[1]
                    bank = free_side(n)
                    pe.wait_ge(*read(SIDE[("cmp_hidden", j)]))
                    if j == 0:
                        mm = pe.matmul(bank[:, 0:NKV * N_CMP], cmp_w2[:, 0, :], hid[:, 0, :], start=True, stop=True)
                    else:
                        for g in range(NKV):
                            mm = pe.matmul(bank[0:N_CMP, g * P:(g + 1) * P], hid[:, 1, g * N_CMP:(g + 1) * N_CMP],
                                           cmp_w2[:, 1, :], start=True, stop=True)
                    mm.then_inc(side_done, 1)
                elif kind == "cmp_logits":
                    g = step[1]
                    bank = free_side(n)
                    if g == 0:
                        pe.wait_ge(*read(SIDE[("cmp_out", 0)]))
                    for t in range(TT):
                        for h in range(HPG):
                            at = (t * HPG + h) * CMP_PAD
                            mm = pe.matmul(bank[:, at:at + N_CMP], qT[:, HPG * g + h, t * P:(t + 1) * P],
                                           kcT[:, g * N_CMP:(g + 1) * N_CMP], start=True, stop=True)
                    mm.then_inc(side_done, 1)
                elif kind == "cmp_turn":
                    a = HEADS[("cmp_logits", step[1])]
                    bank = free_side(n)
                    pe.wait_ge(head_prob, a + 1)
                    for t in range(TT):
                        mm = pe.transpose(bank[:, t * P:(t + 1) * P], p_cmp[:, t * P:(t + 1) * P], ident[:, :])
                    mm.then_inc(side_done, 1)
                elif kind == "cmp_values":
                    g, t = step[1:]
                    a = HEADS[("cmp_logits", g)]
                    bank = free_side(n)
                    pe.wait_ge(*read(SIDE[("cmp_turn", g)]))
                    if g == 0:
                        pe.wait_ge(cmp_vblock, 1)
                    pe.matmul(bank, work[:, probT[a % 2], t * P:(t + 1) * P], v_blocks[:, g, :], start=True,
                              stop=True).then_inc(side_done, 1)
                else:
                    raise ValueError(kind)

            first = {"mk": last_reads(norm_uses("mem")), "mq": last_reads(norm_uses("x")),
                     "wo": last_reads([SIDE[("turn_mix", j)] for j in range(8)]),
                     "su": last_reads(norm_uses("x2")), "glu": [(glu_in, 1)], "so": last_banks("glu"),
                     "kvt": last_reads(norm_uses("x3")), "no": last_reads([SIDE[("turn_o", j)] for j in range(8)])}

            def steps(todo):
                for step in todo:
                    if step[0] == "unit":
                        for w in first.get(step[1], []) if step[2] == 0 else []:
                            pe.wait_ge(*w)
                        plain_unit(step[1], step[2])
                    elif step[0] == "mod_units":
                        mod_units(step[1], range(KT))
                    elif step[0] == "mod_turn":
                        mod_turn(step[1])
                    else:
                        side(step)

            pe.wait_ge(consts_made, CONSTS_MADE)
            pe.wait_ge(consts_landed, 32)
            pe.wait_ge(act_ready, 1)
            steps(MIXER)
            for w in last_reads([SIDE[("turn_y", j)] for j in range(8)]) + last_reads([SIDE[("att_values", N_ATT - 1)]]) \
                    + last_reads([SIDE[("mem_values", N_MEM - 1)]]):
                pe.wait_ge(*w)
            with pe.Fori(0, 2) as i:
                for c in range(2):
                    u, b = c * 20, B0["mix"] + c * 12
                    for src, groups in ((o_aT, 2), (o_bT, 4), (o_cT, 2)):
                        for lhsT, kgs in ((hT, 4), (src, groups)):
                            for kg in range(kgs):
                                n_unit("mix", u, lhsT, kg, kgs, b, i, 5, 6)
                                u += 1
                            b += 2
            steps(AFTER_MIX)
            steps([("unit", "wo", u) for u in range(16)])
            steps(BEFORE_FFN)
            for w in last_reads(norm_uses("x1")):
                pe.wait_ge(*w)
            with pe.Fori(0, FF_T // 4) as i:
                for u in range(8):
                    t_unit("ff", u, h2T, i, 1, 1)
            for w in last_banks("ff"):
                pe.wait_ge(*w)
            for c in range(4):
                for kg in range(FF_T // KG):
                    n_unit("fo", c * (FF_T // KG) + kg, actT, kg, FF_T // KG, B0["fo"] + 2 * c)
            steps(BEFORE_S5)
            steps([("unit", "su", u) for u in range(16)] + [("unit", "sz", u) for u in range(16)])
            for w in last_banks("su"):
                pe.wait_ge(*w)
            pe.nop().then_inc(ssm_y, SSM_Y0)
            with pe.Fori(0, SSM_CHUNKS // SSM_BODY) as i:
                for cc in range(SSM_BODY):
                    buf = cc % 2
                    pe.wait_ge(ssm_landed[buf], i * 32 + 16 * (cc // 2 + 1))
                    n0 = SSM_SIDE0 + cc * (PAIRS + 1)
                    for q in range(PAIRS):
                        n = n0 + q
                        pe.wait_ge(side_read[n % 4], i * 5 + n // 4)
                        for part in range(2):
                            at = (2 * q + part) * P
                            mm = pe.matmul(side_bank(n)[:, part * S:(part + 1) * S], ssm_in[:, buf, at:at + P],
                                           uT[:, bass.ds(i * SSM_BODY + cc, 1), :].rearrange("p a t -> p (a t)"),
                                           start=True, stop=True)
                        mm.then_inc(side_done, 1)
                    mod_units(SSM_PIECE0, range(cc * SSM_BODY, (cc + 1) * SSM_BODY), i)
                    n = n0 + PAIRS
                    pe.wait_ge(side_read[n % 4], i * 5 + n // 4)
                    pe.wait_ge(ssm_cmul, i * SSM_BODY + cc + 1)
                    for q in range(PAIRS):
                        pe.wait_ge(ssm_back, i * (SSM_BODY * PAIRS) + cc * PAIRS + q + 1)
                        back = work[:, SSM_BACK[q % 2], :], work[:, SSM_BACK[2 + q % 2], :]
                        for m, (k, turned, part) in enumerate(((0, 0, 0), (1, 1, 1), (2, 1, 0), (2, 0, 1))):
                            mm = pe.matmul(side_bank(n)[32 * q:32 * q + 32, 0:S], ssm_c[:, buf, k, q, :],
                                           back[turned][:, part * S:(part + 1) * S], start=(m == 0), stop=(m == 3))
                            if m == 3:
                                mm.then_inc(ssm_y, 1)
                mod_turn(SSM_PIECE0, i)
            steps([("unit", "glu", u) for u in range(16)] + BEFORE_S5_OUT + [("unit", "so", u) for u in range(16)])
            pe.wait_ge(late_landed, 16)
            steps(NSA)
            steps(BEFORE_NSA_OUT + [("unit", "no", u) for u in range(16)])

        @block.scalar
        def _(act):
            did = Steps(act, act_steps)

            act.dma_start(cst[:, :], A["cst"]).then_inc(consts_landed, 16)
            act.dma_start(tokens(32), A["mem"].rearrange("(t p) n -> p t n", p=P)).then_inc(mem_landed, 16)
            act.dma_start(early[:, 0:512], A["early"]).then_inc(consts_landed, 16)
            act.dma_start(pos_i, A["positions"].broadcast_to([P, S])).then_inc(pos_landed, 16)
            act.dma_start(x_in, A["x"].rearrange("(t p) n -> p t n", p=P)).then_inc(x_landed, 16)
            act.dma_start(s5_raw, A["s5_raw"]).then_inc(s5_raw_landed, 16)

            def root(n_norm):
                act.wait_ge(norm_mean, n_norm + 1)
                act.activation(stat[:, 2:4], stat[:, 2:4], ACT.Sqrt).then_inc(norm_root, 1)

            def squares(src, n_norm):
                for t in range(TT):
                    if t:
                        did.wait()
                    did(act.activation(junk[:, :], src[:, t, :], ACT.Square, accum_out=stat[:, t:t + 1]))
                did.wait()
                act.nop().then_inc(norm_squares, 1)
                root(n_norm)

            act.wait_ge(consts_landed, 32)
            act.activation(c_act[:, :], vecs[:, V["c"], :], ACT.Silu).then_inc(act_ready, 1)
            act.wait_ge(mem_landed, 16)
            squares(mem_in, 0)
            act.wait_ge(x_landed, 16)
            act.wait_ge(norm_scaled, TT)
            squares(x_in, 1)
            act.wait_ge(s5_raw_landed, 16)
            act.activation(s5_dt, s5_raw[:, 2, :], ACT.Exp).then_inc(s5_ready, 1)
            for which in range(2):
                act.wait_ge(ang_ready, which + 1)
                did(act.activation(ropes[:, 2 * which + 1, :], rope_ang[which], ACT.Sin))
                did(act.activation(rope_abs, rope_ang[which], ACT.Abs))
                did.wait()
                act.activation(ropes[:, 2 * which, :], rope_abs, ACT.Sin, scale=-1.0,
                               bias=half_pi[:, 0:1]).then_inc(rope_ready, 1)
                act.wait_ge(rope_ready, which + 1)
            act.wait_ge(s5_ready, 2)
            did(act.activation(s5_sin, s5_thr, ACT.Sin))
            act.activation(s5_sin2, s5_thr, ACT.Sin, scale=0.5).then_inc(trig_done, 1)

            def exps(a, src, dst, scale):
                at = 16 + 8 * (a % 2)
                did(act.activation(dst[:, 0, :], src[:, 0, :], ACT.Exp, bias=stat[:, at + 2:at + 3], scale=scale,
                                   accum_out=stat[:, at + 4:at + 5]))
                return act.activation(dst[:, 1, :], src[:, 1, :], ACT.Exp, bias=stat[:, at + 3:at + 4], scale=scale,
                                      accum_out=stat[:, at + 5:at + 6])

            def copy_bank(phase, b, dst, func=ACT.Copy):
                act.activation(dst, stream_bank(B0[phase] + b), func).then_inc(evacuated[(B0[phase] + b) % 4], 1)

            T_DST = {"mk": mkT, "mq": mqT, "su": uT, "sz": zT, "nq": qT}
            N_DST = {"mv": mv, "av": av, "rv": rv, "rg": rg}

            def pair(x, b):
                return x[:, 2 * b:2 * b + 2, :].rearrange("p c t -> p (c t)")

            def unit(phase, u):
                if phase in T_DST and u % 2:
                    act.wait_ge(*multiplied(phase, u))
                    copy_bank(phase, u // 2, pair(T_DST[phase], u // 2), ACT.Silu if phase == "sz" else ACT.Copy)
                elif ("rope", phase, u // 2) in ROPE and (u % 2 or phase == "ik"):
                    r = ROPE[("rope", phase, u // 2)]
                    act.wait_ge(*multiplied(phase, u))
                    if r >= 2:
                        act.wait_ge(roped, r - 1)
                    width = S if phase == "ik" else 2 * S
                    b = B0[phase] + u // 2
                    act.activation(work[:, TMP[r % 2], 0:width], stream_bank(b)[:, 0:width],
                                   ACT.Copy).then_inc(evacuated[b % 4], 1)
                elif phase in N_DST and u % 4 == 3:
                    act.wait_ge(*multiplied(phase, u))
                    c = u // 4
                    for t in range(TT):
                        copy_bank(phase, 2 * c + t, N_DST[phase][:, t, c * CHUNK:(c + 1) * CHUNK],
                                  ACT.Silu if phase == "rg" else ACT.Copy)
                elif phase == "kvt" and u % 2 and u >= 8:
                    act.wait_ge(*multiplied(phase, u))
                    copy_bank(phase, u // 2, pair(ksT if u < 12 else kwT, (u // 2) % 2))
                elif phase == "kvn" and u % 4 == 3:
                    act.wait_ge(*multiplied(phase, u))
                    for t in range(TT):
                        copy_bank(phase, u // 4 * 2 + t, (vs if u < 4 else vw)[:, t, :])
                elif phase == "nz" and u % 4 == 3:
                    c = u // 4
                    act.wait_ge(*multiplied(phase, u))
                    if c >= 2:
                        act.wait_ge(o_added, O_AFTER[c - 2])
                    for t in range(TT):
                        copy_bank(phase, 2 * c + t, zs[:, c % 2, t, :], ACT.Silu)

            def side(step):
                kind, n = step[0], SIDE[step]
                done = side_read[n % 4]
                if kind == "norm" and step[1] in ("x2", "x3"):
                    tag, j = step[1:]
                    if j == 0:
                        act.wait_ge(mod_gain, 1 if tag == "x2" else 2)
                    act.wait_ge(*written(n))
                    todo = [(h3T, 0, "s5_shift")] if tag == "x2" else [(hkvT, 1, "kv_shift"), (hnT, 2, "nsa_shift")]
                    for dst, gain, shift in todo:
                        for c in range(2):
                            k = 2 * j + c
                            ins = act.activation(dst[:, k, :], side_bank(n)[:, c * S:(c + 1) * S], ACT.Identity,
                                                 scale=gains[:, gain, k:k + 1], bias=modv[:, PIECES.index(shift), k:k + 1])
                    ins.then_inc(done, 1)
                elif kind == "idx":
                    h = step[1]
                    act.wait_ge(*written(n))
                    if h >= 2:
                        act.wait_ge(idx_added, h - 1)
                    act.activation(work[:, prob[h % 2], :], side_bank(n), ACT.Relu).then_inc(done, 1)
                elif kind == "mem_logits":
                    a = HEADS[step]
                    act.wait_ge(head_max, a + 1)
                    if a >= 2:
                        act.wait_ge(*written(SIDE[TURNS[a - 2]]))
                    exps(a, halves_of(side_bank(n)), halves(prob[a % 2]), 0.0625).then_inc(done, 1)
                elif kind in ("att_logits", "sel_logits", "win_logits"):
                    a = HEADS[step]
                    act.wait_ge(head_max, a + 1)
                    exps(a, halves(prob[a % 2]), halves(prob[a % 2]), HD ** -0.5).then_inc(head_exp, 1)
                elif kind == "cmp_logits":
                    a = HEADS[step]
                    act.wait_ge(head_max, a + 1)
                    p4 = p_cmp.rearrange("p (a n) -> p a n", n=CMP_PAD)[:, :, 0:N_CMP]
                    act.activation(p4, p4, ACT.Exp, scale=HD ** -0.5).then_inc(head_exp, 1)
                elif kind.endswith("_turn"):
                    a = HEADS[(kind[:3] + "_logits", step[1])]
                    act.wait_ge(*written(n))
                    if a >= 2:
                        act.wait_ge(*written(SIDE[VALUES[a - 2]]))
                    width = 2 * P if kind == "cmp_turn" else 2 * S
                    act.activation(work[:, probT[a % 2], 0:width], side_bank(n)[:, 0:width], ACT.Copy).then_inc(done, 1)
                elif kind == "mem_values":
                    act.wait_ge(*written(n))
                    act.activation(pair(o_cT, step[1]), side_bank(n), ACT.Copy).then_inc(done, 1)
                elif kind == "att_values":
                    h = step[1]
                    act.wait_ge(*written(n))
                    act.activation(o_aT[:, h, :], side_bank(n)[:, 0:S], ACT.Copy).then_inc(done, 1)
                    if h == N_ATT - 1:
                        act.dma_start(decay, A["decay"].rearrange("p (h t) -> p h t", h=N_RET)).then_inc(decay_landed, 16)
                elif kind == "ret_values" and step[1] == N_RET - 1:
                    act.wait_ge(ret_var, 1)
                    act.activation(stat[:, 48:64], stat[:, 48:64], ACT.Sqrt).then_inc(ret_root, 1)
                elif kind in ("turn_y", "turn_mix", "turn_o"):
                    dst = {"turn_y": o_bT, "turn_mix": mixT, "turn_o": oT}[kind]
                    act.wait_ge(*written(n))
                    act.activation(pair(dst, step[1]), side_bank(n), ACT.Copy).then_inc(done, 1)
                elif kind == "gate":
                    act.wait_ge(*written(n))
                    act.activation(row[:, step[2] * CHUNK:(step[2] + 1) * CHUNK], side_bank(n), ACT.Copy).then_inc(done, 1)
                elif kind == "cmp_hidden":
                    act.wait_ge(*written(n))
                    act.activation(hid[:, step[1], :], side_bank(n)[:, 0:NKV * N_CMP], ACT.Gelu_apprx_tanh).then_inc(done, 1)
                elif kind == "cmp_out" and step[1] == 0:
                    act.wait_ge(*written(n))
                    act.activation(kcT, side_bank(n)[:, 0:NKV * N_CMP], ACT.Identity, bias=b2_col).then_inc(done, 1)
                elif kind == "ngate":
                    act.wait_ge(*written(n))
                    act.activation(gates.rearrange("p t n -> p (t n)"), side_bank(n)[:, 0:TT * 3 * NQ],
                                   ACT.Sigmoid).then_inc(done, 1)

            def mod_rows(piece, i=None):
                phase = PIECE_PHASE[piece]
                value = U0[phase] + KT
                act.wait_ge(units_done, value if i is None else i * KT + value)
                for c in range(4):
                    b = B0[phase] + c
                    if piece:
                        act.wait_ge(mod_turned, 4 * (piece - 1) + c + 1 if i is None else i * 4 + (4 * (piece - 1) + c + 1))
                        act.wait_ge(consts_made, CONSTS_MADE)
                    act.activation(mod_row[0:1, c * CHUNK:(c + 1) * CHUNK], stream_bank(b)[0:1, :],
                                   ACT.Copy).then_inc(evacuated[b % 4], 1)

            def steps(todo):
                for step in todo:
                    if step[0] == "unit":
                        unit(step[1], step[2])
                    elif step[0] == "mod_units":
                        mod_rows(step[1])
                    elif step[0] != "mod_turn":
                        side(step)

            def branch_out(phase, groups, dst):
                for c in range(4):
                    act.wait_ge(*multiplied(phase, (c + 1) * groups - 1))
                    for t in range(TT):
                        b = B0[phase] + 2 * c + t
                        at = 32 + 4 * t + c
                        if c or t:
                            did.wait()
                        act.activation(dst[:, t, c * CHUNK:(c + 1) * CHUNK], stream_bank(b), ACT.Copy)
                        did(act.activation(work[:, TMP[0], :], stream_bank(b), ACT.Square, accum_out=stat[:, at:at + 1]))
                        did.wait()
                        act.nop().then_inc(evacuated[b % 4], 1)

            def branch_root(n):
                act.wait_ge(res_mean, n + 1)
                act.activation(stat[:, 40:42], stat[:, 40:42], ACT.Sqrt).then_inc(res_root, 1)

            steps(MIXER)
            act.dma_start(xr, A["x"].rearrange("(t p) n -> p t n", p=P)).then_inc(x_again_landed, 16)
            act.dma_start(row, A["g_post_mix"].broadcast_to([P, D])).then_inc(rows_landed, 16)
            act.dma_start(early[:, 0:LATE], A["late"]).then_inc(late_landed, 16)
            with act.Fori(0, 2) as i:
                for m in range(6):
                    b = B0["mix"] + 4 * m
                    u = MIX_UNITS[m]
                    act.wait_ge(units_done, i * 40 + (U0["mix"] + u))
                    for t in range(TT):
                        old = b + t + 2 - 8
                        act.wait_ge(evacuated[old % 4], i * 6 + (old // 4 + 1))
                        act.activation(work[:, (m % 2) * 2 + t, :], stream_bank(b + t),
                                       ACT.Sigmoid).then_inc(evacuated[(b + t) % 4], 1)
            steps(AFTER_MIX)
            branch_out("wo", 4, y)
            branch_root(0)
            act.wait_ge(res_added, TT)
            squares(xr, NORMS["x1"])
            act.dma_start(row, A["g_post_ffn"].broadcast_to([P, D])).then_inc(rows_landed, 16)
            steps(BEFORE_FFN)
            with act.Fori(0, FF_T // 4) as i:
                for k in range(4):
                    b = B0["ff"] + k
                    act.wait_ge(units_done, i * 8 + (U0["ff"] + 2 * k + 2))
                    act.activation(work[:, k, 0:S], stream_bank(b)[:, 0:S], ACT.Silu).then_inc(ff_gate, 1)
            branch_out("fo", FF_T // KG, y2)
            branch_root(1)
            act.wait_ge(res_added, 2 * TT)
            squares(xr, NORMS["x2"])
            steps(BEFORE_S5)
            steps([("unit", "su", u) for u in range(16)] + [("unit", "sz", u) for u in range(16)])

            def tables(value, buf):
                act.wait_ge(ssm_turns, value)
                did(act.activation(whole_t, frac_t, ACT.Identity, bias=round_up[:, 0:1]))
                did.wait()
                act.activation(whole_t, whole_t, ACT.Identity, bias=round_back[:, 0:1]).then_inc(ssm_whole, 1)
                act.wait_ge(ssm_frac, value)
                did(act.activation(abs_t, frac_t, ACT.Abs))
                did(act.activation(sin_t[buf], frac_t, ACT.Sin, scale=TURN_F))
                did.wait()
                act.activation(cos_t[buf], abs_t, ACT.Sin, scale=-TURN_F, bias=half_pi[:, 0:1]).then_inc(ssm_trig, 1)

            act.dma_start(ssm_in[:, 0, :], A["ssm_bc"][0]).then_inc(ssm_landed[0], 16)
            tables(1, 0)
            act.nop().then_inc(ssm_gelu, SSM_GELU0)
            with act.Fori(0, SSM_CHUNKS // SSM_BODY) as i:
                did.enter(i, 3 * SSM_BODY)
                for cc in range(SSM_BODY):
                    buf = (cc + 1) % 2
                    act.wait_ge(ssm_y, i * 16 + SSM_Y0 + 4 * cc)
                    act.dma_start(ssm_in[:, buf, :], A["ssm_bc"][bass.ds(i * SSM_BODY + (cc + 1), 1)]
                                  .rearrange("a p n -> p (a n)")).then_inc(ssm_landed[buf], 16)
                    tables(i * SSM_BODY + (cc + 2), buf)
                    act.wait_ge(ssm_skip, i * SSM_BODY + (cc + 1))
                    act.activation(uT[:, bass.ds(i * SSM_BODY + cc, 1), :].rearrange("p a t -> p (a t)"),
                                   work[:, TMP[0], 0:S], ACT.Gelu_apprx_tanh).then_inc(ssm_gelu, 1)
                mod_rows(SSM_PIECE0, i)
                did.leave(SSM_CHUNKS // SSM_BODY)
            act.wait_ge(ssm_landed[0], 16 * (SSM_CHUNKS // 2 + 1))
            act.wait_ge(ssm_gelu, SSM_CHUNKS + SSM_GELU0)
            act.nop().then_inc(glu_in, 1)
            for b in range(8):
                act.wait_ge(*multiplied("glu", 2 * b + 1))
                for c in range(2):
                    ins = act.activation(work[:, b % 4, c * S:(c + 1) * S], stream_bank(B0["glu"] + b)[:, c * S:(c + 1) * S],
                                         ACT.Sigmoid, bias=vecs[:, V["b_glu"], 2 * b + c:2 * b + c + 1])
                ins.then_inc(glu_gate, 1)
            steps(BEFORE_S5_OUT)
            act.wait_ge(res_added, 3 * TT)
            squares(xr, NORMS["x3"])
            steps(NSA)
            steps(BEFORE_NSA_OUT)
            act.dma_start(final_row, A["final_norm_g"].broadcast_to([P, D])).then_inc(final_row_landed, 16)
            act.wait_ge(res_added, 4 * TT)
            squares(xr, NORMS["out"])

        @block.vector
        def _(dve):
            did = Steps(dve, dve_steps)

            def then(ins):
                did(ins)
                did.wait()

            def rms(n_norm, src, dst):
                dve.wait_ge(norm_squares, n_norm + 1)
                dve.tensor_scalar(stat[:, 2:4], stat[:, 0:2], 1.0 / D, EPS, ALU.mult, ALU.add).then_inc(norm_mean, 1)
                dve.wait_ge(norm_root, n_norm + 1)
                then(dve.reciprocal(stat[:, 4:6], stat[:, 2:4]))
                for t in range(TT):
                    dve.tensor_scalar(dst[:, t, :], src[:, t, :], stat[:, 4 + t:5 + t], None,
                                      ALU.mult).then_inc(norm_scaled, 1)

            dve.wait_ge(consts_landed, 32)
            dve.wait_ge(consts_made, CONSTS_MADE)
            dve.wait_ge(pos_landed, 16)
            then(dve.tensor_copy(rope_pos, pos_i))
            for w in range(2):
                r, k = rope_ang[w], rope_k
                then(dve.tensor_scalar(r, rope_pos, freq[:, w:w + 1], None, ALU.mult))
                then(dve.tensor_scalar(k, r, 1.0 / TURN, ROUND, ALU.mult, ALU.add))
                then(dve.tensor_scalar(k, k, -ROUND, None, ALU.add))
                then(dve.scalar_tensor_tensor(out=r, in0=k, scalar=-TURN_HI, in1=r, op0=ALU.mult, op1=ALU.add))
                then(dve.scalar_tensor_tensor(out=r, in0=k, scalar=-TURN_LO, in1=r, op0=ALU.mult, op1=ALU.add))
                dve.tensor_scalar(r, r, -PI, PI, ALU.max, ALU.min).then_inc(ang_ready, 1)
                dve.wait_ge(ang_ready, w + 1)
            dve.wait_ge(mem_landed, 16)
            rms(0, mem_in, mem_in)
            dve.wait_ge(x_landed, 16)
            rms(1, x_in, x_in)

            lr, li, dt, w_, e_, a_, b_, c_ = (s5_raw[:, 0, :], s5_raw[:, 1, :], s5_dt, s5_tmp[0], s5_tmp[1], s5_tmp[2],
                                             s5_tmp[3], s5_tmp[4])
            mag, turn, kre, kim, nkim = (s5[:, r, 0:SSM_CHUNKS * PAIRS] for r in range(5))
            dve.wait_ge(s5_raw_landed, 16)
            dve.wait_ge(s5_ready, 1)
            then(dve.tensor_tensor(w_, lr, dt, ALU.mult))
            then(dve.tensor_scalar(w_, w_, -20.0, 1.0 / 32, ALU.max, ALU.mult))
            then(dve.tensor_scalar(e_, w_, 1.0 / 8, 1.0, ALU.mult, ALU.add))
            for m in range(7, 1, -1):
                then(dve.tensor_tensor(e_, e_, w_, ALU.mult))
                then(dve.tensor_scalar(e_, e_, 1.0 / m, 1.0, ALU.mult, ALU.add))
            then(dve.tensor_tensor(e_, e_, w_, ALU.mult))
            for _ in range(5):
                then(dve.scalar_tensor_tensor(out=e_, in0=e_, scalar=2.0, in1=e_, op0=ALU.add, op1=ALU.mult))
            then(dve.tensor_scalar(mag, e_, 1.0, None, ALU.add))
            then(dve.tensor_tensor(a_, li, dt, ALU.mult))
            then(dve.tensor_scalar(b_, a_, 1.0 / TURN, ROUND, ALU.mult, ALU.add))
            then(dve.tensor_scalar(b_, b_, -ROUND, None, ALU.add))
            then(dve.scalar_tensor_tensor(out=a_, in0=b_, scalar=-TURN_HI, in1=a_, op0=ALU.mult, op1=ALU.add))
            then(dve.scalar_tensor_tensor(out=a_, in0=b_, scalar=-TURN_LO, in1=a_, op0=ALU.mult, op1=ALU.add))
            then(dve.tensor_scalar(turn, a_, 1.0 / TURN, None, ALU.mult))
            dve.tensor_scalar(s5_thr, a_, -PI, PI, ALU.max, ALU.min).then_inc(s5_ready, 1)
            dve.wait_ge(trig_done, 1)
            then(dve.tensor_tensor(a_, s5_sin, mag, ALU.mult))
            then(dve.tensor_tensor(b_, s5_sin2, s5_sin2, ALU.mult))
            then(dve.tensor_tensor(b_, b_, mag, ALU.mult))
            then(dve.scalar_tensor_tensor(out=e_, in0=b_, scalar=-2.0, in1=e_, op0=ALU.mult, op1=ALU.add))
            then(dve.tensor_tensor(b_, lr, lr, ALU.mult))
            then(dve.tensor_tensor(c_, li, li, ALU.mult))
            then(dve.tensor_tensor(b_, b_, c_, ALU.add))
            then(dve.reciprocal(b_, b_))
            then(dve.tensor_tensor(c_, e_, lr, ALU.mult))
            then(dve.tensor_tensor(w_, a_, li, ALU.mult))
            then(dve.tensor_tensor(c_, c_, w_, ALU.add))
            then(dve.tensor_tensor(kre, c_, b_, ALU.mult))
            then(dve.tensor_tensor(c_, a_, lr, ALU.mult))
            then(dve.tensor_tensor(w_, e_, li, ALU.mult))
            then(dve.tensor_tensor(c_, c_, w_, ALU.subtract))
            then(dve.tensor_tensor(kim, c_, b_, ALU.mult))
            dve.tensor_scalar(nkim, kim, -1.0, None, ALU.mult).then_inc(s5_params, 1)
            dve.wait_ge(s5_params, 1)

            def softmax_tail(a, n, p, masked):
                at = 16 + 8 * (a % 2)
                if masked:
                    dve.wait_ge(head_exp, MASKED[a] + 1)
                else:
                    dve.wait_ge(*read(n))
                then(dve.reciprocal(stat[:, at + 6:at + 8], stat[:, at + 4:at + 6]))
                dve.tensor_tensor(p, p, stat[:, at + 6:at + 8].unsqueeze(2).broadcast_to([P, TT, S]),
                                  ALU.mult).then_inc(head_prob, 1)

            def maximum(a, src, scale):
                at = 16 + 8 * (a % 2)
                then(dve.tensor_reduce(stat[:, at:at + 2], src, AX, ALU.max))
                dve.tensor_scalar(stat[:, at + 2:at + 4], stat[:, at:at + 2], -scale, None, ALU.mult).then_inc(head_max, 1)

            def top_k():
                dve.wait_ge(idx_added, N_IDX)
                for t in range(TT):
                    then(dve.tensor_tensor(top[:, t, :], score[:, t, :], causal[:, t, :], ALU.add))
                    for _ in range(TOPK // 8):
                        then(dve.max(stat[:, 8:16], top[:, t, :]))
                        then(dve.match_replace(out=top[:, t, :], in_to_replace=stat[:, 8:16], in_values=top[:, t, :],
                                               imm_value=TAKEN))
                then(dve.tensor_scalar(top, top, TAKEN, None, ALU.is_equal))
                then(dve.tensor_scalar(top, top, -1.0, -NEG, ALU.add, ALU.mult))
                dve.tensor_tensor(selbias, top, causal, ALU.add).then_inc(sel_ready, 1)
                dve.wait_ge(sel_ready, 1)

            def flat2(ap):
                return ap.rearrange("p (t s) -> p t s", t=TT)

            def side(step):
                kind, n = step[0], SIDE[step]
                done = side_read[n % 4]
                if kind == "norm" and step[1] in ("mem", "x", "x1"):
                    tag, j = step[1:]
                    dst, gain = {"mem": (memT, "g_mem"), "x": (hT, "g_pre_mix"), "x1": (h2T, "g_pre_ffn")}[tag]
                    dve.wait_ge(*written(n))
                    dve.tensor_tensor(dst[:, 2 * j:2 * j + 2, :], flat2(side_bank(n)),
                                      vecs[:, V[gain], 2 * j:2 * j + 2].unsqueeze(2).broadcast_to([P, 2, S]),
                                      ALU.mult).then_inc(done, 1)
                elif kind == "rope":
                    r = ROPE[step]
                    phase, b = step[1:]
                    w = 1 if phase in ("ik", "iq") else 0
                    heads = 1 if phase == "ik" else 2
                    raw = work[:, TMP[r % 2], 0:heads * S].rearrange("p (h t) -> p h t", h=heads)
                    swapped = work[:, TMP[2], 0:heads * S].rearrange("p (h t) -> p h t", h=heads)
                    cos, sin = (ropes[:, 2 * w + k, :].unsqueeze(1).broadcast_to([P, heads, S]) for k in range(2))
                    if r == 0:
                        dve.wait_ge(rope_ready, 2)
                    else:
                        dve.wait_ge(roped, r)
                    dve.wait_ge(*written(n))
                    did(dve.tensor_tensor(raw, raw, cos, ALU.mult))
                    dve.tensor_tensor(swapped, side_bank(n)[:, 0:heads * S].rearrange("p (h t) -> p h t", h=heads), sin,
                                      ALU.mult).then_inc(done, 1)
                    did.wait()
                    dve.wait_ge(*read(n))
                    if phase == "ik":
                        did(dve.tensor_tensor(ikT[0:64, 0, :], raw[0:64, 0, :], swapped[0:64, 0, :], ALU.add))
                        dve.tensor_tensor(ikT[64:128, 1, :], raw[64:128, 0, :], swapped[64:128, 0, :],
                                          ALU.add).then_inc(roped, 1)
                    else:
                        dst = {"iq": iqT, "aq": aqT, "ak": akT, "rq": rqT, "rk": rkT}[phase]
                        dve.tensor_tensor(dst[:, 2 * b:2 * b + 2, :], raw, swapped, ALU.add).then_inc(roped, 1)
                elif kind == "idx_w":
                    dve.wait_ge(*written(n))
                    dve.tensor_scalar(iw[:, :, :], side_bank(n)[:, 0:TT * N_IDX].rearrange("p (t h) -> p t h", t=TT),
                                      64 ** -0.5 * N_IDX ** -0.5, None, ALU.mult).then_inc(done, 1)
                    then(dve.memset(score, 0.0))
                    dve.wait_ge(*read(n))
                elif kind == "idx":
                    h = step[1]
                    dve.wait_ge(*read(n))
                    if h:
                        dve.wait_ge(idx_added, h)
                    for t in range(TT):
                        ins = dve.scalar_tensor_tensor(out=score[:, t, :], in0=halves(prob[h % 2])[:, t, :],
                                                       scalar=iw[:, t, h:h + 1], in1=score[:, t, :], op0=ALU.mult,
                                                       op1=ALU.add)
                    ins.then_inc(idx_added, 1)
                    if h == N_IDX - 1:
                        top_k()
                elif kind == "mem_logits":
                    a = HEADS[step]
                    dve.wait_ge(*written(n))
                    maximum(a, flat2(side_bank(n)), 0.0625)
                    softmax_tail(a, n, halves(prob[a % 2]), False)
                elif kind in ("att_logits", "sel_logits", "win_logits"):
                    a = HEADS[step]
                    p = halves(prob[a % 2])
                    dve.wait_ge(*written(n))
                    dve.wait_ge(*written(SIDE[TURNS[a - 2]]))
                    dve.tensor_tensor(p, flat2(side_bank(n)), selbias if kind == "att_logits" else causal,
                                      ALU.add).then_inc(done, 1)
                    dve.wait_ge(*read(n))
                    maximum(a, p, HD ** -0.5)
                    softmax_tail(a, n, p, True)
                elif kind == "ret_scores":
                    h = step[1]
                    if h == 0:
                        dve.wait_ge(decay_landed, 16)
                    dve.wait_ge(*written(n))
                    if h >= 2:
                        dve.wait_ge(*written(SIDE[("ret_values", h - 2)]))
                    sd = work[:, prob[h % 2], :]
                    dve.tensor_tensor(sd[:, 0:S], side_bank(n)[:, 0:S], decay[:, h, :], ALU.mult)
                    dve.tensor_tensor(sd[:, S:S + P], side_bank(n)[:, S:S + P], decay[:, h, 0:P],
                                      ALU.mult).then_inc(done, 1)
                elif kind == "ret_values":
                    h = step[1]
                    dve.wait_ge(*written(n))
                    if h:
                        did.wait()
                    for t in range(TT):
                        did(dve.bn_stats(bn[:, t, :], side_bank(n)[:, t * RETV:(t + 1) * RETV]))
                    did.wait()
                    for t in range(TT):
                        k = TT * h + t
                        did(dve.bn_aggr(ret_stat[:, k, :], bn[:, t, :]))
                    dve.tensor_copy(rv[:, :, h * RETV:(h + 1) * RETV], flat2(side_bank(n))).then_inc(done, 1)
                    if h == N_RET - 1:
                        dve.wait_ge(*read(n))
                        did.wait()
                        dve.tensor_scalar(stat[:, 48:64], ret_stat[:, :, 1], EPS, None, ALU.add).then_inc(ret_var, 1)
                        dve.wait_ge(ret_root, 1)
                        then(dve.reciprocal(stat[:, 48:64], stat[:, 48:64]))
                        for hh in range(N_RET):
                            for t in range(TT):
                                k = TT * hh + t
                                yh = rv[:, t, hh * RETV:(hh + 1) * RETV]
                                did(dve.tensor_scalar(yh, yh, ret_stat[:, k, 0:1], stat[:, 48 + k:49 + k],
                                                      ALU.subtract, ALU.mult))
                        did.wait()
                        for w in last_banks("rg"):
                            dve.wait_ge(*w)
                        dve.tensor_tensor(rv, rv, rg, ALU.mult).then_inc(ret_gated, 1)
                elif kind == "gate":
                    tag, j = step[1:]
                    piece = PIECES.index(tag + "_gate")
                    g = GATES[step]
                    if tag == "nsa" and j == 0:
                        dve.wait_ge(o_added, O_ADDS)
                    if j >= 2:
                        dve.wait_ge(*written(SIDE[(kind, tag, j - 2)]))
                    for c in range(4):
                        k = 4 * j + c
                        ins = dve.tensor_scalar(work[:, TMP[j % 2], c * P:(c + 1) * P], ident, modv[:, piece, k:k + 1],
                                                None, ALU.mult)
                    ins.then_inc(diag_ready, 1)
                elif kind == "cmp_hidden" and step[1] == 0:
                    then(dve.memset(p_cmp, 0.0))
                elif kind == "cmp_out" and step[1] == 1:
                    dve.wait_ge(*written(n))
                    dve.tensor_tensor(v_tmp[0:N_CMP, :, :],
                                      side_bank(n)[0:N_CMP, :].rearrange("p (g d) -> p g d", g=NKV),
                                      b2_row[0:N_CMP, :].unsqueeze(1).broadcast_to([N_CMP, NKV, P]),
                                      ALU.add).then_inc(done, 1)
                    dve.wait_ge(*read(n))
                    dve.wait_ge(v_zero, 1)
                    for h in range(HPG):
                        ins = dve.tensor_copy(v_blocks[32 * h:32 * h + N_CMP, :, h * P:(h + 1) * P], v_tmp[0:N_CMP, :, :])
                    ins.then_inc(cmp_vblock, 1)
                elif kind == "cmp_logits":
                    a, g = HEADS[step], step[1]
                    p4 = p_cmp.rearrange("p (t h n) -> p t h n", t=TT, h=HPG)[:, :, :, 0:N_CMP]
                    p3 = p_cmp.rearrange("p (a n) -> p a n", n=CMP_PAD)[:, :, 0:N_CMP]
                    add, keep = (m.unsqueeze(2).broadcast_to([P, TT, HPG, N_CMP]) for m in (cmp_add, cmp_keep))
                    logit4 = side_bank(n)[:, 0:2 * P].rearrange("p (t h n) -> p t h n", t=TT, h=HPG)[:, :, :, 0:N_CMP]
                    st = stat[:, 8:16]

                    def row_of(x):
                        return x.unsqueeze(2).broadcast_to([P, TT * HPG, N_CMP])

                    dve.wait_ge(*written(n))
                    if g:
                        dve.wait_ge(*written(SIDE[("cmp_turn", g - 1)]))
                    dve.tensor_tensor(p4, logit4, add, ALU.add).then_inc(done, 1)
                    dve.wait_ge(*read(n))
                    then(dve.tensor_reduce(st, p3, AX, ALU.max))
                    dve.tensor_tensor(p3, p3, row_of(st), ALU.subtract).then_inc(head_max, 1)
                    dve.wait_ge(head_exp, MASKED[a] + 1)
                    then(dve.tensor_reduce(st, p3, AX, ALU.add))
                    then(dve.reciprocal(st, st))
                    then(dve.tensor_tensor(p4, p4, keep, ALU.mult))
                    dve.tensor_tensor(p3, p3, row_of(st), ALU.mult).then_inc(head_prob, 1)
                elif kind in ("cmp_values", "sel_values", "win_values"):
                    br = ("cmp", "sel", "win").index(kind[:3])
                    g = step[1] if br == 0 else step[1] // HPG
                    c = 3 * g + br
                    k = O_INDEX[step]
                    dve.wait_ge(*written(n))
                    if k == 0:
                        dve.wait_ge(*read(SIDE[("ngate", 0)]))
                    else:
                        dve.wait_ge(o_added, k)
                    for w in (emptied(B0["nz"] + 2 * c), emptied(B0["nz"] + 2 * c + 1)):
                        dve.wait_ge(*w)
                    if br == 0:
                        t = step[2]
                        head = gates[:, t, HPG * g:HPG * (g + 1)].unsqueeze(2).broadcast_to([P, HPG, P])
                        part = work[:, TMP[1], :]
                        dve.tensor_tensor(part.rearrange("p (h d) -> p h d", h=HPG),
                                          side_bank(n).rearrange("p (h d) -> p h d", h=HPG), head, ALU.mult).then_inc(done, 1)
                        dve.wait_ge(*read(n))
                        dve.tensor_tensor(o_tok[:, t, g * CHUNK:(g + 1) * CHUNK], part, zs[:, c % 2, t, :],
                                          ALU.mult).then_inc(o_added, 1)
                    else:
                        h = step[1]
                        part = work[:, TMP[1], 0:2 * P].rearrange("p (t d) -> p t d", t=TT)
                        gate = gates[:, :, br * NQ + h:br * NQ + h + 1].broadcast_to([P, TT, P])
                        at, o = (h % HPG) * P, o_tok[:, :, h * P:(h + 1) * P]
                        dve.tensor_tensor(part, side_bank(n)[:, 0:2 * P].rearrange("p (t d) -> p t d", t=TT), gate,
                                          ALU.mult).then_inc(done, 1)
                        dve.wait_ge(*read(n))
                        then(dve.tensor_tensor(part, part, zs[:, c % 2, :, at:at + P], ALU.mult))
                        dve.tensor_tensor(o, o, part, ALU.add).then_inc(o_added, 1)

            def unit(phase, u):
                if phase == "kvt" and u % 2 and u < 8:
                    j, b = u // 4, B0["kvt"] + u // 2
                    dve.wait_ge(*multiplied(phase, u))
                    g0 = 2 * (u // 2 % 2)
                    for half in range(2):
                        pe_ = cmp_pe[:, j, half * CMP_STRIDE:(half + 1) * CMP_STRIDE]
                        ins = dve.tensor_tensor(
                            cin[:, j, half, g0:g0 + 2, :].rearrange("p g (n r) -> p (g n) r", r=CMP_STRIDE),
                            stream_bank(b).rearrange("p (m r) -> p m r", r=CMP_STRIDE),
                            pe_.unsqueeze(1).broadcast_to([P, 2 * S // CMP_STRIDE, CMP_STRIDE]), ALU.add)
                    ins.then_inc(evacuated[b % 4], 1)

            def mod_vec(piece, i=None):
                for c in range(4):
                    b = B0[PIECE_PHASE[piece]] + 4 + c
                    k = slice(4 * c, 4 * c + 4)
                    value = 4 * piece + c + 1
                    dve.wait_ge(mod_turned, value if i is None else i * 4 + value)
                    if i is None:
                        dst, bias = modv[:, piece, k], vecs[:, V[PIECES[piece]], k]
                    else:
                        dst = modv[:, bass.ds(i + piece, 1), k].rearrange("p a k -> p (a k)")
                        bias = vecs[:, bass.ds(i + V[PIECES[piece]], 1), k].rearrange("p a k -> p (a k)")
                    dve.tensor_tensor(dst, stream_bank(b)[:, 0:4], bias, ALU.add).then_inc(evacuated[b % 4], 1)

            def steps(todo):
                for step in todo:
                    if step[0] == "unit":
                        unit(step[1], step[2])
                    elif step[0] == "mod_turn":
                        mod_vec(step[1])
                    elif step[0] != "mod_units":
                        side(step)

            def add_branch(n, phase, src):
                for w in last_banks(phase):
                    dve.wait_ge(*w)
                then(dve.tensor_reduce(stat[:, 40:42], stat[:, 32:40].rearrange("p (t c) -> p t c", t=TT), AX, ALU.add))
                dve.tensor_scalar(stat[:, 40:42], stat[:, 40:42], 1.0 / D, EPS, ALU.mult, ALU.add).then_inc(res_mean, 1)
                dve.wait_ge(res_root, n + 1)
                then(dve.reciprocal(stat[:, 42:44], stat[:, 40:42]))
                dve.wait_ge(rows_landed, 16 * (n + 1))
                if n == 0:
                    dve.wait_ge(x_again_landed, 16)
                for t in range(TT):
                    then(dve.scalar_tensor_tensor(out=src[:, t, :], in0=src[:, t, :], scalar=stat[:, 42 + t:43 + t],
                                                  in1=row, op0=ALU.mult, op1=ALU.mult))
                    dve.tensor_tensor(xr[:, t, :], xr[:, t, :], src[:, t, :], ALU.add).then_inc(res_added, 1)

            def add_gated(n, phase, tag):
                for w in last_reads([SIDE[("gate", tag, j)] for j in range(4)]):
                    dve.wait_ge(*w)
                for c in range(4):
                    dve.wait_ge(*multiplied(phase, 4 * c + 3))
                    for t in range(TT):
                        b = B0[phase] + 2 * c + t
                        part, x = work[:, TMP[t], :], xr[:, t, c * CHUNK:(c + 1) * CHUNK]
                        if c:
                            dve.wait_ge(res_added, TT * n)
                            did.wait()
                        dve.tensor_tensor(part, stream_bank(b), row[:, c * CHUNK:(c + 1) * CHUNK],
                                          ALU.mult).then_inc(evacuated[b % 4], 1)
                        dve.wait_ge(*emptied(b))
                        add = dve.tensor_tensor(x, x, part, ALU.add)
                        if c == 3:
                            add.then_inc(res_added, 1)
                        else:
                            did(add)

            steps(MIXER)
            with dve.Fori(0, 2) as i:
                for m in range(6):
                    c, br = divmod(m, 3)
                    b = B0["mix"] + 4 * m + 2
                    dve.wait_ge(units_done, i * 40 + (U0["mix"] + MIX_ENDS[m]))
                    for t in range(TT):
                        dst = mixed[:, t, bass.ds((i * 2 + c) * CHUNK, CHUNK)]
                        gate = work[:, (m % 2) * 2 + t, :]
                        dve.wait_ge(evacuated[(b - 2 + t) % 4], i * 6 + ((b - 2 + t) // 4 + 1))
                        if br == 0:
                            dve.tensor_tensor(dst, stream_bank(b + t), gate, ALU.mult).then_inc(evacuated[(b + t) % 4], 1)
                        else:
                            dve.tensor_tensor(gate, stream_bank(b + t), gate, ALU.mult).then_inc(mix_part, 1)
                            dve.wait_ge(mix_part, i * 8 + (c * 4 + (br - 1) * 2 + t + 1))
                            dve.wait_ge(evacuated[(b - 4 + t) % 4], i * 6 + ((b - 4 + t) // 4 + 1))
                            dve.tensor_tensor(dst, dst, gate, ALU.add).then_inc(evacuated[(b + t) % 4], 1)
            for w in last_banks("mix"):
                dve.wait_ge(*w)
            dve.nop().then_inc(mix_done, 1)
            steps(AFTER_MIX)
            add_branch(0, "wo", y)
            rms(NORMS["x1"], xr, xn)
            steps(BEFORE_FFN)
            with dve.Fori(0, FF_T // 4) as i:
                for k in range(4):
                    b = B0["ff"] + k
                    dve.wait_ge(ff_gate, i * 4 + (k + 1))
                    dve.tensor_tensor(actT[:, bass.ds(i * 4 + k, 1), :].rearrange("p a t -> p (a t)"),
                                      stream_bank(b)[:, S:2 * S], work[:, k, 0:S], ALU.mult).then_inc(evacuated[b % 4], 1)
            add_branch(1, "fo", y2)
            rms(NORMS["x2"], xr, xn)

            def modulation(row_, gain, scale, n):
                ins = dve.scalar_tensor_tensor(out=gains[:, row_, :], in0=modv[:, PIECES.index(scale), :], scalar=1.0,
                                               in1=vecs[:, V[gain], :], op0=ALU.add, op1=ALU.mult)
                ins.then_inc(mod_gain, 1) if n else did(ins)

            dve.wait_ge(*emptied(B0["m1"] + 7))
            modulation(0, "norm0", "s5_scale", 1)
            steps(BEFORE_S5)
            n_pairs = SSM_BODY * PAIRS
            with dve.Fori(0, SSM_CHUNKS // SSM_BODY) as i:
                did.enter(i, n_pairs * 3)
                for cc in range(SSM_BODY):
                    tab = cc % 2
                    n0 = SSM_SIDE0 + cc * (PAIRS + 1)
                    dve.wait_ge(ssm_trig, i * SSM_BODY + (cc + 1))
                    for q in range(PAIRS):
                        p, n = cc * PAIRS + q, n0 + q
                        one, two = work[:, q % 2, :], work[:, 2 + q % 2, :]
                        cos, sin = (x[tab][:, q * S:(q + 1) * S].unsqueeze(1).broadcast_to([P, 2, S])
                                    for x in (cos_t, sin_t))
                        dve.wait_ge(side_done, i * n_pairs + (SSM_SIDE0 + p + 1))
                        dve.wait_ge(ssm_y, i * n_pairs + max(p - 1 + SSM_Y0, 1))
                        did(dve.tensor_tensor(flat2(one), flat2(side_bank(n)), cos, ALU.mult))
                        did(dve.tensor_tensor(flat2(two), flat2(side_bank(n)), sin, ALU.mult))
                        did.wait()
                        dve.nop().then_inc(side_read[n % 4], 1)
                        dve.nop().then_inc(ssm_prod, 1)
                        dve.wait_ge(ssm_rot, i * n_pairs + (p + 1))
                        col = s5[:, S_MAG, bass.ds(i * n_pairs + p, 1)]
                        for part in range(2):
                            z = one[:, part * S:(part + 1) * S]
                            ins = dve.tensor_tensor_scan(z, col.broadcast_to([P, S]), z, 0.0, ALU.mult, ALU.add)
                        did(ins)
                        did.wait()
                        dve.tensor_tensor(flat2(two), flat2(one), cos, ALU.mult).then_inc(ssm_state, 1)
                        dve.wait_ge(ssm_state, i * n_pairs + (p + 1))
                        dve.tensor_tensor(flat2(one), flat2(one), sin, ALU.mult).then_inc(ssm_back, 1)
                    n = n0 + PAIRS
                    dve.wait_ge(ssm_y, i * n_pairs + (PAIRS * (cc + 1) + SSM_Y0))
                    dve.wait_ge(ssm_gelu, i * SSM_BODY + (cc + SSM_GELU0))
                    d_col = vecs[:, V["d_skip"], bass.ds(i * SSM_BODY + cc, 1)]
                    dve.scalar_tensor_tensor(out=work[:, TMP[0], 0:S],
                                             in0=uT[:, bass.ds(i * SSM_BODY + cc, 1), :].rearrange("p a t -> p (a t)"),
                                             scalar=d_col, in1=side_bank(n)[:, 0:S], op0=ALU.mult,
                                             op1=ALU.add).then_inc(ssm_skip, 1)
                    dve.wait_ge(ssm_skip, i * SSM_BODY + (cc + 1))
                    dve.nop().then_inc(side_read[n % 4], 1)
                    if cc == SSM_BODY - 1:
                        mod_vec(SSM_PIECE0, i)
                did.leave(SSM_CHUNKS // SSM_BODY)
            dve.wait_ge(*emptied(B0["ms"] + 31))
            modulation(1, "kv_norm", "kv_scale", 0)
            modulation(2, "norm1", "nsa_scale", 1)
            for b in range(8):
                sig = work[:, b % 4, :].rearrange("p (c t) -> p c t", c=2)
                zz = zT[:, 2 * b:2 * b + 2, :]
                dve.wait_ge(glu_gate, b + 1)
                then(dve.tensor_tensor(sig, sig, uT[:, 2 * b:2 * b + 2, :], ALU.mult))
                dve.tensor_tensor(zz, zz, sig, ALU.mult).then_inc(evacuated[(B0["glu"] + b) % 4], 1)
            steps(BEFORE_S5_OUT)
            add_gated(2, "so", "s5")
            rms(NORMS["x3"], xr, xn)
            dve.wait_ge(late_landed, 16)
            steps(NSA)
            steps(BEFORE_NSA_OUT)
            add_gated(3, "no", "nsa")
            n_norm = NORMS["out"]
            dve.wait_ge(norm_squares, n_norm + 1)
            dve.tensor_scalar(stat[:, 2:4], stat[:, 0:2], 1.0 / D, EPS, ALU.mult, ALU.add).then_inc(norm_mean, 1)
            dve.wait_ge(norm_root, n_norm + 1)
            then(dve.reciprocal(stat[:, 4:6], stat[:, 2:4]))
            dve.wait_ge(final_row_landed, 16)
            for t in range(TT):
                dve.scalar_tensor_tensor(out=y_out[:, t, :], in0=xr[:, t, :], scalar=stat[:, 4 + t:5 + t], in1=final_row,
                                         op0=ALU.mult, op1=ALU.mult).then_inc(out_ready, 1)

        @block.gpsimd
        def _(pool):
            did = Steps(pool, pool_steps)

            pool.memset(ones[:, :], 1.0).then_inc(consts_made, 1)
            pool.memset(half_pi[:, :], float(np.pi / 2)).then_inc(consts_made, 1)
            pool.memset(round_up[:, :], ROUND).then_inc(consts_made, 1)
            pool.memset(round_back[:, :], -ROUND).then_inc(consts_made, 1)
            pool.memset(ikT, 0.0).then_inc(consts_made, 1)
            pool.memset(s5[:, :, :], 0.0).then_inc(consts_made, 1)
            pool.memset(v_blocks[:, :, :], 0.0).then_inc(v_zero, 1)

            f4 = frac_t.rearrange("p (q t) -> p q t", q=PAIRS)
            times = time_row.unsqueeze(1).broadcast_to([P, PAIRS, S])

            pool.wait_ge(s5_params, 1)
            for w in last_banks("su"):
                pool.wait_ge(*w)
            pool.tensor_tensor(f4, times, s5[:, S_TURN, 0:PAIRS].unsqueeze(2).broadcast_to([P, PAIRS, S]),
                               ALU.mult).then_inc(ssm_turns, 1)
            pool.wait_ge(ssm_whole, 1)
            pool.tensor_tensor(frac_t, frac_t, whole_t, ALU.subtract).then_inc(ssm_frac, 1)
            n_pairs = SSM_BODY * PAIRS
            with pool.Fori(0, SSM_CHUNKS // SSM_BODY) as i:
                did.enter(i, SSM_BODY * (6 + PAIRS))
                for cc in range(SSM_BODY):
                    buf = cc % 2
                    pool.wait_ge(ssm_landed[buf], i * 32 + 16 * (cc // 2 + 1))
                    c_re, c_im = (ssm_in[:, buf, SSM_B + k * P:SSM_B + (k + 1) * P].rearrange("p (q c) -> p q c", q=PAIRS)
                                  for k in range(2))
                    f_re, f_im, f_neg = (s5[:, r, bass.ds(i * n_pairs + cc * PAIRS, PAIRS)].unsqueeze(2)
                                  .broadcast_to([P, PAIRS, 32]) for r in (S_KRE, S_KIM, S_NKIM))
                    k0, k1, k2 = (ssm_c[:, buf, k, :, :] for k in range(3))
                    t0, t1 = (area(61, 2 * P)[:, k * P:(k + 1) * P].rearrange("p (q c) -> p q c", q=PAIRS) for k in range(2))
                    did(pool.tensor_tensor(t0, c_re, f_re, ALU.mult))
                    did(pool.tensor_tensor(t1, c_im, f_im, ALU.mult))
                    did.wait()
                    did(pool.tensor_tensor(k0, t0, t1, ALU.subtract))
                    did(pool.tensor_tensor(k1, t1, t0, ALU.subtract))
                    did.wait()
                    did(pool.tensor_tensor(t0, c_re, f_neg, ALU.mult))
                    did(pool.tensor_tensor(t1, c_im, f_re, ALU.mult))
                    did.wait()
                    pool.tensor_tensor(k2, t0, t1, ALU.subtract).then_inc(ssm_cmul, 1)
                    pool.wait_ge(ssm_cmul, i * SSM_BODY + (cc + 1))
                    for q in range(PAIRS):
                        p = cc * PAIRS + q
                        one, two = work[:, q % 2, :], work[:, 2 + q % 2, :]
                        pool.wait_ge(ssm_prod, i * n_pairs + (p + 1))
                        did(pool.tensor_tensor(one[:, 0:S], one[:, 0:S], two[:, S:2 * S], ALU.add))
                        pool.tensor_tensor(one[:, S:2 * S], one[:, S:2 * S], two[:, 0:S], ALU.subtract).then_inc(ssm_rot, 1)
                        if q == 0:
                            turn = s5[:, S_TURN, bass.ds(i * n_pairs + (cc + 1) * PAIRS, PAIRS)]
                            pool.wait_ge(ssm_trig, i * SSM_BODY + (cc + 1))
                            pool.tensor_tensor(f4, times, turn.unsqueeze(2).broadcast_to([P, PAIRS, S]),
                                               ALU.mult).then_inc(ssm_turns, 1)
                        if q == 1:
                            pool.wait_ge(ssm_whole, i * SSM_BODY + (cc + 2))
                            pool.tensor_tensor(frac_t, frac_t, whole_t, ALU.subtract).then_inc(ssm_frac, 1)
                did.leave(SSM_CHUNKS // SSM_BODY)



def t_units(w):
    k, n = w.shape
    return w.reshape(k // P, P, n // P, P).transpose(2, 1, 0, 3).reshape(n // P, P, -1)


def n_units(w):
    k, n = w.shape
    return w.reshape(k // (KG * P), KG, P, n // CHUNK, CHUNK).transpose(3, 0, 2, 1, 4).reshape(-1, P, UNIT)


def kernel(**inputs):
    import concourse.bacc as bacc
    from concourse.bass_utils import run_bass_kernel_spmd

    x = {n: np.asarray(a) for n, a in inputs.items()}
    f = np.float32

    w = x["w_in"][0]
    cols, at = {}, 0
    for name, n in (("aq", 1024), ("ak", 1024), ("av", 1024), ("iq", 1024), ("ik", 64), ("iw", 16), ("rq", 1024),
                    ("rk", 1024), ("rv", 2048), ("rg", 2048), ("mq", 1024), ("ga", D), ("gb", D), ("gc", D)):
        cols[name] = w[:, at:at + n]
        at += n
    mem_kv, kv = x["w_mem_kv"][0], x["w_kv_2"]
    qg = x["nsa_w_qg_2"][0]
    s_in = x["ssm_w_in_2"][0]
    ff = x["w_ffn_in"][0]
    mix = [n_units(cols["ga"]).reshape(4, 4, P, UNIT), n_units(x["w_branch_a"][0]).reshape(4, 2, P, UNIT),
           n_units(cols["gb"]).reshape(4, 4, P, UNIT), n_units(x["w_branch_b"][0]).reshape(4, 4, P, UNIT),
           n_units(cols["gc"]).reshape(4, 4, P, UNIT), n_units(x["w_branch_c"][0]).reshape(4, 2, P, UNIT)]
    gate_up = np.stack([t_units(ff[:, :FF_T * P]), t_units(ff[:, FF_T * P:])], 1).reshape(2 * FF_T, P, UNIT)
    kv_cols = kv.reshape(D, 6, NKV * HD)
    cw = x["cmp_w1_2"].reshape(2, 2, CMP_STRIDE, HD, HD).transpose(0, 1, 3, 2, 4).reshape(4, P, UNIT)
    z = qg[:, NQ * HD + 3 * NQ:].reshape(D, 3, NKV, HPG * HD).transpose(0, 2, 1, 3).reshape(D, 3 * NQ * HD)
    mod_w, kvm = x["mod_w_2"], x["kv_mod_w_2"]
    m = [a.reshape(KT, P, D) for a in (mod_w[0][:, D:2 * D], mod_w[0][:, :D], kvm[:, :D], mod_w[0][:, 2 * D:], kvm[:, D:],
                                       mod_w[1][:, :D], mod_w[1][:, D:2 * D], mod_w[1][:, 2 * D:])]
    parts = [
        m[0],
        t_units(mem_kv[:, :1024]), n_units(mem_kv[:, 1024:]), t_units(cols["mq"]),
        t_units(np.concatenate([cols["ik"], cols["ik"]], 1)), t_units(cols["iq"]), t_units(cols["aq"]),
        n_units(cols["av"]), t_units(cols["ak"]), t_units(cols["rq"]), t_units(cols["rk"]), n_units(cols["rv"]),
        n_units(cols["rg"]), np.concatenate(mix, 1).reshape(-1, P, UNIT), n_units(x["w_out"][0]), m[1], gate_up,
        n_units(x["w_ffn_out"][0]), m[2], t_units(s_in[:, :D]), t_units(s_in[:, D:]), *m[3:7],
        t_units(x["ssm_w_glu_2"][0]), n_units(x["ssm_w_out_2"][0]), m[7], t_units(kv_cols[:, [0, 1, 2, 4]].reshape(D, -1)), cw,
        n_units(kv_cols[:, [3, 5]].reshape(D, -1)), t_units(qg[:, :NQ * HD]), n_units(z), n_units(x["nsa_w_o_2"][0]),
        np.zeros((STREAM_UNITS - UNITS, P, UNIT), f),
    ]
    mod_b, kvb = x["mod_b_2"], x["kv_mod_b_2"]
    biases = [mod_b[0][D:2 * D], mod_b[0][:D], kvb[:D], mod_b[0][2 * D:], kvb[D:], mod_b[1][:D], mod_b[1][D:2 * D],
              mod_b[1][2 * D:]]

    def on_partitions(v):
        return v.reshape(-1, P).T

    vec_rows = [x["g_pre_mix"][0], x["g_mem"][0], x["g_pre_ffn"][0], x["norm_g_2"][0], x["norm_g_2"][1],
                x["kv_norm_g_2"], x["c_2"][0], x["ssm_b_glu_2"][0], x["ssm_d_2"][0], *biases]

    pos = np.arange(S)
    tok = pos.reshape(TT, P).T
    causal = np.where(pos[None, None] <= tok[:, :, None], 0.0, NEG).astype(f)
    perms = np.zeros((P, 2, P), f)
    freq = np.zeros((P, 2), f)
    for k, d in enumerate((HD, 64)):
        for m in range(P):
            head, r = divmod(m, d)
            perms[head * d + (r + d // 2) % d, k, m] = -1.0 if r < d // 2 else 1.0
        fr = np.power(f(10000.0), (-np.arange(0, d, 2, dtype=f) / f(d)).astype(f)).astype(f)
        freq[:, k] = np.tile(np.concatenate([fr, fr]), P // d)
    log_gamma = np.log1p(-np.exp2(-5.0 - np.arange(N_RET)))
    gap = pos[None, :] - np.arange(P)[:, None]
    decay = np.where(gap[:, None] >= 0, np.exp(np.maximum(gap, 0)[:, None] * log_gamma[None, :, None]), 0.0) * HD ** -0.5
    ends = np.arange(N_CMP) * CMP_STRIDE + CMP_LEN - 1
    keep = (ends[None, None] <= tok[:, :, None])

    cst = np.concatenate([np.eye(P, dtype=f), causal.reshape(P, -1), np.broadcast_to(pos.astype(f), (P, S)),
                          np.concatenate([on_partitions(v) for v in vec_rows], 1), freq], 1)
    w_iw = cols["iw"].reshape(KT, P, N_IDX).transpose(1, 0, 2).reshape(P, -1)
    w_ng = qg[:, NQ * HD:NQ * HD + 3 * NQ].reshape(KT, P, 3 * NQ).transpose(1, 0, 2).reshape(P, -1)
    b1 = np.zeros((P, 2, HD), f)
    b1[0] = x["cmp_b1_2"]
    late = np.concatenate([
        w_ng, x["cmp_w2_2"].transpose(1, 0, 2).reshape(P, -1), b1.reshape(P, -1),
        np.broadcast_to(x["cmp_b2_2"][1], (P, HD)), x["cmp_pe_2"].transpose(2, 0, 1).reshape(P, -1),
        np.where(keep, 0.0, NEG).reshape(P, -1), keep.reshape(P, -1).astype(f), x["cmp_b2_2"][0][:, None]], 1)

    def states(a):
        return a.reshape(-1, P).T
    step = np.repeat(x["ssm_log_step_2"][0][:, None], 64, 1)
    s5_raw = np.stack([states(x["ssm_lam_re_2"][0]), states(x["ssm_lam_im_2"][0]), states(step)], 1)
    bc = np.zeros((SSM_CHUNKS + 1, P, SSM_COLS), f)
    bmat = bc[:SSM_CHUNKS, :, :SSM_B].reshape(SSM_CHUNKS, PAIRS, 2, 16, PAIRS, 2, 2, 64)
    cmat = np.zeros((SSM_CHUNKS, 2, 64, 2, PAIRS, 2, 16), f)
    for part, name in enumerate(("ssm_b_re_2", "ssm_b_im_2")):
        b = x[name][0].reshape(SSM_CHUNKS, PAIRS, 2, 64, 16)
        for q in range(PAIRS):
            for g in range(2):
                bmat[:, q, g, :, q, part, g, :] = b[:, q, g].transpose(0, 2, 1)
    bc[:SSM_CHUNKS, :, :SSM_B] = bmat.reshape(SSM_CHUNKS, P, SSM_B)
    for part, name in enumerate(("ssm_c_re_2", "ssm_c_im_2")):
        c = x[name][0].reshape(SSM_CHUNKS, PAIRS, 2, 16, 64)
        for g in range(2):
            cmat[:, g, :, part, :, g, :] = c[:, :, g].transpose(0, 3, 1, 2)
    bc[:SSM_CHUNKS, :, SSM_B:] = cmat.reshape(SSM_CHUNKS, P, SSM_C)

    arrays = {
        "stream": np.concatenate(parts),
        "x": x["x"][0], "mem": x["mem"][0], "positions": x["positions"], "cst": cst,
        "early": np.concatenate([perms.reshape(P, -1), w_iw], 1), "late": late, "decay": decay.reshape(P, -1),
        "s5_raw": s5_raw, "ssm_bc": bc, "g_post_mix": x["g_post_mix"], "g_post_ffn": x["g_post_ffn"],
        "final_norm_g": x["final_norm_g_2"][None],
    }
    arrays = {n: np.ascontiguousarray(a if a.dtype.kind in "iu" else a.astype(f, copy=False)) for n, a in arrays.items()}
    nc = bacc.Bacc("TRN2", target_bir_lowering=False, num_devices=1)
    A = {n: nc.dram_tensor("in_" + n, a.shape, mybir.dt.from_np(a.dtype), kind="ExternalInput").ap() for n, a in arrays.items()}
    out = nc.dram_tensor("out_0", (S, D), F32, kind="ExternalOutput").ap()
    program(nc, A, out)
    r = run_bass_kernel_spmd(nc, [{"in_" + n: a for n, a in arrays.items()}], core_ids=[0])
    return r.results[0]["out_0"].reshape(1, S, D)
```

```python
from contextlib import ExitStack

import concourse.bass as bass
import numpy as np
from concourse import mybir

F32 = mybir.dt.float32
F32R = mybir.dt.float32r
I32 = mybir.dt.int32
ALU = mybir.AluOpType
ACT = mybir.ActivationFunctionType
AX = mybir.AxisListType.X

P = 128
S = 256
D = 2048
TT = S // P
KT = D // P
EPS = 1e-6
NEG = -1e30
TAKEN = -3e38
N_ATT, N_IDX, N_RET, N_MEM = 8, 16, 8, 4
TOPK = min(256, S // 4)
FF_T = 5632 // P
NQ, NKV, HPG, HD = 16, 4, 4, 128
CMP_STRIDE, CMP_LEN = 16, 32
N_CMP = (S - CMP_LEN) // CMP_STRIDE + 1
ROUND = 1.5 * 2.0 ** 23
TURN = 2 * np.pi
TURN_HI = 6.28125
TURN_LO = float(np.float32(TURN - 6.28125))
PI = 3.1415925
RING, UNIT = 4, 2048
LEAD = 2
CHUNK = 512
KG = 4

FF_PARTS = (24, FF_T - 24)

PIECES = ["s5_scale", "s5_shift", "s5_gate", "kv_shift", "kv_scale", "nsa_shift", "nsa_scale", "nsa_gate"]
MOD_RUNS = [(("mv", "mq", "ik", "iq", "rq", "rk", "rv", "aq", "ak"), (0, 1, 2)), (("fo0",), (5,)), (("fo1",), (6,)),
            (("kvn", "nq"), (7,))]
MIX_PIECE = 3

PHASES = [
    ("mk", 8, 4), ("mv", 8, 4), ("mq", 8, 4), ("ik", 1, 1), ("iq", 8, 4), ("rq", 8, 4), ("rk", 8, 4), ("rv", 16, 8),
    ("aq", 8, 4), ("ak", 8, 4), ("av", 8, 4), ("rg", 16, 8), ("mix", 80, 48), ("wo", 16, 8),
    ("ff0", 2 * FF_PARTS[0], FF_PARTS[0]), ("fo0", FF_PARTS[0], 8), ("ff1", 2 * FF_PARTS[1], FF_PARTS[1]),
    ("fo1", FF_PARTS[1], 8), ("su", 16, 8), ("sz", 16, 32), ("glu", 16, 8), ("so", 16, 8),
    ("kvt", 16, 8), ("cw", 4, 0), ("kvn", 8, 4), ("nq", 16, 8), ("nz", 48, 24), ("no", 16, 8),
]
MIX_LOOPS = 2


def with_mods(units, pieces):
    mods = [("mod", piece, k) for piece in pieces for k in range(KT)]
    out, done = [], 0
    for j, unit in enumerate(units):
        want = j * len(mods) // (len(units) - 1)
        out += [unit, *mods[done:want]]
        done = want
    return out


ORDER, B0, NB = [], {}, {}
BANKS = 0
_run = []
for _name, _units, _banks in PHASES:
    _list = [("unit", _name, _u) for _u in range(_units)]
    _with = [x for x in MOD_RUNS if _name in x[0]]
    if _name == "mix":
        for _i in range(MIX_LOOPS):
            ORDER += with_mods(_list[_units // MIX_LOOPS * _i:][:_units // MIX_LOOPS], [MIX_PIECE + _i])
    elif _with:
        _run += _list
        if _name == _with[0][0][-1]:
            ORDER += with_mods(_run, _with[0][1])
            _run = []
    else:
        ORDER += _list
    B0[_name], NB[_name] = BANKS, _banks
    BANKS += _banks
POS = {x: n for n, x in enumerate(ORDER)}
UNITS = len(ORDER)
STREAM_UNITS = -(-UNITS // RING) * RING
MIX_TURN = POS[("mod", MIX_PIECE + 1, 0)] - POS[("mod", MIX_PIECE, 0)]
MIX_BODY = ORDER[POS[("unit", "mix", 0)]:][:MIX_TURN]


def segment(phase):
    out = []
    for x in ORDER[POS[("unit", phase, 0)]:]:
        if x[0] == "unit" and x[1] != phase:
            break
        out += [x]
    return out


VECS = ["g_pre_mix", "g_mem", "g_pre_ffn", "norm0", "norm1", "kv_norm", "c", "b_glu", "d_skip"] + PIECES
V = {n: i for i, n in enumerate(VECS)}

SSM_CHUNKS, PAIRS = D // P, 4
SSM_BODY = 4
SSM_B, SSM_C = PAIRS * 2 * P, 2 * P
SSM_COLS = SSM_B + SSM_C


CONSTS_MADE = 6
LATE = 1533
SSM_AHEAD = 4
SSM_GELU0 = 1
TURN_F = 6.283185
MIX_GATES = (4, 10, 18, 24, 30, 38)
MIX_ENDS = (6, 14, 20, 26, 34, 40)
CMP_PAD = 32
RETV = 256
S5_PAIRS = (SSM_CHUNKS + 1) * PAIRS
EARLY, CST = 2560, 898 + len(VECS) * KT
ARENA = 48, 64
O_ADDS = NKV * TT + 2 * NQ


def heads_in_turn(name, n, first=0):
    out = []
    for h in range(n + 2):
        out += [(name + "_logits", first + h)] * (h < n)
        out += [(name + "_turn", first + h - 1)] * (1 <= h <= n)
        out += [(name + "_values", first + h - 2)] * (h >= 2)
    return out


def spread(phase, tasks=()):
    out, done = [], 0
    units = segment(phase)
    n = sum(x[0] == "unit" for x in units)
    for step in units:
        out += [step]
        if step[0] == "unit":
            want = -(-len(tasks) * (step[2] + 1) // n)
            out += tasks[done:want]
            done = want
        elif step[2] == KT - 1:
            out += [("mod_turn", step[1], c) for c in range(4)]
    return out


def with_ropes(steps):
    out, due = [], []
    for s in steps:
        out += [s]
        if s[0] == "unit":
            out += due
            due = [("rope", s[1], s[2] // 2)] if s[2] % 2 or s[1] == "ik" else []
    return out + due


def mixer_steps():
    att = heads_in_turn("att", N_ATT)
    ret = [x for h in range(N_RET + 1) for x in [("ret_scores", h)] * (h < N_RET) + [("ret_values", h - 1)] * (h > 0)]
    idx = [("idx_w", 0)] + [("idx", h) for h in range(N_IDX)]
    topk = [("topk", t, r) for t in range(TT) for r in range(TOPK // 16)] + [("topk_end",)]
    s = [("norm", "mem", j) for j in range(KT // 2)] + [("rms", "x")]
    s += spread("mk", [("norm", "x", j) for j in range(KT // 2)] + [("angles",)])
    s += spread("mv", [("s5_params",)]) + spread("mq")
    s += with_ropes(spread("ik") + spread("iq", heads_in_turn("mem", N_MEM)))
    s += with_ropes(spread("rq", idx[:9])) + with_ropes(spread("rk", idx[9:])) + spread("rv", topk)
    s += with_ropes(spread("aq", ret[:6])) + with_ropes(spread("ak", ret[6:12])) + spread("av", ret[12:])
    return s + spread("rg", att) + [("turn_y", j) for j in range(KT // 2)]


def nsa_steps():
    s = [("norm", "x3", j) for j in range(KT // 2)] + spread("kvt")
    s += [("cmp_hidden", 0), ("cmp_hidden", 1)] + spread("kvn", [("cmp_out", 0), ("cmp_out", 1)])
    s += spread("nq", [("ngate", 0)])
    units = spread("nz")
    s += units[:4]
    for c in range(3 * NKV):
        g, br = divmod(c, 3)
        if br == 0:
            tasks = [("cmp_logits", g), ("cmp_turn", g), ("cmp_values", g, 0), ("cmp_values", g, 1)]
        else:
            tasks = heads_in_turn(("cmp", "sel", "win")[br], HPG, HPG * g)
        ahead = units[4 * c + 4:4 * c + 8]
        for u in range(4):
            k = len(tasks) * u // 4, len(tasks) * (u + 1) // 4
            s += ahead[u:u + 1] + tasks[k[0]:k[1]]
    return s + [("turn_o", j) for j in range(KT // 2)]


MIXER, NSA = mixer_steps(), nsa_steps()
MIX_TURNS = [("mod_turn", MIX_PIECE, c) for c in range(4)]
AFTER_MIX = [("turn_mix", j) for j in range(KT // 2)]
OUT, S5_OUT = spread("wo"), spread("so")
BEFORE_FFN = [("norm", "x1", j) for j in range(KT // 2)]
FFN_OUT = [spread("fo0"), spread("fo1")]
BEFORE_S5 = [("norm", "x2", j) for j in range(KT // 2)] + spread("su")
BEFORE_S5_OUT = [("gate", "s5", j) for j in range(D // CHUNK)]
BEFORE_NSA_OUT = [("gate", "nsa", j) for j in range(D // CHUNK)]

LOCAL = ("unit", "mod", "rms", "angles", "s5_params", "topk", "topk_end")
SIDE = {}
_n = 0
for _steps in (MIXER, "mix", AFTER_MIX, OUT, BEFORE_FFN, *FFN_OUT, BEFORE_S5, "s5", BEFORE_S5_OUT, S5_OUT, NSA,
               BEFORE_NSA_OUT):
    if _steps == "s5":
        SSM_SIDE0 = _n
        _n += SSM_CHUNKS * PAIRS
        continue
    if _steps == "mix":
        SIDE.update({_s: _n + _k for _k, _s in enumerate(MIX_TURNS)})
        _n += MIX_LOOPS * len(MIX_TURNS)
        continue
    for _s in _steps:
        if _s[0] not in LOCAL:
            SIDE[_s] = _n
            _n += 1
GATES = {s: n for n, s in enumerate(BEFORE_S5_OUT + BEFORE_NSA_OUT)}
ROPE = {s: n for n, s in enumerate(x for x in MIXER if x[0] == "rope")}
_attn = [x for x in MIXER + NSA if x[0].endswith("_logits")]
TURNS = [(x[0][:3] + "_turn", x[1]) for x in _attn]
VALUES = [(x[0][:3] + "_values", x[1]) + ((1,) if x[0][:3] == "cmp" else ()) for x in _attn]
MASKED = {n: n - N_MEM for n in range(len(_attn))}
O_INDEX = {s: n for n, s in enumerate(x for x in NSA if x[0] in ("cmp_values", "sel_values", "win_values"))}
O_AFTER = [sum(1 for s in O_INDEX if (3 * s[1] if s[0] == "cmp_values" else 3 * (s[1] // HPG) + (1 if s[0][:3] == "sel" else 2)) <= c)
           for c in range(3 * NKV)]
HEADS = {s[:2]: n for n, s in enumerate(x for x in MIXER + NSA if x[0].endswith("_logits"))}
ROUNDED = {s: n for n, s in enumerate(
    x for x in MIXER + AFTER_MIX + BEFORE_FFN + BEFORE_S5 + NSA
    if x[0] in ("norm", "mem_values", "att_values", "turn_y", "turn_mix", "turn_o"))}
NORMS = {"mem": 0, "x": 1, "x1": 2, "x2": 3, "x3": 4, "out": 5}


HI = []
for _x in ORDER:
    HI.append((HI[-1] if HI else 0) + (_x[0] == "unit" and _x[1] != "cw"))
RUN = {}
for _g, _x in enumerate(ORDER):
    if _x[0] == "unit":
        _last = _x
    RUN[_last] = RUN.get(_last, 0) + 1


class Steps:

    def __init__(self, eng, sem):
        self.eng, self.sem, self.n, self.i, self.stride = eng, sem, 0, None, 0

    def __call__(self, ins):
        ins.then_inc(self.sem, 1)
        self.n += 1

    def wait(self):
        self.eng.wait_ge(self.sem, self.n if self.i is None else self.i * self.stride + self.n)

    def enter(self, i, stride):
        self.i, self.stride, self.n0 = i, stride, self.n

    def leave(self, count):
        assert self.n - self.n0 == self.stride, (self.n - self.n0, self.stride)
        self.n, self.i = self.n0 + self.stride * count, None


def program(nc, A, out, x_kept):
    with ExitStack() as ctx:
        def sb(name, shape):
            return ctx.enter_context(nc.sbuf_tensor(name, shape, F32))

        def sem(name):
            return ctx.enter_context(nc.semaphore(name))

        fast = {}

        def two_types(name, shape):
            with nc.sbuf_tensor(name, shape, F32) as whole:
                pass
            fast[name] = ctx.enter_context(nc.sbuf_tensor(name + "_parts", shape, F32R))
            return whole

        def r32(ap):
            return bass.AP(tensor=fast[ap.tensor.name][:].tensor, offset=ap.offset, ap=ap.ap)

        def as32(ap):
            return r32(ap).bitcast(F32)

        ring = two_types("ring", [P, RING, UNIT])
        hi = two_types("hi", [P, RING, UNIT])
        arena = [two_types("arena_low", [P, ARENA[0] * 256]), two_types("arena_high", [P, ARENA[1] * 256])]
        work = sb("work", [P, 7, CHUNK])
        early = sb("early", [P, EARLY])
        perms = early[:, 0:2 * P].rearrange("p (k m) -> p k m", k=2)
        w_iw = early[:, 256:512].rearrange("p (k n) -> p k n", k=KT)
        ropes = early[:, 512:1536].rearrange("p (k t) -> p k t", k=4)
        selbias = early[:, 1536:2048].rearrange("p (t s) -> p t s", t=TT)
        ikT = early[:, 2048:2560].rearrange("p (h s) -> p h s", h=2)
        w_ng = early[:, 0:768].rearrange("p (k n) -> p k n", k=KT)
        cmp_w2 = early[:, 768:1024].rearrange("p (j n) -> p j n", j=2)
        b1_rows = early[:, 1024:1280].rearrange("p (j n) -> p j n", j=2)
        b2_row = early[:, 1280:1408]
        cmp_pe = early[:, 1408:1472].rearrange("p (j l) -> p j l", j=2)
        cmp_add = early[:, 1472:1502].rearrange("p (t n) -> p t n", t=TT)
        cmp_keep = early[:, 1502:1532].rearrange("p (t n) -> p t n", t=TT)
        b2_col = early[:, 1532:1533]
        hid = early[:, 1536:1656].rearrange("p (j n) -> p j n", j=2)
        kcT = early[:, 1656:1716]
        gates = early[:, 1720:1816].rearrange("p (t n) -> p t n", t=TT)
        v_tmp = early[:, 2048:2560].rearrange("p (g n) -> p g n", g=NKV)
        cst = sb("cst", [P, CST])
        ident = cst[:, 0:128]
        causal = cst[:, 128:640].rearrange("p (t s) -> p t s", t=TT)
        time_row = cst[:, 640:896]
        vecs = cst[:, 896:896 + len(VECS) * KT].rearrange("p (v c) -> p v c", c=KT)
        freq = cst[:, CST - 2:CST]
        ones = sb("ones", [P, P])
        modv = sb("modv", [P, len(PIECES), KT])
        gains = sb("gains", [P, 3, KT])
        c_act = sb("c_act", [P, KT])
        iw = sb("iw", [P, TT, N_IDX])
        stat = sb("stat", [P, 64])
        bn = sb("bn", [P, TT, 6])
        s5 = sb("s5", [P, 5, S5_PAIRS])
        half_pi = sb("half_pi", [P, 1])
        round_up, round_back = sb("round_up", [P, 1]), sb("round_back", [P, 1])
        bn_all = sb("bn_all", [P, TT * N_RET, 2])
        psum = ctx.enter_context(nc.psum_tensor("psum", [P, 8, CHUNK], F32))

        def area(kb, n):
            piece, at = (0, kb) if kb < ARENA[0] else (1, kb - ARENA[0])
            return arena[piece][:, at * 256:at * 256 + n]

        def tokens(kb, n=D):
            return area(kb, TT * n).rearrange("p (t n) -> p t n", t=TT)

        def feats(kb, n=KT):
            return area(kb, n * S).rearrange("p (c t) -> p c t", c=n)

        def pair(kb_hi, kb_lo, n=KT):
            return feats(kb_hi, n), feats(kb_lo, n)

        hT, memT, mem_in, x_in = pair(0, 16), pair(32, 48), tokens(64), tokens(80)
        mkT, mv, mqT, o_cT = feats(64, 8), tokens(72, 1024), feats(80, 8), pair(96, 104, 8)
        iqT, score, top = feats(32, 8), tokens(40, S), tokens(42, S)
        rqT, rkT, rv = feats(48, 8), feats(56, 8), tokens(64)
        decay = area(80, N_RET * S).rearrange("p (h t) -> p h t", h=N_RET)
        aqT, akT, av, o_aT = feats(32, 8), feats(40, 8), tokens(88, 1024), pair(48, 56, 8)
        o_bT, mixed, mixT = pair(32, 80), tokens(64), pair(0, 16)
        xr, y, xn, h2T = tokens(32), tokens(96), tokens(80), pair(0, 16)
        actT = pair(48, 48 + FF_PARTS[0], FF_PARTS[0])
        h3T, uT, zT = pair(0, 16), feats(48), pair(0, 64)
        cos_t, sin_t = [area(32, 1024), area(36, 1024)], [area(40, 1024), area(44, 1024)]
        ssm_in = area(96, 2 * SSM_COLS).rearrange("p (b n) -> p b n", b=2)
        ssm_c = area(106, 2 * 3 * P).rearrange("p (b k q c) -> p b k q c", b=2, k=3, q=PAIRS)
        ssm_tmp = area(109, 2 * P)
        yT = pair(80, 96)
        hkvT, hnT, cin = pair(0, 16), pair(64, 48), area(64, 4 * NKV * S).rearrange(
            "p (j h g t) -> p j h g t", j=2, h=2, g=NKV)
        ksT, kwT, vs, vw = feats(96, NKV), feats(100, NKV), tokens(104, 512), tokens(108, 512)
        qT, o_tok, oT = feats(0), tokens(16), pair(64, 48)
        zs = area(80, 2 * TT * CHUNK).rearrange("p (b t n) -> p b t n", b=2, t=TT)
        v_blocks = area(88, NKV * CHUNK).rearrange("p (g n) -> p g n", g=NKV)
        final_row, y_out = area(0, D), tokens(16)

        def halves(i):
            return work[:, i, :].rearrange("p (t s) -> p t s", t=2)

        prob, probT = (0, 1), (2, 3)
        TMP = (4, 5, 6)

        def halves_of(ap):
            return ap.rearrange("p (t s) -> p t s", t=2)

        def both(x, j):
            return x[:, 2 * j:2 * j + 2, :].rearrange("p c t -> p (c t)")

        row, nsa_row, frac_t, abs_t = early[:, 0:D], area(80, D), early[:, 0:1024], early[:, 1024:2048]

        def sums_of(piece):
            if piece < MIX_PIECE:
                return area(88, D)
            return early[:, 0:D] if piece < MIX_PIECE + MIX_LOOPS else work[:, 0:4, :].rearrange("p b n -> p (b n)")


        pos_i = area(96, S).bitcast(I32)
        rope_pos, rope_ang, rope_k, rope_abs = area(97, S), [area(98, S), area(99, S)], area(100, S), area(101, S)
        s5_raw = area(102, 3 * 64).rearrange("p (k n) -> p k n", k=3)
        s5_dt, s5_thr, s5_sin, s5_sin2 = (area(103, 256)[:, 64 * k:64 * k + 64] for k in range(4))
        s5_tmp = [area(104, 320)[:, 64 * k:64 * k + 64] for k in range(5)]
        ret_stat = bn_all[:, :, :]
        ssm_bufs = [area(80 + 2 * k, 2 * S) for k in range(8)] + [work[:, k, :] for k in range(4)]
        ssm_buf = [ssm_bufs[3 * q:3 * q + 3] for q in range(PAIRS)]
        whole_t = cos_t

        def stream_bank(b):
            return psum[:, b % 4, :]

        def side_bank(n):
            return psum[:, 4 + n % 4, :]

        landed = [sem(f"ring_slot{s}_landed") for s in range(RING)]
        units_done = sem("units_done")
        hi_made = sem("hi_made")
        cut_done = sem("cut_done")
        rounded = sem("rounded")
        evacuated = [sem(f"stream_bank{b}_evacuated") for b in range(4)]
        side_done = sem("side_done")
        side_read = [sem(f"side_bank{b}_read") for b in range(4)]
        consts_landed, mem_landed, x_landed = sem("consts_landed"), sem("mem_landed"), sem("x_landed")
        decay_landed, rows_landed = sem("decay_landed"), sem("rows_landed")
        norm_squares, norm_mean, norm_root, norm_scaled = (sem("norm_" + n) for n in ("squares", "mean", "root", "scaled"))
        roped, idx_added = sem("roped"), sem("idx_added")
        head_max, head_exp, head_prob = sem("head_max"), sem("head_exp"), sem("head_prob")
        ret_var, ret_root, ret_gated = sem("ret_var"), sem("ret_root"), sem("ret_gated")
        mix_done = sem("mix_done")
        res_mean, res_root, res_added = sem("res_mean"), sem("res_root"), sem("res_added")
        act_ready, trig_done, s5_ready = sem("c_act_ready"), sem("trig_done"), sem("s5_ready")
        act_steps, dve_steps, pool_steps = sem("act_steps"), sem("dve_steps"), sem("pool_steps")
        ang_ready, rope_ready, const_made = sem("ang_ready"), sem("rope_ready"), sem("const_made")
        diag_ready, mod_gain = sem("diag_ready"), sem("mod_gain")
        ssm_landed = [sem(f"ssm_in{b}_landed") for b in range(2)]
        ssm_cmul, ssm_turns, ssm_whole, ssm_frac, ssm_trig = (
            sem("ssm_" + n) for n in ("cmul", "turns", "whole", "frac", "trig"))
        ssm_prod, ssm_rot, ssm_state, ssm_back, ssm_y, ssm_skip = (
            sem("ssm_" + n) for n in ("prod", "rot", "state", "back", "y", "skip"))
        cmp_key, cmp_vblock, v_zero, silu_z, o_added = sem("cmp_key"), sem("cmp_vblock"), sem("v_zero"), sem("silu_z"), sem("o_added")
        gates_made, out_ready, out_stored = sem("gates_made"), sem("out_ready"), sem("out_stored")
        late_landed, y_hi, y_cut, hn_hi, hn_cut = (sem(n) for n in ("late_landed", "y_hi", "y_cut", "hn_hi", "hn_cut"))
        x_stored = sem("x_stored")
        act_hi, act_cut = sem("ffn_hi"), sem("ffn_cut")
        s5_raw_landed, x_again_landed, final_row_landed = sem("s5_raw_landed"), sem("x_again_landed"), sem("final_row_landed")
        consts_made, ff_gate, res_squares = sem("consts_made"), sem("ff_gate"), sem("res_squares")
        glu_gate, iw_ready, sel_ready, cin_part = sem("glu_gate"), sem("iw_ready"), sem("sel_ready"), sem("cin_part")
        pos_landed, s5_params, mix_part, ssm_gelu = sem("pos_landed"), sem("s5_params"), sem("mix_part"), sem("ssm_gelu")
        p_cmp = work[:, TMP[0], 0:2 * P]
        def written(n):
            return side_done, n + 1

        def read(n):
            return side_read[n % 4], n // 4 + 1

        def multiplied(phase, u):
            return units_done, POS[("unit", phase, u)] + 1

        def visited(step):
            if step[0] == "cmp_hidden":
                return [("unit", "cw", 2 * step[1] + half) for half in range(2)]
            return [step] if step[0] in ("unit", "mod") else []

        def emptied(b):
            return evacuated[b % 4], b // 4 + 1

        def last_banks(phase):
            return [emptied(B0[phase] + NB[phase] - 1 - i) for i in range(min(4, NB[phase]))]

        def last_reads(uses):
            return [read(n) for n in uses[-4:]]

        def norm_uses(tag):
            return [SIDE[("norm", tag, j)] for j in range(KT // 2)]

        NORM_TO = {"mem": (memT, vecs[:, V["g_mem"], :], None), "x": (hT, vecs[:, V["g_pre_mix"], :], None),
                   "x1": (h2T, vecs[:, V["g_pre_ffn"], :], None),
                   "x2": (h3T, gains[:, 0, :], modv[:, PIECES.index("s5_shift"), :]),
                   "x3": (hkvT, gains[:, 1, :], modv[:, PIECES.index("kv_shift"), :])}
        S_MAG, S_TURN, S_KRE, S_KIM, S_NKIM = 0, 1, 2, 3, 4

        block = ctx.enter_context(nc.Block())

        @block.sync
        def _(sp):
            sp.wait_ge(mem_landed, 16)
            for s in range(RING):
                sp.dma_start(ring[:, s, :], A["stream"][s]).then_inc(landed[s], 16)
            with sp.Fori(1, STREAM_UNITS // RING) as turn:
                for s in range(RING):
                    sp.wait_ge(units_done, turn * RING + (s + 1 - RING))
                    sp.wait_ge(cut_done, turn * RING + (s + 1 - RING))
                    sp.dma_start(ring[:, s, :], A["stream"][bass.ds(turn * RING + s, 1)]
                                 .rearrange("a p n -> p (a n)")).then_inc(landed[s], 16)
            sp.wait_ge(out_ready, 2)
            for t in range(TT):
                sp.dma_start(out[t * P:(t + 1) * P, :], y_out[:, t, :]).then_inc(out_stored, 16)
            sp.wait_ge(out_stored, 16 * TT)

        @block.tensor
        def _(pe):
            def slot_of(phase, u, i=None, per=0):
                g = POS[("unit", phase, u)]
                pe.wait_ge(cut_done, g + 1 if i is None else i * per + (g + 1))
                return g % RING

            def release(mm, phase, u):
                mm.then_inc(units_done, RUN[("unit", phase, u)])

            def free_bank(b, i=None, uses=0):
                if b >= 4:
                    pe.wait_ge(evacuated[b % 4], b // 4 if i is None else i * uses + b // 4)
                return stream_bank(b)

            def free_side(n):
                if n >= 4:
                    pe.wait_ge(*read(n - 4))
                return side_bank(n)

            def t_unit(phase, u, x, i=None, per=0, uses=0, own_bank=None):
                slot = slot_of(phase, u, i, per)
                b, half = (B0[phase] + u // 2, (u % 2) * S) if own_bank is None else (own_bank, 0)
                bank = free_bank(b, i, uses) if half == 0 else stream_bank(b)
                for k in range(KT):
                    cols = slice(k * P, (k + 1) * P)
                    for n, (w, part) in enumerate(((hi, 0), (hi, 1), (ring, 0))):
                        mm = pe.matmul(bank[:, half:half + S], r32(w[:, slot, cols]), r32(x[part][:, k, :]),
                                       start=(k == 0 and n == 0), stop=(k == KT - 1 and n == 2))
                release(mm, phase, u)

            def n_unit(phase, u, x, kg, groups, b, i=None, per=0, uses=0):
                slot = slot_of(phase, u, i, per)
                if kg == 0:
                    free_bank(b, i, uses)
                    free_bank(b + 1, i, uses)
                for kk in range(KG):
                    cols = slice(kk * CHUNK, (kk + 1) * CHUNK)
                    for t in range(TT):
                        for n, (part, w) in enumerate(((0, hi), (0, ring), (1, hi))):
                            mm = pe.matmul(stream_bank(b + t), r32(x[part][:, kg * KG + kk, t * P:(t + 1) * P]),
                                           r32(w[:, slot, cols]), start=(kg == 0 and kk == 0 and n == 0),
                                           stop=(kg == groups - 1 and kk == KG - 1 and n == 2))
                release(mm, phase, u)

            def turn_tokens(src, j, n):
                bank = free_side(n)
                for c in range(2):
                    for t in range(TT):
                        mm = pe.transpose(bank[:, c * S + t * P:c * S + (t + 1) * P],
                                          src[:, t, (2 * j + c) * P:(2 * j + c + 1) * P], ident[:, :])
                mm.then_inc(side_done, 1)

            T_RHS = {"mk": memT, "mq": hT, "ik": hT, "iq": hT, "aq": hT, "ak": hT, "rq": hT, "rk": hT,
                     "su": h3T, "sz": h3T, "glu": yT, "kvt": hkvT, "nq": hnT}
            N_LHS = {"mv": memT, "av": hT, "rv": hT, "rg": hT, "wo": mixT, "fo0": actT, "fo1": actT, "so": zT,
                     "kvn": hkvT, "nz": hnT, "no": oT}

            def mod_turn(piece, c, n, i=None):
                if i is None:
                    bank = free_side(n)
                else:
                    pe.wait_ge(side_read[n % 4], i + n // 4)
                    bank = side_bank(n)
                last = POS[("mod", piece, KT - 1)] + 1
                pe.wait_ge(cut_done, last if i is None else i * MIX_TURN + last)
                for k in range(4):
                    at = c * CHUNK + k * P
                    mm = pe.matmul(bank[:, k:k + 1], sums_of(piece)[:, at:at + P], ones[:, 0:1], start=True, stop=True)
                mm.then_inc(side_done, 1)

            def plain_unit(phase, u):
                if phase in T_RHS:
                    t_unit(phase, u, T_RHS[phase])
                else:
                    groups = {"fo0": FF_PARTS[0] // KG, "fo1": FF_PARTS[1] // KG}.get(phase, 4)
                    n_unit(phase, u, N_LHS[phase], u % groups, groups, B0[phase] + u // groups * 2)

            def logits(n, q, k, h, hk):
                bank = free_side(n)
                for t in range(TT):
                    mm = pe.matmul(bank[:, t * S:(t + 1) * S], q[:, h, t * P:(t + 1) * P], k[:, hk, :],
                                   start=True, stop=True)
                mm.then_inc(side_done, 1)

            def turn_probs(n, a):
                bank = free_side(n)
                pe.wait_ge(head_prob, a + 1)
                for blk in range(2):
                    for t in range(TT):
                        mm = pe.transpose(bank[:, blk * S + t * P:blk * S + (t + 1) * P],
                                          halves(prob[a % 2])[:, t, blk * P:(blk + 1) * P], ident[:, :])
                mm.then_inc(side_done, 1)

            def side(step):
                kind, n = step[0], SIDE[step]
                if kind == "norm":
                    tag, j = step[1:]
                    if j == 0:
                        pe.wait_ge(norm_scaled, TT * (NORMS[tag] + 1))
                    turn_tokens({"mem": mem_in, "x": x_in}.get(tag, xn), j, n)
                elif kind == "mod_turn":
                    mod_turn(step[1], step[2], n)
                elif kind == "rope":
                    r = ROPE[step]
                    bank = free_side(n)
                    pe.wait_ge(*emptied(B0[step[1]] + step[2]))
                    width = S if step[1] == "ik" else 2 * S
                    pe.matmul(bank[:, 0:width], perms[:, 1 if step[1] in ("ik", "iq") else 0, :],
                              work[:, TMP[r % 2], 0:width], start=True, stop=True).then_inc(side_done, 1)
                elif kind in ("idx_w", "ngate"):
                    src, w, m = (hT, w_iw, N_IDX) if kind == "idx_w" else (hnT, w_ng, 3 * NQ)
                    bank = free_side(n)
                    for t in range(TT):
                        for k in range(KT):
                            for part in range(2):
                                mm = pe.matmul(bank[:, t * m:(t + 1) * m], as32(src[part][:, k, t * P:(t + 1) * P]), w[:, k, :],
                                               start=(k == 0 and part == 0), stop=(k == KT - 1 and part == 1))
                    mm.then_inc(side_done, 1)
                elif kind == "idx":
                    h = step[1]
                    if h == 0:
                        pe.wait_ge(roped, ROPE[("rope", "iq", 3)] + 1)
                    logits(n, iqT, ikT, h // 2, h % 2)
                elif kind == "mem_logits":
                    h = step[1]
                    bank = free_side(n)
                    if h == 0:
                        for w in last_banks("mk") + last_banks("mq"):
                            pe.wait_ge(*w)
                    for t in range(TT):
                        for kk in range(2):
                            mm = pe.matmul(bank[:, t * S:(t + 1) * S], mqT[:, 2 * h + kk, t * P:(t + 1) * P],
                                           mkT[:, 2 * h + kk, :], start=(kk == 0), stop=(kk == 1))
                    mm.then_inc(side_done, 1)
                elif kind == "att_logits":
                    if step[1] == 0:
                        pe.wait_ge(roped, ROPE[("rope", "ak", 3)] + 1)
                    logits(n, aqT, akT, step[1], step[1])
                elif kind in ("sel_logits", "win_logits"):
                    logits(n, qT, ksT if kind == "sel_logits" else kwT, step[1], step[1] // HPG)
                elif kind.endswith("_turn") and kind != "cmp_turn":
                    turn_probs(n, HEADS[(kind[:3] + "_logits", step[1])])
                elif kind == "mem_values":
                    h = step[1]
                    a = HEADS[("mem_logits", h)]
                    bank = free_side(n)
                    pe.wait_ge(*read(SIDE[("mem_turn", h)]))
                    if h == 0:
                        for w in last_banks("mv"):
                            pe.wait_ge(*w)
                    for e in range(2):
                        for blk in range(2):
                            at = (2 * h + e) * P
                            mm = pe.matmul(bank[:, e * S:(e + 1) * S], mv[:, blk, at:at + P],
                                           halves(probT[a % 2])[:, blk, :], start=(blk == 0), stop=(blk == 1))
                    mm.then_inc(side_done, 1)
                elif kind == "att_values":
                    h = step[1]
                    a = HEADS[("att_logits", h)]
                    bank = free_side(n)
                    pe.wait_ge(*read(SIDE[("att_turn", h)]))
                    if h == 0:
                        for w in last_banks("av"):
                            pe.wait_ge(*w)
                    for blk in range(2):
                        mm = pe.matmul(bank[:, 0:S], av[:, blk, h * P:(h + 1) * P], halves(probT[a % 2])[:, blk, :],
                                       start=(blk == 0), stop=(blk == 1))
                    mm.then_inc(side_done, 1)
                elif kind in ("sel_values", "win_values"):
                    h = step[1]
                    a = HEADS[(kind[:3] + "_logits", h)]
                    v, g = (vs if kind == "sel_values" else vw), h // HPG
                    bank = free_side(n)
                    pe.wait_ge(*read(SIDE[(kind[:3] + "_turn", h)]))
                    for t in range(TT):
                        for blk in range(2):
                            mm = pe.matmul(bank[:, t * P:(t + 1) * P], halves(probT[a % 2])[:, blk, t * P:(t + 1) * P],
                                           v[:, blk, g * P:(g + 1) * P], start=(blk == 0), stop=(blk == 1))
                    mm.then_inc(side_done, 1)
                elif kind == "ret_scores":
                    h = step[1]
                    bank = free_side(n)
                    if h == 0:
                        pe.wait_ge(roped, ROPE[("rope", "rk", 3)] + 1)
                    pe.matmul(bank[:, 0:S], rkT[:, h, 0:P], rqT[:, h, :], start=True, stop=True)
                    pe.matmul(bank[:, S:S + P], rkT[:, h, P:S], rqT[:, h, P:S], start=True,
                              stop=True).then_inc(side_done, 1)
                elif kind == "ret_values":
                    h = step[1]
                    bank = free_side(n)
                    pe.wait_ge(*read(SIDE[("ret_scores", h)]))
                    if h == 0:
                        for w in last_banks("rv"):
                            pe.wait_ge(*w)
                    sd, at = work[:, prob[h % 2], :], h * RETV
                    pe.matmul(bank[:, 0:RETV], sd[:, 0:P], rv[:, 0, at:at + RETV], start=True, stop=True)
                    pe.matmul(bank[:, RETV:2 * RETV], sd[:, P:S], rv[:, 0, at:at + RETV], start=True, stop=False)
                    pe.matmul(bank[:, RETV:2 * RETV], sd[:, S:S + P], rv[:, 1, at:at + RETV], start=False,
                              stop=True).then_inc(side_done, 1)
                elif kind in ("turn_y", "turn_mix", "turn_o"):
                    src, done, value = {"turn_y": (rv, ret_gated, 8), "turn_mix": (mixed, mix_done, 1),
                                        "turn_o": (o_tok, o_added, O_ADDS)}[kind]
                    if step[1] == 0:
                        pe.wait_ge(done, value)
                    turn_tokens(src, step[1], n)
                elif kind == "gate":
                    tag, j = step[1:]
                    bank = free_side(n)
                    pe.wait_ge(diag_ready, GATES[step] + 1)
                    for c in range(4):
                        mm = pe.matmul(bank[:, c * P:(c + 1) * P], ones[:, :], work[:, TMP[j % 2], c * P:(c + 1) * P],
                                       start=True, stop=True)
                    mm.then_inc(side_done, 1)
                elif kind == "cmp_hidden":
                    j = step[1]
                    bank = free_side(n)
                    for b in range(2):
                        pe.wait_ge(*emptied(B0["kvt"] + 2 * j + b))
                    for half in range(2):
                        g = POS[("unit", "cw", 2 * j + half)]
                        pe.wait_ge(landed[g % RING], 16 * (g // RING + 1))
                        slot = g % RING
                        for r in range(CMP_STRIDE):
                            blocks = cin[:, j, half, :, :].rearrange("p g (n r) -> p g n r", r=CMP_STRIDE)
                            mm = pe.matmul(bank[:, 0:NKV * N_CMP], ring[:, slot, r * P:(r + 1) * P],
                                           blocks[:, :, half:half + N_CMP, r], start=(half == 0 and r == 0), stop=False)
                        release(mm, "cw", 2 * j + half)
                    pe.matmul(bank[:, 0:NKV * N_CMP], b1_rows[0:1, j, :], ones[0:1, 0:NKV * N_CMP], start=False,
                              stop=True).then_inc(side_done, 1)
                elif kind == "cmp_out":
                    j = step[1]
                    bank = free_side(n)
                    pe.wait_ge(*read(SIDE[("cmp_hidden", j)]))
                    if j == 0:
                        mm = pe.matmul(bank[:, 0:NKV * N_CMP], cmp_w2[:, 0, :], hid[:, 0, :], start=True, stop=True)
                    else:
                        for g in range(NKV):
                            mm = pe.matmul(bank[0:N_CMP, g * P:(g + 1) * P], hid[:, 1, g * N_CMP:(g + 1) * N_CMP],
                                           cmp_w2[:, 1, :], start=True, stop=True)
                    mm.then_inc(side_done, 1)
                elif kind == "cmp_logits":
                    g = step[1]
                    bank = free_side(n)
                    if g == 0:
                        pe.wait_ge(*read(SIDE[("cmp_out", 0)]))
                    for t in range(TT):
                        for h in range(HPG):
                            at = (t * HPG + h) * CMP_PAD
                            mm = pe.matmul(bank[:, at:at + N_CMP], qT[:, HPG * g + h, t * P:(t + 1) * P],
                                           kcT[:, g * N_CMP:(g + 1) * N_CMP], start=True, stop=True)
                    mm.then_inc(side_done, 1)
                elif kind == "cmp_turn":
                    a = HEADS[("cmp_logits", step[1])]
                    bank = free_side(n)
                    pe.wait_ge(head_prob, a + 1)
                    for t in range(TT):
                        mm = pe.transpose(bank[:, t * P:(t + 1) * P], p_cmp[:, t * P:(t + 1) * P], ident[:, :])
                    mm.then_inc(side_done, 1)
                elif kind == "cmp_values":
                    g, t = step[1:]
                    a = HEADS[("cmp_logits", g)]
                    bank = free_side(n)
                    pe.wait_ge(*read(SIDE[("cmp_turn", g)]))
                    if g == 0:
                        pe.wait_ge(cmp_vblock, 1)
                    pe.matmul(bank, work[:, probT[a % 2], t * P:(t + 1) * P], v_blocks[:, g, :], start=True,
                              stop=True).then_inc(side_done, 1)
                else:
                    raise ValueError(kind)

            first = {"mk": last_reads(norm_uses("mem")), "mq": last_reads(norm_uses("x")),
                     "wo": last_reads([SIDE[("turn_mix", j)] for j in range(8)]), "ff0": last_reads(norm_uses("x1")),
                     "fo0": [(act_cut, FF_PARTS[0])], "fo1": [(act_cut, FF_T)], "su": last_reads(norm_uses("x2")),
                     "glu": [(y_cut, 4)], "so": last_banks("glu"), "kvt": last_reads(norm_uses("x3")),
                     "nq": [(hn_cut, 4)], "no": last_reads([SIDE[("turn_o", j)] for j in range(8)])}

            def steps(todo):
                for step in todo:
                    if step[0] == "unit":
                        for w in first.get(step[1], []) if step[2] == 0 else []:
                            pe.wait_ge(*w)
                        plain_unit(step[1], step[2])
                    elif step[0] not in LOCAL:
                        side(step)

            pe.wait_ge(consts_made, CONSTS_MADE)
            pe.wait_ge(consts_landed, 32)
            steps(MIXER)
            for w in last_reads([SIDE[("turn_y", j)] for j in range(8)]) + last_reads([SIDE[("att_values", N_ATT - 1)]]) \
                    + last_reads([SIDE[("mem_values", N_MEM - 1)]]):
                pe.wait_ge(*w)
            with pe.Fori(0, MIX_LOOPS) as i:
                for c in range(2):
                    u, b = c * 20, B0["mix"] + c * 12
                    for src, groups in ((o_aT, 2), (o_bT, 4), (o_cT, 2)):
                        for x, kgs in ((hT, 4), (src, groups)):
                            for kg in range(kgs):
                                n_unit("mix", u, x, kg, kgs, b, i, MIX_TURN, 6)
                                u += 1
                            b += 2
                for _, piece, c in MIX_TURNS:
                    mod_turn(piece, c, SIDE[("mod_turn", piece, c)], i)
            steps(AFTER_MIX + OUT + BEFORE_FFN)
            for part, tiles in enumerate(FF_PARTS):
                ff = f"ff{part}"
                for w in first[ff] if part == 0 else []:
                    pe.wait_ge(*w)
                with pe.Fori(0, tiles // 4) as i:
                    for u in range(8):
                        t_unit(ff, u, h2T, i, 8, 1)
                steps(FFN_OUT[part])
            steps(BEFORE_S5)
            for w in last_banks("su"):
                pe.wait_ge(*w)
            def inputs(cc, q, i):
                n, buf = SSM_SIDE0 + cc * PAIRS + q, cc % 2
                pe.wait_ge(ssm_prod, i * n_pairs + (cc * PAIRS + q + 1))
                if q == 0:
                    pe.wait_ge(ssm_landed[buf], i * 32 + 16 * (cc // 2 + 1))
                for part in range(2):
                    at = (2 * q + part) * P
                    mm = pe.matmul(side_bank(n)[:, part * S:(part + 1) * S], ssm_in[:, buf, at:at + P],
                                   uT[:, bass.ds(i * SSM_BODY + cc, 1), :].rearrange("p a t -> p (a t)"),
                                   start=True, stop=True)
                mm.then_inc(side_done, 1)

            def outputs(cc, q, bank, i):
                pe.wait_ge(ssm_back, i * n_pairs + (cc * PAIRS + q + 1))
                back = ssm_buf[q][1:]
                for m, (k, turned, part) in enumerate(((0, 0, 0), (1, 1, 1), (2, 1, 0), (2, 0, 1))):
                    mm = pe.matmul(bank[32 * q:32 * q + 32, 0:S], ssm_c[:, cc % 2, k, q, :],
                                   back[turned][:, part * S:(part + 1) * S], start=(m == 0), stop=(m == 3))
                mm.then_inc(ssm_y, 1)

            n_pairs = SSM_BODY * PAIRS
            for n in range(SSM_SIDE0 - 4, SSM_SIDE0):
                pe.wait_ge(*read(n))
            pe.nop().then_inc(ssm_y, SSM_AHEAD)
            with pe.Fori(0, SSM_CHUNKS // SSM_BODY) as i:
                for q in range(PAIRS):
                    inputs(0, q, i)
                for cc in range(SSM_BODY):
                    b = B0["sz"] + 2 * cc
                    bank = free_bank(b + 1, i, 2)
                    pe.wait_ge(ssm_cmul, i * SSM_BODY + cc + 1)
                    for q in range(PAIRS):
                        outputs(cc, q, bank, i)
                        if cc + 1 < SSM_BODY:
                            inputs(cc + 1, q, i)
                        if q == 0:
                            t_unit("sz", cc, h3T, i, SSM_BODY, 2, b)
            steps([("unit", "glu", u) for u in range(16)] + BEFORE_S5_OUT + S5_OUT)
            pe.wait_ge(late_landed, 16)
            steps(NSA)
            steps(BEFORE_NSA_OUT + [("unit", "no", u) for u in range(16)])

        @block.scalar
        def _(act):
            did = Steps(act, act_steps)

            act.dma_start(mem_in, A["mem"].rearrange("(t p) n -> p t n", p=P)).then_inc(mem_landed, 16)
            act.dma_start(cst[:, :], A["cst"]).then_inc(consts_landed, 16)
            act.dma_start(early[:, 0:512], A["early"]).then_inc(consts_landed, 16)
            act.dma_start(x_in, A["x"].rearrange("(t p) n -> p t n", p=P)).then_inc(x_landed, 16)
            act.dma_start(pos_i, A["positions"].broadcast_to([P, S])).then_inc(pos_landed, 16)
            act.dma_start(s5_raw, A["s5_raw"]).then_inc(s5_raw_landed, 16)

            def root(n_norm):
                act.wait_ge(norm_mean, n_norm + 1)
                act.activation(stat[:, 2:4], stat[:, 2:4], ACT.Sqrt).then_inc(norm_root, 1)

            def squares(src, n_norm, junk):
                for t in range(TT):
                    if t:
                        did.wait()
                    did(act.activation(junk, src[:, t, :], ACT.Square, accum_out=stat[:, t:t + 1]))
                did.wait()
                act.nop().then_inc(norm_squares, 1)
                root(n_norm)

            def local(step):
                if step[0] == "rms":
                    act.wait_ge(x_landed, 16)
                    act.wait_ge(norm_scaled, TT)
                    squares(x_in, 1, tokens(0)[:, 1, :])
                elif step[0] == "angles":
                    for which in range(2):
                        act.wait_ge(ang_ready, which + 1)
                        did(act.activation(ropes[:, 2 * which + 1, :], rope_ang[which], ACT.Sin))
                        did(act.activation(rope_abs, rope_ang[which], ACT.Abs))
                        did.wait()
                        act.activation(ropes[:, 2 * which, :], rope_abs, ACT.Sin, scale=-1.0,
                                       bias=half_pi[:, 0:1]).then_inc(rope_ready, 1)
                        act.wait_ge(rope_ready, which + 1)
                elif step[0] == "s5_params":
                    act.wait_ge(s5_raw_landed, 16)
                    act.activation(s5_dt, s5_raw[:, 2, :], ACT.Exp).then_inc(s5_ready, 1)
                    act.wait_ge(s5_ready, 2)
                    did(act.activation(s5_sin, s5_thr, ACT.Sin))
                    act.activation(s5_sin2, s5_thr, ACT.Sin, scale=0.5).then_inc(trig_done, 1)

            def exps(a, src, dst, scale):
                at = 16 + 8 * (a % 2)
                did(act.activation(dst[:, 0, :], src[:, 0, :], ACT.Exp, bias=stat[:, at + 2:at + 3], scale=scale,
                                   accum_out=stat[:, at + 4:at + 5]))
                return act.activation(dst[:, 1, :], src[:, 1, :], ACT.Exp, bias=stat[:, at + 3:at + 4], scale=scale,
                                      accum_out=stat[:, at + 5:at + 6])

            def copy_bank(phase, b, dst, func=ACT.Copy):
                act.activation(dst, stream_bank(B0[phase] + b), func).then_inc(evacuated[(B0[phase] + b) % 4], 1)

            T_DST = {"mk": mkT, "mq": mqT, "su": uT, "sz": zT[1], "nq": qT}
            N_DST = {"mv": mv, "av": av, "rv": rv}

            def cut(g, i=None, per=0):
                if g >= UNITS or ORDER[g][0] == "mod" or ORDER[g][1] == "cw":
                    return
                act.wait_ge(landed[g % RING], 16 * (g // RING + 1) if i is None else i * (per // RING * 16) + 16 * (g // RING + 1))
                if g >= RING:
                    act.wait_ge(units_done, g + 1 - RING if i is None else i * per + (g + 1 - RING))
                act.activation(r32(hi[:, g % RING, :]), ring[:, g % RING, :], ACT.Copy).then_inc(hi_made, 1)

            def square(c, t):
                did.wait()
                at = 32 + 4 * t + c
                return act.activation(work[:, TMP[0], :], y[:, t, c * CHUNK:(c + 1) * CHUNK], ACT.Square,
                                      accum_out=stat[:, at:at + 1])

            def out_unit(phase, u):
                if u % 4 == 3:
                    c = u // 4
                    act.wait_ge(*multiplied(phase, u))
                    for t in range(TT):
                        b = B0[phase] + 2 * c + t
                        did(act.activation(y[:, t, c * CHUNK:(c + 1) * CHUNK], stream_bank(b), ACT.Copy))
                        did(square(c, t))
                        did.wait()
                        act.nop().then_inc(evacuated[b % 4], 1)

            def unit(phase, u):
                if phase in T_DST and u % 2:
                    act.wait_ge(*multiplied(phase, u))
                    copy_bank(phase, u // 2, both(T_DST[phase], u // 2), ACT.Silu if phase == "sz" else ACT.Copy)
                elif ("rope", phase, u // 2) in ROPE and (u % 2 or phase == "ik"):
                    r = ROPE[("rope", phase, u // 2)]
                    act.wait_ge(*multiplied(phase, u))
                    if r >= 2:
                        act.wait_ge(roped, r - 1)
                    width = S if phase == "ik" else 2 * S
                    b = B0[phase] + u // 2
                    act.activation(work[:, TMP[r % 2], 0:width], stream_bank(b)[:, 0:width],
                                   ACT.Copy).then_inc(evacuated[b % 4], 1)
                elif phase in N_DST and u % 4 == 3:
                    act.wait_ge(*multiplied(phase, u))
                    c = u // 4
                    for t in range(TT):
                        copy_bank(phase, 2 * c + t, N_DST[phase][:, t, c * CHUNK:(c + 1) * CHUNK])
                elif phase == "rg" and u % 4 == 3:
                    act.wait_ge(*multiplied(phase, u))
                    c = u // 4
                    if c:
                        act.wait_ge(ret_gated, TT * c)
                    for t in range(TT):
                        copy_bank(phase, 2 * c + t, work[:, TMP[t], :], ACT.Silu)
                elif phase == "wo":
                    out_unit(phase, u)
                elif phase == "fo0" and (u + 1) % (FF_PARTS[0] // KG) == 0:
                    act.wait_ge(*multiplied(phase, u))
                    c = u // (FF_PARTS[0] // KG)
                    for t in range(TT):
                        copy_bank(phase, 2 * c + t, y[:, t, c * CHUNK:(c + 1) * CHUNK])
                elif phase == "fo1" and (u + 1) % (FF_PARTS[1] // KG) == 0:
                    c = u // (FF_PARTS[1] // KG)
                    for t in range(TT):
                        act.wait_ge(*emptied(B0[phase] + 2 * c + t))
                        did(square(c, t))
                elif phase == "glu" and u % 2:
                    act.wait_ge(*multiplied(phase, u))
                    b = u // 2
                    for c in range(2):
                        ins = act.activation(work[:, b % 4, c * S:(c + 1) * S], stream_bank(B0["glu"] + b)[:, c * S:(c + 1) * S],
                                             ACT.Sigmoid, bias=vecs[:, V["b_glu"], 2 * b + c:2 * b + c + 1])
                    ins.then_inc(glu_gate, 1)
                elif phase == "kvt" and u % 2 and u >= 8:
                    act.wait_ge(*multiplied(phase, u))
                    copy_bank(phase, u // 2, both(ksT if u < 12 else kwT, (u // 2) % 2))
                elif phase == "kvn" and u % 4 == 3:
                    act.wait_ge(*multiplied(phase, u))
                    for t in range(TT):
                        copy_bank(phase, u // 4 * 2 + t, (vs if u < 4 else vw)[:, t, :])
                elif phase == "nz" and u % 4 == 3:
                    c = u // 4
                    act.wait_ge(*multiplied(phase, u))
                    if c >= 2:
                        act.wait_ge(o_added, O_AFTER[c - 2])
                    for t in range(TT):
                        copy_bank(phase, 2 * c + t, zs[:, c % 2, t, :], ACT.Silu)

            def side(step):
                kind, n = step[0], SIDE[step]
                done = side_read[n % 4]
                if kind == "norm":
                    tag, j = step[1:]
                    if tag in ("x2", "x3") and j == 0:
                        act.wait_ge(mod_gain, 1 if tag == "x2" else 2)
                    act.wait_ge(*written(n))
                    dst, gain, shift = NORM_TO[tag]
                    for c in range(2):
                        k = 2 * j + c
                        part = side_bank(n)[:, c * S:(c + 1) * S]
                        ins = act.activation(r32(dst[0][:, k, :]), part, ACT.Identity, scale=gain[:, k:k + 1],
                                             bias=0.0 if shift is None else shift[:, k:k + 1])
                        if tag == "x3":
                            gain2, shift2 = gains[:, 2, k:k + 1], modv[:, PIECES.index("nsa_shift"), k:k + 1]
                            ins = act.activation(hnT[1][:, k, :], part, ACT.Identity, scale=gain2, bias=shift2)
                    ins.then_inc(rounded, 1)
                elif kind == "idx":
                    h = step[1]
                    act.wait_ge(*written(n))
                    if h >= 2:
                        act.wait_ge(idx_added, h - 1)
                    act.activation(work[:, prob[h % 2], :], side_bank(n), ACT.Relu).then_inc(done, 1)
                elif kind == "mem_logits":
                    a = HEADS[step]
                    act.wait_ge(head_max, a + 1)
                    if a >= 2:
                        act.wait_ge(*written(SIDE[TURNS[a - 2]]))
                    exps(a, halves_of(side_bank(n)), halves(prob[a % 2]), 0.0625).then_inc(done, 1)
                elif kind in ("att_logits", "sel_logits", "win_logits"):
                    a = HEADS[step]
                    act.wait_ge(head_max, a + 1)
                    exps(a, halves(prob[a % 2]), halves(prob[a % 2]), HD ** -0.5).then_inc(head_exp, 1)
                elif kind == "cmp_logits":
                    a = HEADS[step]
                    act.wait_ge(head_max, a + 1)
                    p4 = p_cmp.rearrange("p (a n) -> p a n", n=CMP_PAD)[:, :, 0:N_CMP]
                    act.activation(p4, p4, ACT.Exp, scale=HD ** -0.5).then_inc(head_exp, 1)
                elif kind.endswith("_turn") and kind != "mod_turn":
                    a = HEADS[(kind[:3] + "_logits", step[1])]
                    act.wait_ge(*written(n))
                    if a >= 2:
                        act.wait_ge(*written(SIDE[VALUES[a - 2]]))
                    width = 2 * P if kind == "cmp_turn" else 2 * S
                    act.activation(work[:, probT[a % 2], 0:width], side_bank(n)[:, 0:width], ACT.Copy).then_inc(done, 1)
                elif kind in ("mem_values", "att_values", "turn_y", "turn_mix", "turn_o"):
                    j = step[1]
                    act.wait_ge(*written(n))
                    dst = {"mem_values": o_cT, "att_values": o_aT, "turn_y": o_bT, "turn_mix": mixT, "turn_o": oT}[kind][0]
                    if kind == "att_values":
                        act.activation(r32(dst[:, j, :]), side_bank(n)[:, 0:S], ACT.Copy).then_inc(rounded, 1)
                    else:
                        act.activation(r32(both(dst, j)), side_bank(n), ACT.Copy).then_inc(rounded, 1)
                    if kind == "mem_values" and j == N_MEM - 1:
                        act.dma_start(decay, A["decay"].rearrange("p (h t) -> p h t", h=N_RET)).then_inc(decay_landed, 16)
                elif kind == "ret_values" and step[1] == N_RET - 1:
                    act.wait_ge(ret_var, 1)
                    act.activation(stat[:, 48:64], stat[:, 48:64], ACT.Sqrt).then_inc(ret_root, 1)
                elif kind == "gate":
                    act.wait_ge(*written(n))
                    to = row if step[1] == "s5" else nsa_row
                    act.activation(to[:, step[2] * CHUNK:(step[2] + 1) * CHUNK], side_bank(n), ACT.Copy).then_inc(done, 1)
                elif kind == "cmp_hidden":
                    act.wait_ge(*written(n))
                    act.activation(hid[:, step[1], :], side_bank(n)[:, 0:NKV * N_CMP], ACT.Gelu_apprx_tanh).then_inc(done, 1)
                elif kind == "cmp_out" and step[1] == 1:
                    for q in range(4):
                        act.activation(r32(hnT[0][:, 4 * q:4 * q + 4, :]), hnT[1][:, 4 * q:4 * q + 4, :],
                                       ACT.Copy).then_inc(hn_hi, 1)
                elif kind == "cmp_out" and step[1] == 0:
                    act.wait_ge(*written(n))
                    act.activation(kcT, side_bank(n)[:, 0:NKV * N_CMP], ACT.Identity, bias=b2_col).then_inc(done, 1)
                elif kind == "ngate":
                    act.wait_ge(*written(n))
                    act.activation(gates.rearrange("p t n -> p (t n)"), side_bank(n)[:, 0:TT * 3 * NQ],
                                   ACT.Sigmoid).then_inc(done, 1)

            def steps(todo):
                for step in todo:
                    for x in visited(step):
                        cut(POS[x] + LEAD)
                    if step[0] == "unit":
                        unit(step[1], step[2])
                    elif step[0] in LOCAL:
                        if step[0] != "mod":
                            local(step)
                    else:
                        side(step)

            def branch_root(n):
                act.wait_ge(res_mean, n + 1)
                act.activation(stat[:, 40:42], stat[:, 40:42], ACT.Sqrt).then_inc(res_root, 1)

            act.wait_ge(mem_landed, 16)
            squares(mem_in, 0, tokens(0)[:, 0, :])
            act.wait_ge(consts_landed, 32)
            act.activation(c_act[:, :], vecs[:, V["c"], :], ACT.Silu).then_inc(act_ready, 1)
            cut(0)
            cut(1)
            steps(MIXER)
            with act.Fori(0, MIX_LOOPS) as i:
                for step in MIX_BODY:
                    cut(POS[step] + LEAD, i, MIX_TURN)
                    if step[0] != "unit" or step[2] + 1 not in MIX_GATES:
                        continue
                    m = MIX_GATES.index(step[2] + 1)
                    b = B0["mix"] + 4 * m
                    act.wait_ge(units_done, i * MIX_TURN + (POS[step] + 1))
                    for t in range(TT):
                        old = b + t + 2 - 8
                        act.wait_ge(evacuated[old % 4], i * 6 + (old // 4 + 1))
                        act.activation(work[:, (m % 2) * 2 + t, :], stream_bank(b + t),
                                       ACT.Sigmoid).then_inc(evacuated[(b + t) % 4], 1)
            steps(AFTER_MIX)
            act.dma_start(xr, A["x"].rearrange("(t p) n -> p t n", p=P)).then_inc(x_again_landed, 16)
            act.dma_start(row, A["g_post_mix"].broadcast_to([P, D])).then_inc(rows_landed, 16)
            steps(OUT)
            branch_root(0)
            act.wait_ge(res_added, TT)
            squares(xr, NORMS["x1"], xn[:, 0, :])
            act.dma_start(row, A["g_post_ffn"].broadcast_to([P, D])).then_inc(rows_landed, 16)
            steps(BEFORE_FFN)
            for part, tiles in enumerate(FF_PARTS):
                ff = f"ff{part}"
                with act.Fori(0, tiles // 4) as i:
                    for u in range(8):
                        g = POS[("unit", ff, u)]
                        cut(g + LEAD, i, 8)
                        if u % 2:
                            act.wait_ge(units_done, i * 8 + (g + 1))
                            act.activation(work[:, u // 2, 0:S], stream_bank(B0[ff] + u // 2)[:, 0:S],
                                           ACT.Silu).then_inc(ff_gate, 1)
                steps(FFN_OUT[part])
            did.wait()
            act.nop().then_inc(res_squares, 1)
            branch_root(1)
            act.wait_ge(res_added, 2 * TT)
            squares(xr, NORMS["x2"], xn[:, 0, :])
            act.dma_start(x_kept.rearrange("(t p) n -> p t n", p=P), xr).then_inc(x_stored, 16)
            steps(BEFORE_S5)

            def tables(value, buf):
                act.wait_ge(ssm_turns, value)
                did(act.activation(whole_t[buf], frac_t, ACT.Identity, bias=round_up[:, 0:1]))
                did.wait()
                act.activation(whole_t[buf], whole_t[buf], ACT.Identity, bias=round_back[:, 0:1]).then_inc(ssm_whole, 1)
                act.wait_ge(ssm_frac, value)
                did(act.activation(abs_t, frac_t, ACT.Abs))
                did(act.activation(sin_t[buf], frac_t, ACT.Sin, scale=TURN_F))
                did.wait()
                act.activation(cos_t[buf], abs_t, ACT.Sin, scale=-TURN_F, bias=half_pi[:, 0:1]).then_inc(ssm_trig, 1)

            act.dma_start(ssm_in[:, 0, :], A["ssm_bc"][0]).then_inc(ssm_landed[0], 16)
            act.wait_ge(x_stored, 16)
            tables(1, 0)
            act.nop().then_inc(ssm_gelu, SSM_GELU0)
            with act.Fori(0, SSM_CHUNKS // SSM_BODY) as i:
                did.enter(i, 3 * SSM_BODY)
                def gelu(cc):
                    b = B0["sz"] + 2 * cc + 1
                    act.wait_ge(evacuated[b % 4], i * 2 + (b // 4 + 1))
                    act.activation(uT[:, bass.ds(i * SSM_BODY + cc, 1), :].rearrange("p a t -> p (a t)"),
                                   work[:, TMP[cc % 2], 0:S], ACT.Gelu_apprx_tanh).then_inc(ssm_gelu, 1)

                for cc in range(SSM_BODY):
                    buf = (cc + 1) % 2
                    act.wait_ge(ssm_y, i * (SSM_BODY * PAIRS) + PAIRS * cc + SSM_AHEAD)
                    act.dma_start(ssm_in[:, buf, :], A["ssm_bc"][bass.ds(i * SSM_BODY + (cc + 1), 1)]
                                  .rearrange("a p n -> p (a n)")).then_inc(ssm_landed[buf], 16)
                    g = POS[("unit", "sz", cc)]
                    cut(g + LEAD, i, SSM_BODY)
                    if cc:
                        gelu(cc - 1)
                    tables(i * SSM_BODY + (cc + 2), buf)
                    b = B0["sz"] + 2 * cc
                    act.wait_ge(units_done, i * SSM_BODY + (g + 1))
                    act.activation(zT[1][:, bass.ds(i * SSM_BODY + cc, 1), :].rearrange("p a t -> p (a t)"),
                                   stream_bank(b)[:, 0:S], ACT.Silu).then_inc(evacuated[b % 4], 1)
                gelu(SSM_BODY - 1)
                did.leave(SSM_CHUNKS // SSM_BODY)
            act.wait_ge(ssm_landed[0], 16 * (SSM_CHUNKS // 2 + 1))
            act.wait_ge(ssm_gelu, SSM_CHUNKS + SSM_GELU0)
            act.wait_ge(ssm_trig, SSM_CHUNKS + 1)
            act.dma_start(xr, x_kept.rearrange("(t p) n -> p t n", p=P)).then_inc(x_again_landed, 16)
            for q in range(4):
                act.activation(r32(yT[0][:, 4 * q:4 * q + 4, :]), uT[:, 4 * q:4 * q + 4, :], ACT.Copy).then_inc(y_hi, 1)
            steps([("unit", "glu", u) for u in range(16)] + BEFORE_S5_OUT + S5_OUT)
            act.wait_ge(res_added, 3 * TT)
            squares(xr, NORMS["x3"], xn[:, 0, :])
            act.dma_start(early[:, 0:LATE], A["late"]).then_inc(late_landed, 16)
            steps(NSA)
            steps(BEFORE_NSA_OUT + [("unit", "no", u) for u in range(16)])
            act.dma_start(final_row, A["final_norm_g"].broadcast_to([P, D])).then_inc(final_row_landed, 16)
            act.wait_ge(res_added, 4 * TT)
            squares(xr, NORMS["out"], xn[:, 0, :])

        @block.vector
        def _(dve):
            did = Steps(dve, dve_steps)

            def then(ins):
                did(ins)
                did.wait()

            def rms(n_norm, src, dst):
                dve.wait_ge(norm_squares, n_norm + 1)
                dve.tensor_scalar(stat[:, 2:4], stat[:, 0:2], 1.0 / D, EPS, ALU.mult, ALU.add).then_inc(norm_mean, 1)
                dve.wait_ge(norm_root, n_norm + 1)
                then(dve.reciprocal(stat[:, 4:6], stat[:, 2:4]))
                for t in range(TT):
                    dve.tensor_scalar(dst[:, t, :], src[:, t, :], stat[:, 4 + t:5 + t], None,
                                      ALU.mult).then_inc(norm_scaled, 1)

            def angles():
                dve.wait_ge(pos_landed, 16)
                then(dve.tensor_copy(rope_pos, pos_i))
                for w in range(2):
                    r, k = rope_ang[w], rope_k
                    then(dve.tensor_scalar(r, rope_pos, freq[:, w:w + 1], None, ALU.mult))
                    then(dve.tensor_scalar(k, r, 1.0 / TURN, ROUND, ALU.mult, ALU.add))
                    then(dve.tensor_scalar(k, k, -ROUND, None, ALU.add))
                    then(dve.scalar_tensor_tensor(out=r, in0=k, scalar=-TURN_HI, in1=r, op0=ALU.mult, op1=ALU.add))
                    then(dve.scalar_tensor_tensor(out=r, in0=k, scalar=-TURN_LO, in1=r, op0=ALU.mult, op1=ALU.add))
                    dve.tensor_scalar(r, r, -PI, PI, ALU.max, ALU.min).then_inc(ang_ready, 1)
                    dve.wait_ge(ang_ready, w + 1)

            def s5_states():
                lr, li, dt, w_, e_, a_, b_, c_ = (s5_raw[:, 0, :], s5_raw[:, 1, :], s5_dt, s5_tmp[0], s5_tmp[1], s5_tmp[2],
                                                 s5_tmp[3], s5_tmp[4])
                mag, turn, kre, kim, nkim = (s5[:, r, 0:SSM_CHUNKS * PAIRS] for r in range(5))
                dve.wait_ge(s5_raw_landed, 16)
                dve.wait_ge(s5_ready, 1)
                then(dve.tensor_tensor(w_, lr, dt, ALU.mult))
                then(dve.tensor_scalar(w_, w_, -20.0, 1.0 / 32, ALU.max, ALU.mult))
                then(dve.tensor_scalar(e_, w_, 1.0 / 8, 1.0, ALU.mult, ALU.add))
                for m in range(7, 1, -1):
                    then(dve.tensor_tensor(e_, e_, w_, ALU.mult))
                    then(dve.tensor_scalar(e_, e_, 1.0 / m, 1.0, ALU.mult, ALU.add))
                then(dve.tensor_tensor(e_, e_, w_, ALU.mult))
                for _ in range(5):
                    then(dve.scalar_tensor_tensor(out=e_, in0=e_, scalar=2.0, in1=e_, op0=ALU.add, op1=ALU.mult))
                then(dve.tensor_scalar(mag, e_, 1.0, None, ALU.add))
                then(dve.tensor_tensor(a_, li, dt, ALU.mult))
                then(dve.tensor_scalar(b_, a_, 1.0 / TURN, ROUND, ALU.mult, ALU.add))
                then(dve.tensor_scalar(b_, b_, -ROUND, None, ALU.add))
                then(dve.scalar_tensor_tensor(out=a_, in0=b_, scalar=-TURN_HI, in1=a_, op0=ALU.mult, op1=ALU.add))
                then(dve.scalar_tensor_tensor(out=a_, in0=b_, scalar=-TURN_LO, in1=a_, op0=ALU.mult, op1=ALU.add))
                then(dve.tensor_scalar(turn, a_, 1.0 / TURN, None, ALU.mult))
                dve.tensor_scalar(s5_thr, a_, -PI, PI, ALU.max, ALU.min).then_inc(s5_ready, 1)
                dve.wait_ge(trig_done, 1)
                then(dve.tensor_tensor(a_, s5_sin, mag, ALU.mult))
                then(dve.tensor_tensor(b_, s5_sin2, s5_sin2, ALU.mult))
                then(dve.tensor_tensor(b_, b_, mag, ALU.mult))
                then(dve.scalar_tensor_tensor(out=e_, in0=b_, scalar=-2.0, in1=e_, op0=ALU.mult, op1=ALU.add))
                then(dve.tensor_tensor(b_, lr, lr, ALU.mult))
                then(dve.tensor_tensor(c_, li, li, ALU.mult))
                then(dve.tensor_tensor(b_, b_, c_, ALU.add))
                then(dve.reciprocal(b_, b_))
                then(dve.tensor_tensor(c_, e_, lr, ALU.mult))
                then(dve.tensor_tensor(w_, a_, li, ALU.mult))
                then(dve.tensor_tensor(c_, c_, w_, ALU.add))
                then(dve.tensor_tensor(kre, c_, b_, ALU.mult))
                then(dve.tensor_tensor(c_, a_, lr, ALU.mult))
                then(dve.tensor_tensor(w_, e_, li, ALU.mult))
                then(dve.tensor_tensor(c_, c_, w_, ALU.subtract))
                then(dve.tensor_tensor(kim, c_, b_, ALU.mult))
                dve.tensor_scalar(nkim, kim, -1.0, None, ALU.mult).then_inc(s5_params, 1)
                dve.wait_ge(s5_params, 1)

            def softmax_tail(a, n, p, masked):
                at = 16 + 8 * (a % 2)
                if masked:
                    dve.wait_ge(head_exp, MASKED[a] + 1)
                else:
                    dve.wait_ge(*read(n))
                then(dve.reciprocal(stat[:, at + 6:at + 8], stat[:, at + 4:at + 6]))
                dve.tensor_tensor(p, p, stat[:, at + 6:at + 8].unsqueeze(2).broadcast_to([P, TT, S]),
                                  ALU.mult).then_inc(head_prob, 1)

            def maximum(a, src, scale):
                at = 16 + 8 * (a % 2)
                then(dve.tensor_reduce(stat[:, at:at + 2], src, AX, ALU.max))
                dve.tensor_scalar(stat[:, at + 2:at + 4], stat[:, at:at + 2], -scale, None, ALU.mult).then_inc(head_max, 1)

            def top_k(step):
                if step[0] == "topk":
                    t, part = step[1:]
                    if (t, part) == (0, 0):
                        dve.wait_ge(idx_added, N_IDX)
                    if part == 0:
                        then(dve.tensor_tensor(top[:, t, :], score[:, t, :], causal[:, t, :], ALU.add))
                    for _ in range(2):
                        then(dve.max(stat[:, 8:16], top[:, t, :]))
                        then(dve.match_replace(out=top[:, t, :], in_to_replace=stat[:, 8:16], in_values=top[:, t, :],
                                               imm_value=TAKEN))
                else:
                    then(dve.tensor_scalar(top, top, TAKEN, None, ALU.is_equal))
                    then(dve.tensor_scalar(top, top, -1.0, -NEG, ALU.add, ALU.mult))
                    dve.tensor_tensor(selbias, top, causal, ALU.add).then_inc(sel_ready, 1)
                    dve.wait_ge(sel_ready, 1)

            def local(step):
                if step[0] == "rms":
                    dve.wait_ge(x_landed, 16)
                    rms(1, x_in, x_in)
                elif step[0] == "angles":
                    angles()
                elif step[0] == "s5_params":
                    s5_states()
                else:
                    top_k(step)

            def flat2(ap):
                return ap.rearrange("p (t s) -> p t s", t=TT)

            def side(step):
                kind, n = step[0], SIDE[step]
                done = side_read[n % 4]
                if kind == "norm":
                    tag, j = step[1:]
                    dst, gain, shift = NORM_TO[tag]
                    dve.wait_ge(rounded, ROUNDED[step] + 1)
                    for c in range(2):
                        k = 2 * j + c
                        part, hi_k, lo_k = side_bank(n)[:, c * S:(c + 1) * S], dst[0][:, k, :], dst[1][:, k, :]
                        if shift is None:
                            ins = dve.scalar_tensor_tensor(out=r32(lo_k), in0=part, scalar=gain[:, k:k + 1], in1=as32(hi_k),
                                                           op0=ALU.mult, op1=ALU.subtract)
                        else:
                            then(dve.tensor_scalar(lo_k, part, gain[:, k:k + 1], shift[:, k:k + 1], ALU.mult, ALU.add))
                            ins = dve.tensor_tensor(r32(lo_k), lo_k, as32(hi_k), ALU.subtract)
                    ins.then_inc(done, 1)
                elif kind in ("mem_values", "att_values", "turn_y", "turn_mix", "turn_o"):
                    j = step[1]
                    dst = {"mem_values": o_cT, "att_values": o_aT, "turn_y": o_bT, "turn_mix": mixT, "turn_o": oT}[kind]
                    dve.wait_ge(rounded, ROUNDED[step] + 1)
                    if kind == "att_values":
                        dve.tensor_tensor(r32(dst[1][:, j, :]), side_bank(n)[:, 0:S], as32(dst[0][:, j, :]),
                                          ALU.subtract).then_inc(done, 1)
                    else:
                        dve.tensor_tensor(r32(both(dst[1], j)), side_bank(n), as32(both(dst[0], j)), ALU.subtract).then_inc(done, 1)
                elif kind == "mod_turn":
                    mod_vec(step[1], step[2], n)
                elif kind == "rope":
                    r = ROPE[step]
                    phase, b = step[1:]
                    w = 1 if phase in ("ik", "iq") else 0
                    heads = 1 if phase == "ik" else 2
                    raw = work[:, TMP[r % 2], 0:heads * S].rearrange("p (h t) -> p h t", h=heads)
                    swapped = work[:, TMP[2], 0:heads * S].rearrange("p (h t) -> p h t", h=heads)
                    cos, sin = (ropes[:, 2 * w + k, :].unsqueeze(1).broadcast_to([P, heads, S]) for k in range(2))
                    if r == 0:
                        dve.wait_ge(rope_ready, 2)
                    else:
                        dve.wait_ge(roped, r)
                    dve.wait_ge(*written(n))
                    did(dve.tensor_tensor(raw, raw, cos, ALU.mult))
                    dve.tensor_tensor(swapped, side_bank(n)[:, 0:heads * S].rearrange("p (h t) -> p h t", h=heads), sin,
                                      ALU.mult).then_inc(done, 1)
                    did.wait()
                    dve.wait_ge(*read(n))
                    if phase == "ik":
                        did(dve.tensor_tensor(ikT[0:64, 0, :], raw[0:64, 0, :], swapped[0:64, 0, :], ALU.add))
                        dve.tensor_tensor(ikT[64:128, 1, :], raw[64:128, 0, :], swapped[64:128, 0, :],
                                          ALU.add).then_inc(roped, 1)
                    else:
                        dst = {"iq": iqT, "aq": aqT, "ak": akT, "rq": rqT, "rk": rkT}[phase]
                        dve.tensor_tensor(dst[:, 2 * b:2 * b + 2, :], raw, swapped, ALU.add).then_inc(roped, 1)
                elif kind == "idx_w":
                    dve.wait_ge(*written(n))
                    dve.tensor_scalar(iw[:, :, :], side_bank(n)[:, 0:TT * N_IDX].rearrange("p (t h) -> p t h", t=TT),
                                      64 ** -0.5 * N_IDX ** -0.5, None, ALU.mult).then_inc(done, 1)
                    then(dve.memset(score, 0.0))
                    dve.wait_ge(*read(n))
                elif kind == "idx":
                    h = step[1]
                    dve.wait_ge(*read(n))
                    if h:
                        dve.wait_ge(idx_added, h)
                    for t in range(TT):
                        ins = dve.scalar_tensor_tensor(out=score[:, t, :], in0=halves(prob[h % 2])[:, t, :],
                                                       scalar=iw[:, t, h:h + 1], in1=score[:, t, :], op0=ALU.mult,
                                                       op1=ALU.add)
                    ins.then_inc(idx_added, 1)
                elif kind == "mem_logits":
                    a = HEADS[step]
                    dve.wait_ge(*written(n))
                    maximum(a, flat2(side_bank(n)), 0.0625)
                    softmax_tail(a, n, halves(prob[a % 2]), False)
                elif kind in ("att_logits", "sel_logits", "win_logits"):
                    a = HEADS[step]
                    p = halves(prob[a % 2])
                    dve.wait_ge(*written(n))
                    dve.wait_ge(*written(SIDE[TURNS[a - 2]]))
                    dve.tensor_tensor(p, flat2(side_bank(n)), selbias if kind == "att_logits" else causal,
                                      ALU.add).then_inc(done, 1)
                    dve.wait_ge(*read(n))
                    maximum(a, p, HD ** -0.5)
                    softmax_tail(a, n, p, True)
                elif kind == "ret_scores":
                    h = step[1]
                    if h == 0:
                        dve.wait_ge(decay_landed, 16)
                    dve.wait_ge(*written(n))
                    if h >= 2:
                        dve.wait_ge(*written(SIDE[("ret_values", h - 2)]))
                    sd = work[:, prob[h % 2], :]
                    dve.tensor_tensor(sd[:, 0:S], side_bank(n)[:, 0:S], decay[:, h, :], ALU.mult)
                    dve.tensor_tensor(sd[:, S:S + P], side_bank(n)[:, S:S + P], decay[:, h, 0:P],
                                      ALU.mult).then_inc(done, 1)
                elif kind == "ret_values":
                    h = step[1]
                    dve.wait_ge(*written(n))
                    if h:
                        did.wait()
                    for t in range(TT):
                        did(dve.bn_stats(bn[:, t, :], side_bank(n)[:, t * RETV:(t + 1) * RETV]))
                    did.wait()
                    for t in range(TT):
                        k = TT * h + t
                        did(dve.bn_aggr(ret_stat[:, k, :], bn[:, t, :]))
                    dve.tensor_copy(rv[:, :, h * RETV:(h + 1) * RETV], flat2(side_bank(n))).then_inc(done, 1)
                    if h == N_RET - 1:
                        dve.wait_ge(*read(n))
                        did.wait()
                        dve.tensor_scalar(stat[:, 48:64], ret_stat[:, :, 1], EPS, None, ALU.add).then_inc(ret_var, 1)
                        dve.wait_ge(ret_root, 1)
                        then(dve.reciprocal(stat[:, 48:64], stat[:, 48:64]))
                        for hh in range(N_RET):
                            for t in range(TT):
                                k = TT * hh + t
                                yh = rv[:, t, hh * RETV:(hh + 1) * RETV]
                                did(dve.tensor_scalar(yh, yh, ret_stat[:, k, 0:1], stat[:, 48 + k:49 + k],
                                                      ALU.subtract, ALU.mult))
                        did.wait()
                elif kind == "gate":
                    tag, j = step[1:]
                    piece = PIECES.index(tag + "_gate")
                    g = GATES[step]
                    if tag == "nsa" and j == 0:
                        dve.wait_ge(o_added, O_ADDS)
                    if j >= 2:
                        dve.wait_ge(*written(SIDE[(kind, tag, j - 2)]))
                    for c in range(4):
                        k = 4 * j + c
                        ins = dve.tensor_scalar(work[:, TMP[j % 2], c * P:(c + 1) * P], ident, modv[:, piece, k:k + 1],
                                                None, ALU.mult)
                    ins.then_inc(diag_ready, 1)
                elif kind == "cmp_hidden" and step[1] == 0:
                    then(dve.memset(p_cmp, 0.0))
                elif kind == "cmp_out" and step[1] == 1:
                    dve.wait_ge(*written(n))
                    dve.tensor_tensor(v_tmp[0:N_CMP, :, :],
                                      side_bank(n)[0:N_CMP, :].rearrange("p (g d) -> p g d", g=NKV),
                                      b2_row[0:N_CMP, :].unsqueeze(1).broadcast_to([N_CMP, NKV, P]),
                                      ALU.add).then_inc(done, 1)
                    dve.wait_ge(*read(n))
                    dve.wait_ge(v_zero, 1)
                    for h in range(HPG):
                        ins = dve.tensor_copy(v_blocks[32 * h:32 * h + N_CMP, :, h * P:(h + 1) * P], v_tmp[0:N_CMP, :, :])
                    ins.then_inc(cmp_vblock, 1)
                    for q in range(4):
                        dve.wait_ge(hn_hi, q + 1)
                        whole, top_part = (x[:, 4 * q:4 * q + 4, :] for x in (hnT[1], hnT[0]))
                        dve.tensor_tensor(r32(whole), whole, as32(top_part), ALU.subtract).then_inc(hn_cut, 1)
                elif kind == "cmp_logits":
                    a, g = HEADS[step], step[1]
                    p4 = p_cmp.rearrange("p (t h n) -> p t h n", t=TT, h=HPG)[:, :, :, 0:N_CMP]
                    p3 = p_cmp.rearrange("p (a n) -> p a n", n=CMP_PAD)[:, :, 0:N_CMP]
                    add, keep = (m.unsqueeze(2).broadcast_to([P, TT, HPG, N_CMP]) for m in (cmp_add, cmp_keep))
                    logit4 = side_bank(n)[:, 0:2 * P].rearrange("p (t h n) -> p t h n", t=TT, h=HPG)[:, :, :, 0:N_CMP]
                    st = stat[:, 8:16]

                    def row_of(x):
                        return x.unsqueeze(2).broadcast_to([P, TT * HPG, N_CMP])

                    dve.wait_ge(*written(n))
                    if g:
                        dve.wait_ge(*written(SIDE[("cmp_turn", g - 1)]))
                    dve.tensor_tensor(p4, logit4, add, ALU.add).then_inc(done, 1)
                    dve.wait_ge(*read(n))
                    then(dve.tensor_reduce(st, p3, AX, ALU.max))
                    dve.tensor_tensor(p3, p3, row_of(st), ALU.subtract).then_inc(head_max, 1)
                    dve.wait_ge(head_exp, MASKED[a] + 1)
                    then(dve.tensor_reduce(st, p3, AX, ALU.add))
                    then(dve.reciprocal(st, st))
                    then(dve.tensor_tensor(p4, p4, keep, ALU.mult))
                    dve.tensor_tensor(p3, p3, row_of(st), ALU.mult).then_inc(head_prob, 1)
                elif kind in ("cmp_values", "sel_values", "win_values"):
                    br = ("cmp", "sel", "win").index(kind[:3])
                    g = step[1] if br == 0 else step[1] // HPG
                    c = 3 * g + br
                    k = O_INDEX[step]
                    dve.wait_ge(*written(n))
                    if k == 0:
                        dve.wait_ge(*read(SIDE[("ngate", 0)]))
                    else:
                        dve.wait_ge(o_added, k)
                    for w in (emptied(B0["nz"] + 2 * c), emptied(B0["nz"] + 2 * c + 1)):
                        dve.wait_ge(*w)
                    if br == 0:
                        t = step[2]
                        head = gates[:, t, HPG * g:HPG * (g + 1)].unsqueeze(2).broadcast_to([P, HPG, P])
                        part = work[:, TMP[1], :]
                        dve.tensor_tensor(part.rearrange("p (h d) -> p h d", h=HPG),
                                          side_bank(n).rearrange("p (h d) -> p h d", h=HPG), head, ALU.mult).then_inc(done, 1)
                        dve.wait_ge(*read(n))
                        dve.tensor_tensor(o_tok[:, t, g * CHUNK:(g + 1) * CHUNK], part, zs[:, c % 2, t, :],
                                          ALU.mult).then_inc(o_added, 1)
                    else:
                        h = step[1]
                        part = work[:, TMP[1], 0:2 * P].rearrange("p (t d) -> p t d", t=TT)
                        gate = gates[:, :, br * NQ + h:br * NQ + h + 1].broadcast_to([P, TT, P])
                        at, o = (h % HPG) * P, o_tok[:, :, h * P:(h + 1) * P]
                        dve.tensor_tensor(part, side_bank(n)[:, 0:2 * P].rearrange("p (t d) -> p t d", t=TT), gate,
                                          ALU.mult).then_inc(done, 1)
                        dve.wait_ge(*read(n))
                        then(dve.tensor_tensor(part, part, zs[:, c % 2, :, at:at + P], ALU.mult))
                        dve.tensor_tensor(o, o, part, ALU.add).then_inc(o_added, 1)

            def unit(phase, u):
                if phase == "kvt" and u % 2 and u < 8:
                    j, b = u // 4, B0["kvt"] + u // 2
                    dve.wait_ge(*multiplied(phase, u))
                    g0 = 2 * (u // 2 % 2)
                    for half in range(2):
                        pe_ = cmp_pe[:, j, half * CMP_STRIDE:(half + 1) * CMP_STRIDE]
                        ins = dve.tensor_tensor(
                            cin[:, j, half, g0:g0 + 2, :].rearrange("p g (n r) -> p (g n) r", r=CMP_STRIDE),
                            stream_bank(b).rearrange("p (m r) -> p m r", r=CMP_STRIDE),
                            pe_.unsqueeze(1).broadcast_to([P, 2 * S // CMP_STRIDE, CMP_STRIDE]), ALU.add)
                    ins.then_inc(evacuated[b % 4], 1)
                elif phase == "rg" and u % 4 == 3:
                    c = u // 4
                    for t in range(TT):
                        dve.wait_ge(*emptied(B0[phase] + 2 * c + t))
                        yc = rv[:, t, c * CHUNK:(c + 1) * CHUNK]
                        dve.tensor_tensor(yc, yc, work[:, TMP[t], :], ALU.mult).then_inc(ret_gated, 1)
                elif phase == "fo1" and (u + 1) % (FF_PARTS[1] // KG) == 0:
                    dve.wait_ge(*multiplied(phase, u))
                    c = u // (FF_PARTS[1] // KG)
                    for t in range(TT):
                        b = B0[phase] + 2 * c + t
                        yc = y[:, t, c * CHUNK:(c + 1) * CHUNK]
                        dve.wait_ge(*emptied(B0["fo0"] + 2 * c + t))
                        dve.tensor_tensor(yc, stream_bank(b), yc, ALU.add).then_inc(evacuated[b % 4], 1)
                elif phase == "glu" and u % 2:
                    b = u // 2
                    sig = work[:, b % 4, :]
                    top_part, whole = both(zT[0], b), both(zT[1], b)
                    dve.wait_ge(glu_gate, b + 1)
                    then(dve.tensor_tensor(sig, sig, both(uT, b), ALU.mult))
                    then(dve.tensor_tensor(whole, whole, sig, ALU.mult))
                    then(dve.tensor_scalar(r32(top_part), whole, 1.0, None, ALU.mult))
                    dve.tensor_tensor(r32(whole), whole, as32(top_part), ALU.subtract).then_inc(evacuated[(B0["glu"] + b) % 4], 1)
                elif phase in ("so", "no") and u % 4 == 3:
                    add_gated(2 if phase == "so" else 3, phase, u // 4)

            def cut(g, i=None, per=0, per_hi=0):
                if g >= UNITS:
                    return
                slot = ring[:, g % RING, :]
                if ORDER[g][1] == "cw":
                    dve.wait_ge(cut_done, g)
                    dve.nop().then_inc(cut_done, 1)
                elif ORDER[g][0] == "unit":
                    dve.wait_ge(hi_made, HI[g] if i is None else i * per_hi + HI[g])
                    dve.tensor_tensor(r32(slot), slot, as32(hi[:, g % RING, :]), ALU.subtract).then_inc(cut_done, 1)
                else:
                    _, piece, k = ORDER[g]
                    sums = sums_of(piece)
                    dve.wait_ge(landed[g % RING], 16 * (g // RING + 1) if i is None else i * (per // RING * 16) + 16 * (g // RING + 1))
                    if k == 0 and i is not None:
                        dve.wait_ge(side_done, i * 4 + SIDE[("mod_turn", MIX_PIECE, 0)])
                    elif k == 0 and ("mod_turn", piece - 1, 3) in SIDE:
                        dve.wait_ge(*written(SIDE[("mod_turn", piece - 1, 3)]))
                    if k == 0 and piece in (5, 6):
                        dve.wait_ge(act_cut, sum(FF_PARTS[:piece - 4]))
                    dve.wait_ge(cut_done, g if i is None else i * per + g)
                    if k == 0:
                        ins = dve.tensor_scalar(sums, slot, c_act[:, k:k + 1], None, ALU.mult)
                    else:
                        ins = dve.scalar_tensor_tensor(out=sums, in0=slot, scalar=c_act[:, k:k + 1], in1=sums,
                                                       op0=ALU.mult, op1=ALU.add)
                    ins.then_inc(cut_done, 1)

            def mod_vec(piece, c, n, i=None):
                k = slice(4 * c, 4 * c + 4)
                if i is None:
                    dve.wait_ge(*written(n))
                    dst, bias = modv[:, piece, k], vecs[:, V[PIECES[piece]], k]
                else:
                    dve.wait_ge(side_done, i * 4 + (n + 1))
                    dst = modv[:, bass.ds(i + piece, 1), k].rearrange("p a k -> p (a k)")
                    bias = vecs[:, bass.ds(i + V[PIECES[piece]], 1), k].rearrange("p a k -> p (a k)")
                dve.tensor_tensor(dst, side_bank(n)[:, 0:4], bias, ALU.add).then_inc(side_read[n % 4], 1)

            def steps(todo):
                for step in todo:
                    for x in visited(step):
                        cut(POS[x] + LEAD)
                    if step[0] == "unit":
                        unit(step[1], step[2])
                    elif step[0] in LOCAL:
                        if step[0] != "mod":
                            local(step)
                    else:
                        side(step)

            def add_branch(n, src):
                then(dve.tensor_reduce(stat[:, 40:42], stat[:, 32:40].rearrange("p (t c) -> p t c", t=TT), AX, ALU.add))
                dve.tensor_scalar(stat[:, 40:42], stat[:, 40:42], 1.0 / D, EPS, ALU.mult, ALU.add).then_inc(res_mean, 1)
                dve.wait_ge(res_root, n + 1)
                then(dve.reciprocal(stat[:, 42:44], stat[:, 40:42]))
                dve.wait_ge(rows_landed, 16 * (n + 1))
                if n == 0:
                    dve.wait_ge(x_again_landed, 16)
                for t in range(TT):
                    then(dve.scalar_tensor_tensor(out=src[:, t, :], in0=src[:, t, :], scalar=stat[:, 42 + t:43 + t],
                                                  in1=row, op0=ALU.mult, op1=ALU.mult))
                    dve.tensor_tensor(xr[:, t, :], xr[:, t, :], src[:, t, :], ALU.add).then_inc(res_added, 1)

            def add_gated(n, phase, c):
                tag = "s5" if phase == "so" else "nsa"
                gate = row if phase == "so" else nsa_row
                if c == 0:
                    if phase == "so":
                        dve.wait_ge(x_again_landed, 32)
                    for w in last_reads([SIDE[("gate", tag, j)] for j in range(4)]):
                        dve.wait_ge(*w)
                    for j in range(2):
                        dve.wait_ge(*written(SIDE[("gate", tag, 2 + j)]))
                dve.wait_ge(*multiplied(phase, 4 * c + 3))
                for t in range(TT):
                    b = B0[phase] + 2 * c + t
                    part, x = work[:, TMP[t], :], xr[:, t, c * CHUNK:(c + 1) * CHUNK]
                    if c:
                        did.wait()
                    dve.tensor_tensor(part, stream_bank(b), gate[:, c * CHUNK:(c + 1) * CHUNK],
                                      ALU.mult).then_inc(evacuated[b % 4], 1)
                    dve.wait_ge(*emptied(b))
                    add = dve.tensor_tensor(x, x, part, ALU.add)
                    if c == 3:
                        add.then_inc(res_added, 1)
                    else:
                        did(add)

            dve.wait_ge(consts_landed, 32)
            dve.wait_ge(consts_made, CONSTS_MADE)
            dve.wait_ge(mem_landed, 16)
            rms(0, mem_in, mem_in)
            dve.wait_ge(act_ready, 1)
            cut(0)
            cut(1)
            steps(MIXER)
            with dve.Fori(0, MIX_LOOPS) as i:
                for step in MIX_BODY:
                    cut(POS[step] + LEAD, i, MIX_TURN, 80 // MIX_LOOPS)
                    if step[0] != "unit" or step[2] + 1 not in MIX_ENDS:
                        continue
                    m = MIX_ENDS.index(step[2] + 1)
                    c, br = divmod(m, 3)
                    b = B0["mix"] + 4 * m + 2
                    dve.wait_ge(units_done, i * MIX_TURN + (POS[step] + 1))
                    for t in range(TT):
                        dst = mixed[:, t, bass.ds((i * 2 + c) * CHUNK, CHUNK)]
                        gate = work[:, (m % 2) * 2 + t, :]
                        dve.wait_ge(evacuated[(b - 2 + t) % 4], i * 6 + ((b - 2 + t) // 4 + 1))
                        if br == 0:
                            dve.tensor_tensor(dst, stream_bank(b + t), gate, ALU.mult).then_inc(evacuated[(b + t) % 4], 1)
                        else:
                            dve.tensor_tensor(gate, stream_bank(b + t), gate, ALU.mult).then_inc(mix_part, 1)
                            dve.wait_ge(mix_part, i * 8 + (c * 4 + (br - 1) * 2 + t + 1))
                            dve.wait_ge(evacuated[(b - 4 + t) % 4], i * 6 + ((b - 4 + t) // 4 + 1))
                            dve.tensor_tensor(dst, dst, gate, ALU.add).then_inc(evacuated[(b + t) % 4], 1)
                for _, piece, c in MIX_TURNS:
                    mod_vec(piece, c, SIDE[("mod_turn", piece, c)], i)
            for w in last_banks("mix"):
                dve.wait_ge(*w)
            dve.nop().then_inc(mix_done, 1)
            steps(AFTER_MIX + OUT)
            for w in last_banks("wo"):
                dve.wait_ge(*w)
            add_branch(0, y)
            rms(NORMS["x1"], xr, xn)
            steps(BEFORE_FFN)
            tile0 = 0
            for part, tiles in enumerate(FF_PARTS):
                ff = f"ff{part}"
                with dve.Fori(0, tiles // 4) as i:
                    for u in range(8):
                        g = POS[("unit", ff, u)]
                        cut(g + LEAD, i, 8, 8)
                        if u % 2 == 0:
                            continue
                        k = u // 2
                        b = B0[ff] + k
                        top_part, low_part = (x[:, bass.ds(i * 4 + k, 1), :].rearrange("p a t -> p (a t)") for x in actT)
                        whole = work[:, k, S:2 * S]
                        dve.wait_ge(ff_gate, i * 4 + (tile0 + k + 1))
                        dve.tensor_tensor(whole, stream_bank(b)[:, S:2 * S], work[:, k, 0:S],
                                          ALU.mult).then_inc(evacuated[b % 4], 1)
                        dve.wait_ge(evacuated[b % 4], i + (b // 4 + 1))
                        dve.tensor_scalar(r32(top_part), whole, 1.0, None, ALU.mult).then_inc(act_hi, 1)
                        dve.wait_ge(act_hi, i * 4 + (tile0 + k + 1))
                        dve.tensor_tensor(r32(low_part), whole, as32(top_part), ALU.subtract).then_inc(act_cut, 1)
                tile0 += tiles
                steps(FFN_OUT[part])
            dve.wait_ge(res_squares, 1)
            add_branch(1, y)
            rms(NORMS["x2"], xr, xn)

            def modulation(row_, gain, scale, n):
                ins = dve.scalar_tensor_tensor(out=gains[:, row_, :], in0=modv[:, PIECES.index(scale), :], scalar=1.0,
                                               in1=vecs[:, V[gain], :], op0=ALU.add, op1=ALU.mult)
                ins.then_inc(mod_gain, 1) if n else did(ins)

            modulation(0, "norm0", "s5_scale", 1)
            steps(BEFORE_S5)
            modulation(1, "kv_norm", "kv_scale", 0)
            modulation(2, "norm1", "nsa_scale", 1)
            n_pairs = SSM_BODY * PAIRS
            dve.nop().then_inc(ssm_prod, SSM_AHEAD)
            with dve.Fori(0, SSM_CHUNKS // SSM_BODY) as i:
                did.enter(i, n_pairs * 2)

                def table(t, cc, q):
                    return t[cc % 2][:, q * S:(q + 1) * S].unsqueeze(1).broadcast_to([P, 2, S])

                def products(cc, q):
                    p = cc * PAIRS + q
                    bank = flat2(side_bank(SSM_SIDE0 + p))
                    dve.wait_ge(side_done, i * n_pairs + (SSM_SIDE0 + p + 1))
                    dve.wait_ge(ssm_y, i * n_pairs + (p + 1))
                    did(dve.tensor_tensor(flat2(ssm_buf[q][0]), bank, table(cos_t, cc, q), ALU.mult))
                    dve.tensor_tensor(flat2(ssm_buf[q][1]), bank, table(sin_t, cc, q), ALU.mult).then_inc(ssm_prod, 1)

                def scans(cc, q):
                    p = cc * PAIRS + q
                    dve.wait_ge(ssm_rot, i * n_pairs + (p + 1))
                    col = s5[:, S_MAG, bass.ds(i * n_pairs + p, 1)]
                    for part in range(2):
                        z = ssm_buf[q][0][:, part * S:(part + 1) * S]
                        ins = dve.tensor_tensor_scan(z, col.broadcast_to([P, S]), z, 0.0, ALU.mult, ALU.add)
                    ins.then_inc(ssm_state, 1)

                def back(cc, q):
                    p = cc * PAIRS + q
                    dve.wait_ge(ssm_state, i * n_pairs + (p + 1))
                    did(dve.tensor_tensor(flat2(ssm_buf[q][1]), flat2(ssm_buf[q][0]), table(cos_t, cc, q), ALU.mult))
                    dve.tensor_tensor(flat2(ssm_buf[q][2]), flat2(ssm_buf[q][0]), table(sin_t, cc, q),
                                      ALU.mult).then_inc(ssm_back, 1)

                def skip(cc):
                    b = B0["sz"] + 2 * cc + 1
                    dve.wait_ge(ssm_y, i * n_pairs + (PAIRS * (cc + 1) + SSM_AHEAD))
                    dve.wait_ge(ssm_gelu, i * SSM_BODY + max(cc - 1 + SSM_GELU0, 1))
                    d_col = vecs[:, V["d_skip"], bass.ds(i * SSM_BODY + cc, 1)]
                    dve.scalar_tensor_tensor(out=work[:, TMP[cc % 2], 0:S],
                                             in0=uT[:, bass.ds(i * SSM_BODY + cc, 1), :].rearrange("p a t -> p (a t)"),
                                             scalar=d_col, in1=stream_bank(b)[:, 0:S], op0=ALU.mult,
                                             op1=ALU.add).then_inc(evacuated[b % 4], 1)

                for cc in range(SSM_BODY):
                    dve.wait_ge(ssm_trig, i * SSM_BODY + (cc + 1))
                    products(cc, 0)
                    products(cc, 1)
                    cut(POS[("unit", "sz", cc)] + LEAD, i, SSM_BODY, SSM_BODY)
                    if cc:
                        skip(cc - 1)
                    for q in range(PAIRS):
                        scans(cc, q)
                        if q + 2 < PAIRS:
                            products(cc, q + 2)
                        back(cc, q)
                skip(SSM_BODY - 1)
                did.leave(SSM_CHUNKS // SSM_BODY)
            dve.wait_ge(ssm_back, SSM_CHUNKS * PAIRS)
            for b in range(4):
                dve.nop().then_inc(side_read[b], SSM_CHUNKS)
            for q in range(4):
                dve.wait_ge(y_hi, q + 1)
                dve.tensor_tensor(r32(yT[1][:, 4 * q:4 * q + 4, :]), uT[:, 4 * q:4 * q + 4, :], as32(yT[0][:, 4 * q:4 * q + 4, :]),
                                  ALU.subtract).then_inc(y_cut, 1)
            steps([("unit", "glu", u) for u in range(16)] + BEFORE_S5_OUT + S5_OUT)
            rms(NORMS["x3"], xr, xn)
            dve.wait_ge(late_landed, 16)
            steps(NSA)
            steps(BEFORE_NSA_OUT + [("unit", "no", u) for u in range(16)])
            n_norm = NORMS["out"]
            dve.wait_ge(norm_squares, n_norm + 1)
            dve.tensor_scalar(stat[:, 2:4], stat[:, 0:2], 1.0 / D, EPS, ALU.mult, ALU.add).then_inc(norm_mean, 1)
            dve.wait_ge(norm_root, n_norm + 1)
            then(dve.reciprocal(stat[:, 4:6], stat[:, 2:4]))
            dve.wait_ge(final_row_landed, 16)
            for t in range(TT):
                dve.scalar_tensor_tensor(out=y_out[:, t, :], in0=xr[:, t, :], scalar=stat[:, 4 + t:5 + t], in1=final_row,
                                         op0=ALU.mult, op1=ALU.mult).then_inc(out_ready, 1)

        @block.gpsimd
        def _(pool):
            did = Steps(pool, pool_steps)

            pool.memset(ones[:, :], 1.0).then_inc(consts_made, 1)
            pool.memset(half_pi[:, :], float(np.pi / 2)).then_inc(consts_made, 1)
            pool.memset(round_up[:, :], ROUND).then_inc(consts_made, 1)
            pool.memset(round_back[:, :], -ROUND).then_inc(consts_made, 1)
            pool.memset(ikT, 0.0).then_inc(consts_made, 1)
            pool.memset(s5[:, :, :], 0.0).then_inc(consts_made, 1)

            f4 = frac_t.rearrange("p (q t) -> p q t", q=PAIRS)
            times = time_row.unsqueeze(1).broadcast_to([P, PAIRS, S])

            pool.wait_ge(s5_params, 1)
            for w in last_banks("su"):
                pool.wait_ge(*w)
            pool.tensor_tensor(f4, times, s5[:, S_TURN, 0:PAIRS].unsqueeze(2).broadcast_to([P, PAIRS, S]),
                               ALU.mult).then_inc(ssm_turns, 1)
            pool.wait_ge(ssm_whole, 1)
            pool.tensor_tensor(frac_t, frac_t, whole_t[0], ALU.subtract).then_inc(ssm_frac, 1)
            n_pairs = SSM_BODY * PAIRS
            with pool.Fori(0, SSM_CHUNKS // SSM_BODY) as i:
                did.enter(i, SSM_BODY * (6 + PAIRS))
                for cc in range(SSM_BODY):
                    buf = cc % 2
                    c_re, c_im = (ssm_in[:, buf, SSM_B + k * P:SSM_B + (k + 1) * P].rearrange("p (q c) -> p q c", q=PAIRS)
                                  for k in range(2))
                    f_re, f_im, f_neg = (s5[:, r, bass.ds(i * n_pairs + cc * PAIRS, PAIRS)].unsqueeze(2)
                                         .broadcast_to([P, PAIRS, 32]) for r in (S_KRE, S_KIM, S_NKIM))
                    k0, k1, k2 = (ssm_c[:, buf, k, :, :] for k in range(3))
                    t0, t1 = (ssm_tmp[:, k * P:(k + 1) * P].rearrange("p (q c) -> p q c", q=PAIRS) for k in range(2))
                    for q in range(PAIRS):
                        p = cc * PAIRS + q
                        one, two = ssm_buf[q][0:2]
                        pool.wait_ge(ssm_prod, i * n_pairs + (p + 1 + SSM_AHEAD))
                        did(pool.tensor_tensor(one[:, 0:S], one[:, 0:S], two[:, S:2 * S], ALU.add))
                        pool.tensor_tensor(one[:, S:2 * S], one[:, S:2 * S], two[:, 0:S], ALU.subtract).then_inc(ssm_rot, 1)
                        if q == 0:
                            pool.wait_ge(ssm_landed[buf], i * 32 + 16 * (cc // 2 + 1))
                            did(pool.tensor_tensor(t0, c_re, f_re, ALU.mult))
                            did(pool.tensor_tensor(t1, c_im, f_im, ALU.mult))
                            did.wait()
                            did(pool.tensor_tensor(k0, t0, t1, ALU.subtract))
                            did(pool.tensor_tensor(k1, t1, t0, ALU.subtract))
                            did.wait()
                            did(pool.tensor_tensor(t0, c_re, f_neg, ALU.mult))
                            did(pool.tensor_tensor(t1, c_im, f_re, ALU.mult))
                            did.wait()
                            pool.tensor_tensor(k2, t0, t1, ALU.subtract).then_inc(ssm_cmul, 1)
                            pool.wait_ge(ssm_cmul, i * SSM_BODY + (cc + 1))
                        if q == 1:
                            turn = s5[:, S_TURN, bass.ds(i * n_pairs + (cc + 1) * PAIRS, PAIRS)]
                            pool.wait_ge(ssm_trig, i * SSM_BODY + (cc + 1))
                            pool.tensor_tensor(f4, times, turn.unsqueeze(2).broadcast_to([P, PAIRS, S]),
                                               ALU.mult).then_inc(ssm_turns, 1)
                        if q == 2:
                            pool.wait_ge(ssm_whole, i * SSM_BODY + (cc + 2))
                            pool.tensor_tensor(frac_t, frac_t, whole_t[(cc + 1) % 2], ALU.subtract).then_inc(ssm_frac, 1)
                did.leave(SSM_CHUNKS // SSM_BODY)
            pool.wait_ge(*written(SIDE[("cmp_hidden", 1)]))
            pool.memset(v_blocks, 0.0).then_inc(v_zero, 1)



def t_units(w):
    k, n = w.shape
    return w.reshape(k // P, P, n // P, P).transpose(2, 1, 0, 3).reshape(n // P, P, -1)


def n_units(w):
    k, n = w.shape
    return w.reshape(k // (KG * P), KG, P, n // CHUNK, CHUNK).transpose(3, 0, 2, 1, 4).reshape(-1, P, UNIT)


def kernel(**inputs):
    import concourse.bacc as bacc
    from concourse.bass_utils import run_bass_kernel_spmd

    x = {n: np.asarray(a) for n, a in inputs.items()}
    f = np.float32

    w = x["w_in"][0]
    cols, at = {}, 0
    for name, n in (("aq", 1024), ("ak", 1024), ("av", 1024), ("iq", 1024), ("ik", 64), ("iw", 16), ("rq", 1024),
                    ("rk", 1024), ("rv", 2048), ("rg", 2048), ("mq", 1024), ("ga", D), ("gb", D), ("gc", D)):
        cols[name] = w[:, at:at + n]
        at += n
    mem_kv, kv = x["w_mem_kv"][0], x["w_kv_2"]
    qg = x["nsa_w_qg_2"][0]
    s_in = x["ssm_w_in_2"][0]
    ff = x["w_ffn_in"][0]
    mix = [n_units(cols["ga"]).reshape(4, 4, P, UNIT), n_units(x["w_branch_a"][0]).reshape(4, 2, P, UNIT),
           n_units(cols["gb"]).reshape(4, 4, P, UNIT), n_units(x["w_branch_b"][0]).reshape(4, 4, P, UNIT),
           n_units(cols["gc"]).reshape(4, 4, P, UNIT), n_units(x["w_branch_c"][0]).reshape(4, 2, P, UNIT)]
    gate_up = np.stack([t_units(ff[:, :FF_T * P]), t_units(ff[:, FF_T * P:])], 1).reshape(2 * FF_T, P, UNIT)
    kv_cols = kv.reshape(D, 6, NKV * HD)
    cw = x["cmp_w1_2"].reshape(2, 2, CMP_STRIDE, HD, HD).transpose(0, 1, 3, 2, 4).reshape(4, P, UNIT)
    z = qg[:, NQ * HD + 3 * NQ:].reshape(D, 3, NKV, HPG * HD).transpose(0, 2, 1, 3).reshape(D, 3 * NQ * HD)
    mod_w, kvm = x["mod_w_2"], x["kv_mod_w_2"]
    m = [a.reshape(KT, P, D) for a in (mod_w[0][:, D:2 * D], mod_w[0][:, :D], mod_w[0][:, 2 * D:], kvm[:, :D], kvm[:, D:],
                                       mod_w[1][:, :D], mod_w[1][:, D:2 * D], mod_w[1][:, 2 * D:])]
    fo = x["w_ffn_out"][0]
    split = FF_PARTS[0]
    phases = {
        "mk": t_units(mem_kv[:, :1024]), "mv": n_units(mem_kv[:, 1024:]), "mq": t_units(cols["mq"]),
        "ik": t_units(np.concatenate([cols["ik"], cols["ik"]], 1)), "iq": t_units(cols["iq"]), "aq": t_units(cols["aq"]),
        "av": n_units(cols["av"]), "ak": t_units(cols["ak"]), "rq": t_units(cols["rq"]), "rk": t_units(cols["rk"]),
        "rv": n_units(cols["rv"]), "rg": n_units(cols["rg"]), "mix": np.concatenate(mix, 1).reshape(-1, P, UNIT),
        "wo": n_units(x["w_out"][0]), "ff0": gate_up[:2 * split], "ff1": gate_up[2 * split:],
        "fo0": n_units(fo[:split * P]), "fo1": n_units(fo[split * P:]),
        "su": t_units(s_in[:, :D]), "sz": t_units(s_in[:, D:]), "glu": t_units(x["ssm_w_glu_2"][0]),
        "so": n_units(x["ssm_w_out_2"][0]), "kvt": t_units(kv_cols[:, [0, 1, 2, 4]].reshape(D, -1)), "cw": cw,
        "kvn": n_units(kv_cols[:, [3, 5]].reshape(D, -1)), "nq": t_units(qg[:, :NQ * HD]), "nz": n_units(z),
        "no": n_units(x["nsa_w_o_2"][0]),
    }
    stream = np.zeros((STREAM_UNITS, P, UNIT), f)
    for g, (kind, name, u) in enumerate(ORDER):
        stream[g] = phases[name][u] if kind == "unit" else m[name][u]
    mod_b, kvb = x["mod_b_2"], x["kv_mod_b_2"]
    biases = [mod_b[0][D:2 * D], mod_b[0][:D], mod_b[0][2 * D:], kvb[:D], kvb[D:], mod_b[1][:D], mod_b[1][D:2 * D],
              mod_b[1][2 * D:]]

    def on_partitions(v):
        return v.reshape(-1, P).T

    vec_rows = [x["g_pre_mix"][0], x["g_mem"][0], x["g_pre_ffn"][0], x["norm_g_2"][0], x["norm_g_2"][1],
                x["kv_norm_g_2"], x["c_2"][0], x["ssm_b_glu_2"][0], x["ssm_d_2"][0], *biases]

    pos = np.arange(S)
    tok = pos.reshape(TT, P).T
    causal = np.where(pos[None, None] <= tok[:, :, None], 0.0, NEG).astype(f)
    perms = np.zeros((P, 2, P), f)
    freq = np.zeros((P, 2), f)
    for k, d in enumerate((HD, 64)):
        for m in range(P):
            head, r = divmod(m, d)
            perms[head * d + (r + d // 2) % d, k, m] = -1.0 if r < d // 2 else 1.0
        fr = np.power(f(10000.0), (-np.arange(0, d, 2, dtype=f) / f(d)).astype(f)).astype(f)
        freq[:, k] = np.tile(np.concatenate([fr, fr]), P // d)
    log_gamma = np.log1p(-np.exp2(-5.0 - np.arange(N_RET)))
    gap = pos[None, :] - np.arange(P)[:, None]
    decay = np.where(gap[:, None] >= 0, np.exp(np.maximum(gap, 0)[:, None] * log_gamma[None, :, None]), 0.0) * HD ** -0.5
    ends = np.arange(N_CMP) * CMP_STRIDE + CMP_LEN - 1
    keep = (ends[None, None] <= tok[:, :, None])

    cst = np.concatenate([np.eye(P, dtype=f), causal.reshape(P, -1), np.broadcast_to(pos.astype(f), (P, S)),
                          np.concatenate([on_partitions(v) for v in vec_rows], 1), freq], 1)
    w_iw = cols["iw"].reshape(KT, P, N_IDX).transpose(1, 0, 2).reshape(P, -1)
    w_ng = qg[:, NQ * HD:NQ * HD + 3 * NQ].reshape(KT, P, 3 * NQ).transpose(1, 0, 2).reshape(P, -1)
    b1 = np.zeros((P, 2, HD), f)
    b1[0] = x["cmp_b1_2"]
    late = np.concatenate([
        w_ng, x["cmp_w2_2"].transpose(1, 0, 2).reshape(P, -1), b1.reshape(P, -1),
        np.broadcast_to(x["cmp_b2_2"][1], (P, HD)), x["cmp_pe_2"].transpose(2, 0, 1).reshape(P, -1),
        np.where(keep, 0.0, NEG).reshape(P, -1), keep.reshape(P, -1).astype(f), x["cmp_b2_2"][0][:, None]], 1)

    def states(a):
        return a.reshape(-1, P).T
    step = np.repeat(x["ssm_log_step_2"][0][:, None], 64, 1)
    s5_raw = np.stack([states(x["ssm_lam_re_2"][0]), states(x["ssm_lam_im_2"][0]), states(step)], 1)
    bc = np.zeros((SSM_CHUNKS + 1, P, SSM_COLS), f)
    bmat = bc[:SSM_CHUNKS, :, :SSM_B].reshape(SSM_CHUNKS, PAIRS, 2, 16, PAIRS, 2, 2, 64)
    cmat = np.zeros((SSM_CHUNKS, 2, 64, 2, PAIRS, 2, 16), f)
    for part, name in enumerate(("ssm_b_re_2", "ssm_b_im_2")):
        b = x[name][0].reshape(SSM_CHUNKS, PAIRS, 2, 64, 16)
        for q in range(PAIRS):
            for g in range(2):
                bmat[:, q, g, :, q, part, g, :] = b[:, q, g].transpose(0, 2, 1)
    bc[:SSM_CHUNKS, :, :SSM_B] = bmat.reshape(SSM_CHUNKS, P, SSM_B)
    for part, name in enumerate(("ssm_c_re_2", "ssm_c_im_2")):
        c = x[name][0].reshape(SSM_CHUNKS, PAIRS, 2, 16, 64)
        for g in range(2):
            cmat[:, g, :, part, :, g, :] = c[:, :, g].transpose(0, 3, 1, 2)
    bc[:SSM_CHUNKS, :, SSM_B:] = cmat.reshape(SSM_CHUNKS, P, SSM_C)

    arrays = {
        "stream": stream, "x": x["x"][0], "mem": x["mem"][0], "positions": x["positions"], "cst": cst,
        "early": np.concatenate([perms.reshape(P, -1), w_iw], 1), "late": late, "decay": decay.reshape(P, -1),
        "s5_raw": s5_raw, "ssm_bc": bc, "g_post_mix": x["g_post_mix"], "g_post_ffn": x["g_post_ffn"],
        "final_norm_g": x["final_norm_g_2"][None],
    }
    arrays = {n: np.ascontiguousarray(a if a.dtype.kind in "iu" else a.astype(f, copy=False)) for n, a in arrays.items()}
    nc = bacc.Bacc("TRN2", target_bir_lowering=False, num_devices=1)
    A = {n: nc.dram_tensor("in_" + n, a.shape, mybir.dt.from_np(a.dtype), kind="ExternalInput").ap() for n, a in arrays.items()}
    out = nc.dram_tensor("out_0", (S, D), F32, kind="ExternalOutput").ap()
    x_kept = nc.dram_tensor("x_kept", (S, D), F32, kind="Internal").ap()
    program(nc, A, out, x_kept)
    r = run_bass_kernel_spmd(nc, [{"in_" + n: a for n, a in arrays.items()}], core_ids=[0])
    return r.results[0]["out_0"].reshape(1, S, D)
```

```python
from contextlib import ExitStack

import concourse.bass as bass
import numpy as np
from concourse import mybir

F32 = mybir.dt.float32
F32R = mybir.dt.float32r
I32 = mybir.dt.int32
ALU = mybir.AluOpType
ACT = mybir.ActivationFunctionType
AX = mybir.AxisListType.X

P = 128
S = 256
D = 2048
TT = S // P
KT = D // P
EPS = 1e-6
NEG = -1e30
TAKEN = -3e38
N_ATT, N_IDX, N_RET, N_MEM = 8, 16, 8, 4
TOPK = min(256, S // 4)
FF_T = 5632 // P
NQ, NKV, HPG, HD = 16, 4, 4, 128
CMP_STRIDE, CMP_LEN = 16, 32
N_CMP = (S - CMP_LEN) // CMP_STRIDE + 1
ROUND = 1.5 * 2.0 ** 23
TURN = 2 * np.pi
TURN_HI = 6.28125
TURN_LO = float(np.float32(TURN - 6.28125))
PI = 3.1415925
RING, UNIT = 4, 2048
HALF = UNIT // 2
LEAD = 2
CHUNK = 512
KG = 4

FF_PARTS = (24, FF_T - 24)

PIECES = ["s5_scale", "s5_shift", "s5_gate", "kv_shift", "kv_scale", "nsa_shift", "nsa_scale", "nsa_gate"]
MOD_RUNS = [(("mv", "mq", "ik", "iq", "rq", "rk", "rv", "aq", "ak"), (0, 1, 2)), (("fo0",), (5,)), (("fo1",), (6,)),
            (("kvn", "nq"), (7,))]
MIX_PIECE = 3

PHASES = [
    ("mk", 8, 4), ("mv", 8, 4), ("mq", 8, 4), ("ik", 1, 1), ("iq", 8, 4), ("rq", 8, 4), ("rk", 8, 4), ("rv", 16, 8),
    ("aq", 8, 4), ("ak", 8, 4), ("av", 8, 4), ("rg", 16, 8), ("mix", 80, 48), ("wo", 16, 8),
    ("ff0", 2 * FF_PARTS[0], FF_PARTS[0]), ("fo0", FF_PARTS[0], 8), ("ff1", 2 * FF_PARTS[1], FF_PARTS[1]),
    ("fo1", FF_PARTS[1], 8), ("su", 16, 8), ("sz", 16, 32), ("glu", 16, 8), ("so", 16, 8),
    ("kvt", 16, 8), ("cw", 4, 0), ("kvn", 8, 4), ("nq", 16, 8), ("nz", 48, 24), ("no", 16, 8),
]
MIX_LOOPS = 2


def with_mods(units, pieces):
    mods = [("mod", piece, k) for piece in pieces for k in range(KT)]
    out, done = [], 0
    for j, unit in enumerate(units):
        want = j * len(mods) // (len(units) - 1)
        out += [unit, *mods[done:want]]
        done = want
    return out


ORDER, B0, NB = [], {}, {}
BANKS = 0
_run = []
for _name, _units, _banks in PHASES:
    _list = [("unit", _name, _u) for _u in range(_units)]
    _with = [x for x in MOD_RUNS if _name in x[0]]
    if _name == "mix":
        for _i in range(MIX_LOOPS):
            ORDER += with_mods(_list[_units // MIX_LOOPS * _i:][:_units // MIX_LOOPS], [MIX_PIECE + _i])
    elif _with:
        _run += _list
        if _name == _with[0][0][-1]:
            ORDER += with_mods(_run, _with[0][1])
            _run = []
    else:
        ORDER += _list
    B0[_name], NB[_name] = BANKS, _banks
    BANKS += _banks
POS = {x: n for n, x in enumerate(ORDER)}
UNITS = len(ORDER)
STREAM_UNITS = -(-UNITS // RING) * RING
MIX_TURN = POS[("mod", MIX_PIECE + 1, 0)] - POS[("mod", MIX_PIECE, 0)]
MIX_BODY = ORDER[POS[("unit", "mix", 0)]:][:MIX_TURN]


def segment(phase):
    out = []
    for x in ORDER[POS[("unit", phase, 0)]:]:
        if x[0] == "unit" and x[1] != phase:
            break
        out += [x]
    return out


VECS = ["g_pre_mix", "g_mem", "g_pre_ffn", "norm0", "norm1", "kv_norm", "c", "b_glu", "d_skip"] + PIECES
V = {n: i for i, n in enumerate(VECS)}

SSM_CHUNKS, PAIRS = D // P, 4
SSM_BODY = 4
SSM_B, SSM_C = PAIRS * 2 * P, 2 * P
SSM_COLS = SSM_B + SSM_C


CONSTS_MADE = 6
LATE = 1533
SSM_AHEAD = 4
SSM_GELU0 = 1
TURN_F = 6.283185
MIX_GATES = (4, 10, 18, 24, 30, 38)
MIX_ENDS = (6, 14, 20, 26, 34, 40)
CMP_PAD = 32
RETV = 256
S5_PAIRS = (SSM_CHUNKS + 2) * PAIRS
EARLY, CST = 2560, 898 + len(VECS) * KT
ARENA = 48, 64
O_ADDS = NKV * TT + 2 * NQ


def heads_in_turn(name, n, first=0):
    out = []
    for h in range(n + 2):
        out += [(name + "_logits", first + h)] * (h < n)
        out += [(name + "_turn", first + h - 1)] * (1 <= h <= n)
        out += [(name + "_values", first + h - 2)] * (h >= 2)
    return out


def spread(phase, tasks=()):
    out, done = [], 0
    units = segment(phase)
    n = sum(x[0] == "unit" for x in units)
    for step in units:
        out += [step]
        if step[0] == "unit":
            want = -(-len(tasks) * (step[2] + 1) // n)
            out += tasks[done:want]
            done = want
        elif step[2] == KT - 1:
            out += [("mod_turn", step[1], c) for c in range(4)]
    return out


def with_ropes(steps):
    out, due = [], []
    for s in steps:
        out += [s]
        if s[0] == "unit":
            out += due
            due = [("rope", s[1], s[2] // 2)] if s[2] % 2 or s[1] == "ik" else []
    return out + due


def mixer_steps():
    att = heads_in_turn("att", N_ATT)
    ret = [x for h in range(N_RET + 1) for x in [("ret_scores", h)] * (h < N_RET) + [("ret_values", h - 1)] * (h > 0)]
    idx = [("idx_w", 0), ("idx_w_back", 0)] + [("idx", h) for h in range(N_IDX)]
    topk = [("topk", t, r) for t in range(TT) for r in range(TOPK // 16)] + [("topk_end",)]
    s = [("norm", "mem", j) for j in range(KT // 2)] + [("rms", "x")]
    s += spread("mk", [("norm", "x", j) for j in range(KT // 2)] + [("angles",)])
    s += spread("mv", [("s5_params", part) for part in range(5)]) + spread("mq")
    s += with_ropes(spread("ik") + spread("iq", heads_in_turn("mem", N_MEM)))
    s += with_ropes(spread("rq", idx[:9])) + with_ropes(spread("rk", idx[9:])) + spread("rv", topk)
    s += with_ropes(spread("aq", ret[:6])) + with_ropes(spread("ak", ret[6:12])) + spread("av", ret[12:])
    return s + spread("rg", att) + [("turn_y", j) for j in range(KT // 2)]


def nsa_steps():
    s = [("norm", "x3", j) for j in range(KT // 2)] + spread("kvt")
    s += [("cmp_hidden", 0), ("cmp_hidden", 1)] + spread("kvn", [("cmp_out", 0), ("cmp_out", 1)])
    s += spread("nq", [("ngate", 0), ("ngate_back", 0)])
    behind = {}

    def put(u, place, task):
        behind.setdefault(u, []).append((place, task))

    for c in range(3 * NKV):
        g, br = divmod(c, 3)
        u = 4 * c + 1
        if br == 0:
            put(u, 2, ("cmp_logits", g))
            put(u + 1, 1, ("cmp_turn", g))
            for t in range(TT):
                put(u + 3, 0, ("cmp_values", g, t))
            continue
        for j in range(HPG):
            name, h = ("cmp", "sel", "win")[br], HPG * g + j
            put(u + j, 2, (name + "_logits", h))
            put(u + j + 1, 1, (name + "_turn", h))
            put(u + j + 3, 0, (name + "_values", h))

    def tasks(u):
        return [task for _, task in sorted(behind.pop(u, []), key=lambda x: x[0])]

    for step in spread("nz"):
        s += [step]
        if step[0] == "unit":
            s += tasks(step[2])
    for u in sorted(behind):
        s += tasks(u)
    return s + [("turn_o", j) for j in range(KT // 2)]


MIXER, NSA = mixer_steps(), nsa_steps()
MIX_TURNS = [("mod_turn", MIX_PIECE, c) for c in range(4)]
AFTER_MIX = [("turn_mix", j) for j in range(KT // 2)]
OUT = spread("wo")
BEFORE_FFN = [("norm", "x1", j) for j in range(KT // 2)]
FFN_OUT = [spread("fo0"), spread("fo1")]
BEFORE_S5 = [("norm", "x2", j) for j in range(KT // 2)] + spread("su")
def with_gate(phase, tag):
    out = []
    for step in spread(phase):
        out += [step]
        if step[0] == "unit" and step[2] < 3:
            out += [("gate", tag, j) for j in range(D // CHUNK) if min(j, 2) == step[2]]
    return out


S5_GLU, S5_OUT, NSA_OUT = spread("glu"), with_gate("so", "s5"), with_gate("no", "nsa")

LOCAL = ("unit", "mod", "rms", "angles", "s5_params", "topk", "topk_end")
SIDE = {}
_n = 0
for _steps in (MIXER, "mix", AFTER_MIX, OUT, BEFORE_FFN, *FFN_OUT, BEFORE_S5, "s5", S5_GLU, S5_OUT, NSA, NSA_OUT):
    if _steps == "s5":
        SSM_SIDE0 = _n
        _n += (SSM_CHUNKS + 1) * PAIRS
        continue
    if _steps == "mix":
        SIDE.update({_s: _n + _k for _k, _s in enumerate(MIX_TURNS)})
        _n += MIX_LOOPS * len(MIX_TURNS)
        continue
    for _s in _steps:
        if _s[0] not in LOCAL:
            SIDE[_s] = _n
            _n += 1
GATES = {s: n for n, s in enumerate(x for x in S5_OUT + NSA_OUT if x[0] == "gate")}
ROPE = {s: n for n, s in enumerate(x for x in MIXER if x[0] == "rope")}
_attn = [x for x in MIXER + NSA if x[0].endswith("_logits")]
TURNS = [(x[0][:3] + "_turn", x[1]) for x in _attn]
VALUES = [(x[0][:3] + "_values", x[1]) + ((1,) if x[0][:3] == "cmp" else ()) for x in _attn]
MASKED = {n: n - N_MEM for n in range(len(_attn))}
O_INDEX = {s: n for n, s in enumerate(x for x in NSA if x[0] in ("cmp_values", "sel_values", "win_values"))}
O_AFTER = [sum(1 for s in O_INDEX if (3 * s[1] if s[0] == "cmp_values" else 3 * (s[1] // HPG) + (1 if s[0][:3] == "sel" else 2)) <= c)
           for c in range(3 * NKV)]
HEADS = {s[:2]: n for n, s in enumerate(x for x in MIXER + NSA if x[0].endswith("_logits"))}
ROUNDED = {s: n for n, s in enumerate(
    x for x in MIXER + AFTER_MIX + BEFORE_FFN + BEFORE_S5 + NSA
    if x[0] in ("norm", "mem_values", "att_values", "turn_y", "turn_mix", "turn_o"))}
NORMS = {"mem": 0, "x": 1, "x1": 2, "x2": 3, "x3": 4, "out": 5}
NORM_PARTS = {"mem": 1, "x": 1, "x1": 2, "x2": 2, "x3": 4, "out": 4}
SQUARES = {n: 2 * sum(list(NORM_PARTS.values())[:k + 1]) for n, k in NORMS.items()}
RES_ADDED = {n: SQUARES[n] - SQUARES["x"] for n in ("x1", "x2", "x3", "out")}


HI = []
for _x in ORDER:
    HI.append((HI[-1] if HI else 0) + (_x[0] == "unit" and _x[1] != "cw"))
RUN = {}
for _g, _x in enumerate(ORDER):
    if _x[0] == "unit":
        _last = _x
    RUN[_last] = RUN.get(_last, 0) + 1


class Steps:

    def __init__(self, eng, sem):
        self.eng, self.sem, self.n, self.i, self.stride = eng, sem, 0, None, 0

    def __call__(self, ins):
        ins.then_inc(self.sem, 1)
        self.n += 1

    def wait(self):
        self.eng.wait_ge(self.sem, self.n if self.i is None else self.i * self.stride + self.n)

    def enter(self, i, stride):
        self.i, self.stride, self.n0 = i, stride, self.n

    def leave(self, count):
        assert self.n - self.n0 == self.stride, (self.n - self.n0, self.stride)
        self.n, self.i = self.n0 + self.stride * count, None


def program(nc, A, out, x_kept):
    with ExitStack() as ctx:
        def sb(name, shape):
            return ctx.enter_context(nc.sbuf_tensor(name, shape, F32))

        def sem(name):
            return ctx.enter_context(nc.semaphore(name))

        fast = {}

        def two_types(name, shape):
            with nc.sbuf_tensor(name, shape, F32) as whole:
                pass
            fast[name] = ctx.enter_context(nc.sbuf_tensor(name + "_parts", shape, F32R))
            return whole

        def r32(ap):
            return bass.AP(tensor=fast[ap.tensor.name][:].tensor, offset=ap.offset, ap=ap.ap)

        def as32(ap):
            return r32(ap).bitcast(F32)

        ring = two_types("ring", [P, RING, UNIT])
        hi = two_types("hi", [P, RING, UNIT])
        arena = [two_types("arena_low", [P, ARENA[0] * 256]), two_types("arena_high", [P, ARENA[1] * 256])]
        work = sb("work", [P, 7, CHUNK])
        early = sb("early", [P, EARLY])
        perms = early[:, 0:2 * P].rearrange("p (k m) -> p k m", k=2)
        w_iw = early[:, 256:512].rearrange("p (k n) -> p k n", k=KT)
        ropes = early[:, 512:1536].rearrange("p (k t) -> p k t", k=4)
        selbias = early[:, 1536:2048].rearrange("p (t s) -> p t s", t=TT)
        ikT = early[:, 2048:2560].rearrange("p (h s) -> p h s", h=2)
        w_ng = early[:, 0:768].rearrange("p (k n) -> p k n", k=KT)
        cmp_w2 = early[:, 768:1024].rearrange("p (j n) -> p j n", j=2)
        b1_rows = early[:, 1024:1280].rearrange("p (j n) -> p j n", j=2)
        b2_row = early[:, 1280:1408]
        cmp_pe = early[:, 1408:1472].rearrange("p (j l) -> p j l", j=2)
        cmp_add = early[:, 1472:1502].rearrange("p (t n) -> p t n", t=TT)
        cmp_keep = early[:, 1502:1532].rearrange("p (t n) -> p t n", t=TT)
        b2_col = early[:, 1532:1533]
        hid = early[:, 1536:1656].rearrange("p (j n) -> p j n", j=2)
        kcT = early[:, 1656:1716]
        gates = early[:, 1720:1816].rearrange("p (t n) -> p t n", t=TT)
        v_tmp = early[:, 2048:2560].rearrange("p (g n) -> p g n", g=NKV)
        cst = sb("cst", [P, CST])
        ident = cst[:, 0:128]
        causal = cst[:, 128:640].rearrange("p (t s) -> p t s", t=TT)
        time_row = cst[:, 640:896]
        vecs = cst[:, 896:896 + len(VECS) * KT].rearrange("p (v c) -> p v c", c=KT)
        freq = cst[:, CST - 2:CST]
        ones = sb("ones", [P, P])
        modv = sb("modv", [P, len(PIECES), KT])
        gains = sb("gains", [P, 3, KT])
        c_act = sb("c_act", [P, KT])
        iw = sb("iw", [P, TT, N_IDX])
        stat = sb("stat", [P, 64])
        bn = sb("bn", [P, TT, 6])
        s5 = sb("s5", [P, 5, S5_PAIRS])
        biases = sb("biases", [P, 3])
        half_pi, round_up, round_back = biases[:, 0:1], biases[:, 1:2], biases[:, 2:3]
        bn_all = sb("bn_all", [P, TT * N_RET, 2])
        psum = ctx.enter_context(nc.psum_tensor("psum", [P, 8, CHUNK], F32))

        def area(kb, n):
            piece, at = (0, kb) if kb < ARENA[0] else (1, kb - ARENA[0])
            return arena[piece][:, at * 256:at * 256 + n]

        def tokens(kb, n=D):
            return area(kb, TT * n).rearrange("p (t n) -> p t n", t=TT)

        def feats(kb, n=KT):
            return area(kb, n * S).rearrange("p (c t) -> p c t", c=n)

        def pair(kb_hi, kb_lo, n=KT):
            return feats(kb_hi, n), feats(kb_lo, n)

        hT, memT, mem_in, x_in = pair(0, 16), pair(32, 48), tokens(64), tokens(80)
        mkT, mv, mqT, o_cT = feats(64, 8), tokens(72, 1024), feats(80, 8), pair(96, 104, 8)
        iqT, score, top = feats(32, 8), tokens(40, S), tokens(42, S)
        rqT, rkT, rv = feats(48, 8), feats(56, 8), tokens(64)
        decay = area(80, N_RET * S).rearrange("p (h t) -> p h t", h=N_RET)
        aqT, akT, av, o_aT = feats(32, 8), feats(40, 8), tokens(88, 1024), pair(48, 56, 8)
        o_bT, mixed, mixT = pair(32, 80), tokens(64), pair(0, 16)
        xr, y, xn, h2T = tokens(32), tokens(96), tokens(80), pair(0, 16)
        actT = pair(48, 48 + FF_PARTS[0], FF_PARTS[0])
        h3T, uT, zT = pair(0, 16), feats(48), pair(0, 64)
        uT_on = feats(48, SSM_CHUNKS + 1)
        cos_t, sin_t = [area(32, 1024), area(36, 1024)], [area(40, 1024), area(44, 1024)]
        ssm_in = area(96, 2 * SSM_COLS).rearrange("p (b n) -> p b n", b=2)
        ssm_c = area(106, 2 * 3 * P).rearrange("p (b k q c) -> p b k q c", b=2, k=3, q=PAIRS)
        ssm_tmp = area(109, 2 * P)
        yT = pair(80, 96)
        hkvT, hnT, cin = pair(0, 16), pair(64, 48), area(64, 4 * NKV * S).rearrange(
            "p (j h g t) -> p j h g t", j=2, h=2, g=NKV)
        ksT, kwT, vs, vw = feats(96, NKV), feats(100, NKV), tokens(104, 512), tokens(108, 512)
        qT, o_tok, oT = feats(0), tokens(16), pair(64, 48)
        zs = area(80, 2 * TT * CHUNK).rearrange("p (b t n) -> p b t n", b=2, t=TT)
        v_blocks = area(88, NKV * CHUNK).rearrange("p (g n) -> p g n", g=NKV)
        final_row, y_out = area(0, D), tokens(16)

        def halves(i):
            return work[:, i, :].rearrange("p (t s) -> p t s", t=2)

        prob, probT = (0, 1), (2, 3)
        TMP = (4, 5, 6)

        def halves_of(ap):
            return ap.rearrange("p (t s) -> p t s", t=2)

        def both(x, j):
            return x[:, 2 * j:2 * j + 2, :].rearrange("p c t -> p (c t)")

        row, nsa_row, frac_t, abs_t = early[:, 0:D], area(80, D), early[:, 0:1024], early[:, 1024:2048]

        def sums_of(piece):
            if piece < MIX_PIECE:
                return area(88, D)
            return early[:, 0:D] if piece < MIX_PIECE + MIX_LOOPS else work[:, 0:4, :].rearrange("p b n -> p (b n)")


        pos_i = area(96, S).bitcast(I32)
        rope_pos, rope_ang, rope_k, rope_abs = area(97, S), [area(98, S), area(99, S)], area(100, S), area(101, S)
        s5_raw = area(102, 3 * 64).rearrange("p (k n) -> p k n", k=3)
        s5_dt, s5_thr, s5_sin, s5_sin2 = (area(103, 256)[:, 64 * k:64 * k + 64] for k in range(4))
        s5_tmp = [area(104, 320)[:, 64 * k:64 * k + 64] for k in range(5)]
        ret_stat = bn_all[:, :, :]
        ssm_bufs = [area(80 + 2 * k, 2 * S) for k in range(8)] + [work[:, k, :] for k in range(4)]
        ssm_buf = [ssm_bufs[3 * q:3 * q + 3] for q in range(PAIRS)]
        whole_t = cos_t

        def stream_bank(b):
            return psum[:, b % 4, :]

        def side_bank(n):
            return psum[:, 4 + n % 4, :]

        landed = [sem(f"ring_half{s}_landed") for s in range(2 * RING)]
        units_done = sem("units_done")
        hi_made = sem("hi_made")
        cut_done = sem("cut_done")
        rounded = sem("rounded")
        evacuated = [sem(f"stream_bank{b}_evacuated") for b in range(4)]
        side_done = sem("side_done")
        side_read = [sem(f"side_bank{b}_read") for b in range(4)]
        consts_landed, x_landed = sem("consts_landed"), sem("x_landed")
        mem_landed = [sem(f"mem_tile{t}_landed") for t in range(TT)]
        decay_landed, rows_landed = sem("decay_landed"), sem("rows_landed")
        norm_squares, norm_mean, norm_root, norm_scaled = (sem("norm_" + n) for n in ("squares", "mean", "root", "scaled"))
        roped, idx_added = sem("roped"), sem("idx_added")
        head_max, head_exp, head_prob = sem("head_max"), sem("head_exp"), sem("head_prob")
        ret_var, ret_root, ret_gated = sem("ret_var"), sem("ret_root"), sem("ret_gated")
        mix_done = sem("mix_done")
        res_mean, res_root, res_added = sem("res_mean"), sem("res_root"), sem("res_added")
        act_ready, trig_done, s5_ready = sem("c_act_ready"), sem("trig_done"), sem("s5_ready")
        act_steps, dve_steps, pool_steps = sem("act_steps"), sem("dve_steps"), sem("pool_steps")
        ang_ready, rope_ready = sem("ang_ready"), sem("rope_ready")
        diag_ready, mod_gain = sem("diag_ready"), sem("mod_gain")
        ssm_landed = [sem(f"ssm_in{b}_landed") for b in range(2)]
        ssm_cmul, ssm_turns, ssm_whole, ssm_frac, ssm_trig = (
            sem("ssm_" + n) for n in ("cmul", "turns", "whole", "frac", "trig"))
        ssm_prod, ssm_rot, ssm_state, ssm_back, ssm_y = (
            sem("ssm_" + n) for n in ("prod", "rot", "state", "back", "y"))
        cmp_vblock, v_zero, o_added = sem("cmp_vblock"), sem("v_zero"), sem("o_added")
        out_ready, out_stored = sem("out_ready"), sem("out_stored")
        late_landed, y_hi, y_cut, hn_hi, hn_cut = (sem(n) for n in ("late_landed", "y_hi", "y_cut", "hn_hi", "hn_cut"))
        x_stored = sem("x_stored")
        act_hi, act_cut = sem("ffn_hi"), sem("ffn_cut")
        s5_raw_landed, x_again_landed, final_row_landed = sem("s5_raw_landed"), sem("x_again_landed"), sem("final_row_landed")
        consts_made, ff_gate, res_squares = sem("consts_made"), sem("ff_gate"), sem("res_squares")
        glu_gate, sel_ready = sem("glu_gate"), sem("sel_ready")
        pos_landed, s5_params, mix_part, ssm_gelu = sem("pos_landed"), sem("s5_params"), sem("mix_part"), sem("ssm_gelu")
        p_cmp = work[:, TMP[0], 0:2 * P]
        few = {"idx_w": work[:, probT[0], 0:S], "ngate": work[:, TMP[2], 0:S]}
        def written(n):
            return side_done, n + 1

        def read(n):
            return side_read[n % 4], n // 4 + 1

        def multiplied(phase, u):
            return units_done, 2 * POS[("unit", phase, u)] + 2

        def visited(step):
            if step[0] == "cmp_hidden":
                return [("unit", "cw", 2 * step[1] + half) for half in range(2)]
            return [step] if step[0] in ("unit", "mod") else []

        def emptied(b):
            return evacuated[b % 4], b // 4 + 1

        def last_banks(phase):
            return [emptied(B0[phase] + NB[phase] - 1 - i) for i in range(min(4, NB[phase]))]

        def last_reads(uses):
            return [read(n) for n in uses[-4:]]

        NORM_TO = {"mem": (memT, vecs[:, V["g_mem"], :], None), "x": (hT, vecs[:, V["g_pre_mix"], :], None),
                   "x1": (h2T, vecs[:, V["g_pre_ffn"], :], None),
                   "x2": (h3T, gains[:, 0, :], modv[:, PIECES.index("s5_shift"), :]),
                   "x3": (hkvT, gains[:, 1, :], modv[:, PIECES.index("kv_shift"), :])}
        S_MAG, S_TURN, S_KRE, S_KIM, S_NKIM = 0, 1, 2, 3, 4

        block = ctx.enter_context(nc.Block())

        @block.sync
        def _(sp):
            for t in range(TT):
                sp.wait_ge(mem_landed[t], 16)
            halves_of_ring = ring[:].rearrange("p s (h n) -> p (s h) n", h=2)
            for s in range(2 * RING):
                sp.dma_start(halves_of_ring[:, s, :], A["stream"][s]).then_inc(landed[s], 16)
            with sp.Fori(1, STREAM_UNITS // RING) as turn:
                for s in range(2 * RING):
                    sp.wait_ge(units_done, turn * (2 * RING) + (s + 1 - 2 * RING))
                    sp.wait_ge(cut_done, turn * (2 * RING) + (s + 1 - 2 * RING))
                    sp.dma_start(halves_of_ring[:, s, :], A["stream"][bass.ds(turn * (2 * RING) + s, 1)]
                                 .rearrange("a p n -> p (a n)")).then_inc(landed[s], 16)
            for k in range(2 * TT):
                sp.wait_ge(out_ready, k + 1)
                t, cols = k // 2, slice(k % 2 * (D // 2), (k % 2 + 1) * (D // 2))
                sp.dma_start(out[t * P:(t + 1) * P, cols], y_out[:, t, cols]).then_inc(out_stored, 16)
            sp.wait_ge(out_stored, 16 * 2 * TT)

        @block.tensor
        def _(pe):
            def cut_half(phase, u, h, i=None, per=0):
                g = POS[("unit", phase, u)]
                value = 2 * g + h + 1
                pe.wait_ge(cut_done, value if i is None else i * (2 * per) + value)
                return g % RING

            def release(mm, phase, u, h):
                mm.then_inc(units_done, 1 if h == 0 else 2 * RUN[("unit", phase, u)] - 1)

            def free_bank(b, i=None, uses=0):
                if b >= 4:
                    pe.wait_ge(evacuated[b % 4], b // 4 if i is None else i * uses + b // 4)
                return stream_bank(b)

            def free_side(n):
                if n >= 4:
                    pe.wait_ge(*read(n - 4))
                return side_bank(n)

            def from_side(name, k, *tag):
                return [] if k % 2 else [read(SIDE[(name, *tag, k // 2)])]

            operand = {"mk": lambda k: from_side("norm", k, "mem"), "mq": lambda k: from_side("norm", k, "x"),
                       "ff0": lambda k: from_side("norm", k, "x1"), "su": lambda k: from_side("norm", k, "x2"),
                       "kvt": lambda k: from_side("norm", k, "x3"), "wo": lambda k: from_side("turn_mix", k),
                       "no": lambda k: from_side("turn_o", k), "fo0": lambda k: [(act_cut, k + 1)],
                       "fo1": lambda k: [(act_cut, FF_PARTS[0] + k + 1)],
                       "glu": lambda k: [] if k % 4 else [(y_cut, k // 4 + 1)],
                       "nq": lambda k: [] if k % 4 else [(hn_cut, k // 4 + 1)],
                       "so": lambda k: [] if k % 2 else [emptied(B0["glu"] + k // 2)]}

            def t_unit(phase, u, x, i=None, per=0, uses=0, own_bank=None):
                b, half = (B0[phase] + u // 2, (u % 2) * S) if own_bank is None else (own_bank, 0)
                for h in range(2):
                    slot = cut_half(phase, u, h, i, per)
                    if h == 0:
                        bank = free_bank(b, i, uses) if half == 0 else stream_bank(b)
                    for k in range(h * KT // 2, (h + 1) * KT // 2):
                        for w in operand[phase](k) if u == 0 and phase in operand else []:
                            pe.wait_ge(*w)
                        cols = slice(k * P, (k + 1) * P)
                        for n, (w, part) in enumerate(((hi, 0), (hi, 1), (ring, 0))):
                            mm = pe.matmul(bank[:, half:half + S], r32(w[:, slot, cols]), r32(x[part][:, k, :]),
                                           start=(k == 0 and n == 0), stop=(k == KT - 1 and n == 2))
                    release(mm, phase, u, h)

            def n_unit(phase, u, x, kg, groups, b, i=None, per=0, uses=0):
                if kg == 0:
                    free_bank(b, i, uses)
                    free_bank(b + 1, i, uses)
                for h in range(2):
                    slot = cut_half(phase, u, h, i, per)
                    for kk in range(h * KG // 2, (h + 1) * KG // 2):
                        for w in operand[phase](kg * KG + kk) if u == kg and phase in operand else []:
                            pe.wait_ge(*w)
                        cols = slice(kk * CHUNK, (kk + 1) * CHUNK)
                        for t in range(TT):
                            for n, (part, w) in enumerate(((0, hi), (0, ring), (1, hi))):
                                mm = pe.matmul(stream_bank(b + t), r32(x[part][:, kg * KG + kk, t * P:(t + 1) * P]),
                                               r32(w[:, slot, cols]), start=(kg == 0 and kk == 0 and n == 0),
                                               stop=(kg == groups - 1 and kk == KG - 1 and n == 2))
                    release(mm, phase, u, h)

            def turn_tokens(src, j, n):
                bank = free_side(n)
                for c in range(2):
                    for t in range(TT):
                        mm = pe.transpose(bank[:, c * S + t * P:c * S + (t + 1) * P],
                                          src[:, t, (2 * j + c) * P:(2 * j + c + 1) * P], ident[:, :])
                mm.then_inc(side_done, 1)

            T_RHS = {"mk": memT, "mq": hT, "ik": hT, "iq": hT, "aq": hT, "ak": hT, "rq": hT, "rk": hT,
                     "su": h3T, "sz": h3T, "glu": yT, "kvt": hkvT, "nq": hnT}
            N_LHS = {"mv": memT, "av": hT, "rv": hT, "rg": hT, "wo": mixT, "fo0": actT, "fo1": actT, "so": zT,
                     "kvn": hkvT, "nz": hnT, "no": oT}

            def mod_turn(piece, c, n, i=None):
                if i is None:
                    bank = free_side(n)
                else:
                    pe.wait_ge(side_read[n % 4], i + n // 4)
                    bank = side_bank(n)
                last = 2 * POS[("mod", piece, KT - 1)] + 2
                pe.wait_ge(cut_done, last if i is None else i * (2 * MIX_TURN) + last)
                for k in range(4):
                    at = c * CHUNK + k * P
                    mm = pe.matmul(bank[:, k:k + 1], sums_of(piece)[:, at:at + P], ones[:, 0:1], start=True, stop=True)
                mm.then_inc(side_done, 1)

            def plain_unit(phase, u):
                if phase in T_RHS:
                    t_unit(phase, u, T_RHS[phase])
                else:
                    groups = {"fo0": FF_PARTS[0] // KG, "fo1": FF_PARTS[1] // KG}.get(phase, 4)
                    n_unit(phase, u, N_LHS[phase], u % groups, groups, B0[phase] + u // groups * 2)

            def logits(n, q, k, h, hk):
                bank = free_side(n)
                for t in range(TT):
                    mm = pe.matmul(bank[:, t * S:(t + 1) * S], q[:, h, t * P:(t + 1) * P], k[:, hk, :],
                                   start=True, stop=True)
                mm.then_inc(side_done, 1)

            def turn_probs(n, a):
                bank = free_side(n)
                pe.wait_ge(head_prob, a + 1)
                for blk in range(2):
                    for t in range(TT):
                        mm = pe.transpose(bank[:, blk * S + t * P:blk * S + (t + 1) * P],
                                          halves(prob[a % 2])[:, t, blk * P:(blk + 1) * P], ident[:, :])
                mm.then_inc(side_done, 1)

            def side(step):
                kind, n = step[0], SIDE[step]
                if kind == "norm":
                    tag, j = step[1:]
                    if j % 2 == 0:
                        pe.wait_ge(norm_scaled, TT * (4 * NORMS[tag] + j // 2 + 1))
                    turn_tokens({"mem": mem_in, "x": x_in}.get(tag, xn), j, n)
                elif kind == "mod_turn":
                    mod_turn(step[1], step[2], n)
                elif kind == "rope":
                    r = ROPE[step]
                    bank = free_side(n)
                    pe.wait_ge(*emptied(B0[step[1]] + step[2]))
                    width = S if step[1] == "ik" else 2 * S
                    pe.matmul(bank[:, 0:width], perms[:, 1 if step[1] in ("ik", "iq") else 0, :],
                              work[:, TMP[r % 2], 0:width], start=True, stop=True).then_inc(side_done, 1)
                elif kind in ("idx_w", "ngate"):
                    src, w, m = (hT, w_iw, N_IDX) if kind == "idx_w" else (hnT, w_ng, 3 * NQ)
                    bank = free_side(n)
                    for k in range(KT):
                        for part in range(2):
                            mm = pe.matmul(bank[0:m, 0:S], w[:, k, :], as32(src[part][:, k, :]),
                                           start=(k == 0 and part == 0), stop=(k == KT - 1 and part == 1))
                    mm.then_inc(side_done, 1)
                elif kind in ("idx_w_back", "ngate_back"):
                    m = N_IDX if kind == "idx_w_back" else 3 * NQ
                    bank = free_side(n)
                    pe.wait_ge(*read(SIDE[(kind[:5], 0)]))
                    for t in range(TT):
                        mm = pe.transpose(bank[:, t * m:(t + 1) * m], few[kind[:5]][0:m, t * P:(t + 1) * P], ident[0:m, 0:m])
                    mm.then_inc(side_done, 1)
                elif kind == "idx":
                    h = step[1]
                    if h == 0:
                        pe.wait_ge(roped, ROPE[("rope", "iq", 3)] + 1)
                    logits(n, iqT, ikT, h // 2, h % 2)
                elif kind == "mem_logits":
                    h = step[1]
                    bank = free_side(n)
                    if h == 0:
                        for w in last_banks("mk") + last_banks("mq"):
                            pe.wait_ge(*w)
                    for t in range(TT):
                        for kk in range(2):
                            mm = pe.matmul(bank[:, t * S:(t + 1) * S], mqT[:, 2 * h + kk, t * P:(t + 1) * P],
                                           mkT[:, 2 * h + kk, :], start=(kk == 0), stop=(kk == 1))
                    mm.then_inc(side_done, 1)
                elif kind == "att_logits":
                    if step[1] == 0:
                        pe.wait_ge(roped, ROPE[("rope", "ak", 3)] + 1)
                    logits(n, aqT, akT, step[1], step[1])
                elif kind in ("sel_logits", "win_logits"):
                    logits(n, qT, ksT if kind == "sel_logits" else kwT, step[1], step[1] // HPG)
                elif kind.endswith("_turn") and kind != "cmp_turn":
                    turn_probs(n, HEADS[(kind[:3] + "_logits", step[1])])
                elif kind == "mem_values":
                    h = step[1]
                    a = HEADS[("mem_logits", h)]
                    bank = free_side(n)
                    pe.wait_ge(*read(SIDE[("mem_turn", h)]))
                    if h == 0:
                        for w in last_banks("mv"):
                            pe.wait_ge(*w)
                    for e in range(2):
                        for blk in range(2):
                            at = (2 * h + e) * P
                            mm = pe.matmul(bank[:, e * S:(e + 1) * S], mv[:, blk, at:at + P],
                                           halves(probT[a % 2])[:, blk, :], start=(blk == 0), stop=(blk == 1))
                    mm.then_inc(side_done, 1)
                elif kind == "att_values":
                    h = step[1]
                    a = HEADS[("att_logits", h)]
                    bank = free_side(n)
                    pe.wait_ge(*read(SIDE[("att_turn", h)]))
                    if h == 0:
                        for w in last_banks("av"):
                            pe.wait_ge(*w)
                    for blk in range(2):
                        mm = pe.matmul(bank[:, 0:S], av[:, blk, h * P:(h + 1) * P], halves(probT[a % 2])[:, blk, :],
                                       start=(blk == 0), stop=(blk == 1))
                    mm.then_inc(side_done, 1)
                elif kind in ("sel_values", "win_values"):
                    h = step[1]
                    a = HEADS[(kind[:3] + "_logits", h)]
                    v, g = (vs if kind == "sel_values" else vw), h // HPG
                    bank = free_side(n)
                    pe.wait_ge(*read(SIDE[(kind[:3] + "_turn", h)]))
                    for t in range(TT):
                        for blk in range(2):
                            mm = pe.matmul(bank[:, t * P:(t + 1) * P], halves(probT[a % 2])[:, blk, t * P:(t + 1) * P],
                                           v[:, blk, g * P:(g + 1) * P], start=(blk == 0), stop=(blk == 1))
                    mm.then_inc(side_done, 1)
                elif kind == "ret_scores":
                    h = step[1]
                    bank = free_side(n)
                    if h == 0:
                        pe.wait_ge(roped, ROPE[("rope", "rk", 3)] + 1)
                    pe.matmul(bank[:, 0:S], rkT[:, h, 0:P], rqT[:, h, :], start=True, stop=True)
                    pe.matmul(bank[:, S:S + P], rkT[:, h, P:S], rqT[:, h, P:S], start=True,
                              stop=True).then_inc(side_done, 1)
                elif kind == "ret_values":
                    h = step[1]
                    bank = free_side(n)
                    pe.wait_ge(*read(SIDE[("ret_scores", h)]))
                    if h == 0:
                        for w in last_banks("rv"):
                            pe.wait_ge(*w)
                    sd, at = work[:, prob[h % 2], :], h * RETV
                    pe.matmul(bank[:, 0:RETV], sd[:, 0:P], rv[:, 0, at:at + RETV], start=True, stop=True)
                    pe.matmul(bank[:, RETV:2 * RETV], sd[:, P:S], rv[:, 0, at:at + RETV], start=True, stop=False)
                    pe.matmul(bank[:, RETV:2 * RETV], sd[:, S:S + P], rv[:, 1, at:at + RETV], start=False,
                              stop=True).then_inc(side_done, 1)
                elif kind in ("turn_y", "turn_mix", "turn_o"):
                    src, done, value = {"turn_y": (rv, ret_gated, 8), "turn_mix": (mixed, mix_done, 1),
                                        "turn_o": (o_tok, o_added, O_ADDS)}[kind]
                    if step[1] == 0:
                        pe.wait_ge(done, value)
                    turn_tokens(src, step[1], n)
                elif kind == "gate":
                    tag, j = step[1:]
                    bank = free_side(n)
                    pe.wait_ge(diag_ready, GATES[step] + 1)
                    for c in range(4):
                        mm = pe.matmul(bank[:, c * P:(c + 1) * P], ones[:, :], work[:, TMP[j % 2], c * P:(c + 1) * P],
                                       start=True, stop=True)
                    mm.then_inc(side_done, 1)
                elif kind == "cmp_hidden":
                    j = step[1]
                    bank = free_side(n)
                    for b in range(2):
                        pe.wait_ge(*emptied(B0["kvt"] + 2 * j + b))
                    for half in range(2):
                        g = POS[("unit", "cw", 2 * j + half)]
                        for h in range(2):
                            pe.wait_ge(landed[(2 * g + h) % (2 * RING)], 16 * (g // RING + 1))
                        slot = g % RING
                        for r in range(CMP_STRIDE):
                            blocks = cin[:, j, half, :, :].rearrange("p g (n r) -> p g n r", r=CMP_STRIDE)
                            mm = pe.matmul(bank[:, 0:NKV * N_CMP], ring[:, slot, r * P:(r + 1) * P],
                                           blocks[:, :, half:half + N_CMP, r], start=(half == 0 and r == 0), stop=False)
                        mm.then_inc(units_done, 2 * RUN[("unit", "cw", 2 * j + half)])
                    pe.matmul(bank[:, 0:NKV * N_CMP], b1_rows[0:1, j, :], ones[0:1, 0:NKV * N_CMP], start=False,
                              stop=True).then_inc(side_done, 1)
                elif kind == "cmp_out":
                    j = step[1]
                    bank = free_side(n)
                    pe.wait_ge(*read(SIDE[("cmp_hidden", j)]))
                    if j == 0:
                        mm = pe.matmul(bank[:, 0:NKV * N_CMP], cmp_w2[:, 0, :], hid[:, 0, :], start=True, stop=True)
                    else:
                        for g in range(NKV):
                            mm = pe.matmul(bank[0:N_CMP, g * P:(g + 1) * P], hid[:, 1, g * N_CMP:(g + 1) * N_CMP],
                                           cmp_w2[:, 1, :], start=True, stop=True)
                    mm.then_inc(side_done, 1)
                elif kind == "cmp_logits":
                    g = step[1]
                    bank = free_side(n)
                    if g == 0:
                        pe.wait_ge(*read(SIDE[("cmp_out", 0)]))
                    for t in range(TT):
                        for h in range(HPG):
                            at = (t * HPG + h) * CMP_PAD
                            mm = pe.matmul(bank[:, at:at + N_CMP], qT[:, HPG * g + h, t * P:(t + 1) * P],
                                           kcT[:, g * N_CMP:(g + 1) * N_CMP], start=True, stop=True)
                    mm.then_inc(side_done, 1)
                elif kind == "cmp_turn":
                    a = HEADS[("cmp_logits", step[1])]
                    bank = free_side(n)
                    pe.wait_ge(head_prob, a + 1)
                    for t in range(TT):
                        mm = pe.transpose(bank[:, t * P:(t + 1) * P], p_cmp[:, t * P:(t + 1) * P], ident[:, :])
                    mm.then_inc(side_done, 1)
                elif kind == "cmp_values":
                    g, t = step[1:]
                    a = HEADS[("cmp_logits", g)]
                    bank = free_side(n)
                    pe.wait_ge(*read(SIDE[("cmp_turn", g)]))
                    if g == 0:
                        pe.wait_ge(cmp_vblock, 1)
                    pe.matmul(bank, work[:, probT[a % 2], t * P:(t + 1) * P], v_blocks[:, g, :], start=True,
                              stop=True).then_inc(side_done, 1)
                else:
                    raise ValueError(kind)

            def steps(todo):
                for step in todo:
                    if step[0] == "unit":
                        plain_unit(step[1], step[2])
                    elif step[0] not in LOCAL:
                        side(step)

            pe.wait_ge(consts_made, CONSTS_MADE)
            pe.wait_ge(consts_landed, 32)
            steps(MIXER)
            for w in last_reads([SIDE[("turn_y", j)] for j in range(8)]) + last_reads([SIDE[("att_values", N_ATT - 1)]]) \
                    + last_reads([SIDE[("mem_values", N_MEM - 1)]]):
                pe.wait_ge(*w)
            with pe.Fori(0, MIX_LOOPS) as i:
                for c in range(2):
                    u, b = c * 20, B0["mix"] + c * 12
                    for src, groups in ((o_aT, 2), (o_bT, 4), (o_cT, 2)):
                        for x, kgs in ((hT, 4), (src, groups)):
                            for kg in range(kgs):
                                n_unit("mix", u, x, kg, kgs, b, i, MIX_TURN, 6)
                                u += 1
                            b += 2
                for _, piece, c in MIX_TURNS:
                    mod_turn(piece, c, SIDE[("mod_turn", piece, c)], i)
            steps(AFTER_MIX + OUT + BEFORE_FFN)
            for part, tiles in enumerate(FF_PARTS):
                ff = f"ff{part}"
                with pe.Fori(0, tiles // 4) as i:
                    for u in range(8):
                        t_unit(ff, u, h2T, i, 8, 1)
                steps(FFN_OUT[part])
            steps(BEFORE_S5)
            for w in last_banks("su"):
                pe.wait_ge(*w)
            def inputs(cc, q, i=0):
                n, buf = SSM_SIDE0 + cc * PAIRS + q, cc % 2
                pe.wait_ge(ssm_prod, i * n_pairs + (cc * PAIRS + q + 1))
                if q == 0:
                    pe.wait_ge(ssm_landed[buf], i * 32 + 16 * (cc // 2 + 1))
                for part in range(2):
                    at = (2 * q + part) * P
                    mm = pe.matmul(side_bank(n)[:, part * S:(part + 1) * S], ssm_in[:, buf, at:at + P],
                                   uT_on[:, bass.ds(i * SSM_BODY + cc, 1), :].rearrange("p a t -> p (a t)"),
                                   start=True, stop=True)
                mm.then_inc(side_done, 1)

            def outputs(cc, q, bank, i):
                pe.wait_ge(ssm_back, i * n_pairs + (cc * PAIRS + q + 1))
                back = ssm_buf[q][1:]
                for m, (k, turned, part) in enumerate(((0, 0, 0), (1, 1, 1), (2, 1, 0), (2, 0, 1))):
                    mm = pe.matmul(bank[32 * q:32 * q + 32, 0:S], ssm_c[:, cc % 2, k, q, :],
                                   back[turned][:, part * S:(part + 1) * S], start=(m == 0), stop=(m == 3))
                mm.then_inc(ssm_y, 1)

            n_pairs = SSM_BODY * PAIRS
            for n in range(SSM_SIDE0 - 4, SSM_SIDE0):
                pe.wait_ge(*read(n))
            pe.nop().then_inc(ssm_y, SSM_AHEAD)
            for q in range(PAIRS):
                inputs(0, q)
            with pe.Fori(0, SSM_CHUNKS // SSM_BODY) as i:
                for cc in range(SSM_BODY):
                    b = B0["sz"] + 2 * cc
                    t_unit("sz", cc, h3T, i, SSM_BODY, 2, b)
                    bank = free_bank(b + 1, i, 2)
                    pe.wait_ge(ssm_cmul, i * SSM_BODY + cc + 1)
                    for q in range(PAIRS):
                        outputs(cc, q, bank, i)
                        inputs(cc + 1, q, i)
            steps(S5_GLU + S5_OUT)
            pe.wait_ge(late_landed, 16)
            steps(NSA)
            steps(NSA_OUT)

        @block.scalar
        def _(act):
            did = Steps(act, act_steps)

            for t in range(TT):
                act.dma_start(mem_in[:, t, :], A["mem"][t * P:(t + 1) * P, :]).then_inc(mem_landed[t], 16)
            act.dma_start(cst[:, :], A["cst"]).then_inc(consts_landed, 16)
            act.dma_start(early[:, 0:512], A["early"]).then_inc(consts_landed, 16)
            def root(n_norm):
                act.wait_ge(norm_mean, n_norm + 1)
                act.activation(stat[:, 2:4], stat[:, 2:4], ACT.Sqrt).then_inc(norm_root, 1)

            def squares(tag, src, junk, loaded):
                for t in range(TT):
                    act.wait_ge(loaded[t], 16)
                    if t:
                        act.wait_ge(norm_squares, SQUARES[tag] - 1)
                    act.activation(junk, src[:, t, :], ACT.Square, accum_out=stat[:, 32 + 4 * t:33 + 4 * t]).then_inc(norm_squares, 1)
                root(NORMS[tag])

            def squares_of_sum(tag, c):
                parts = NORM_PARTS[tag]
                cols = slice(c * D // parts, (c + 1) * D // parts)
                for t in range(TT):
                    k = TT * c + t - TT * parts + 1
                    act.wait_ge(res_added, RES_ADDED[tag] + k)
                    act.wait_ge(norm_squares, SQUARES[tag] + k - 1)
                    act.activation(xn[:, 1, 0:D // parts], xr[:, t, cols], ACT.Square,
                                   accum_out=stat[:, 32 + 4 * t + c:33 + 4 * t + c]).then_inc(norm_squares, 1)
                if c == parts - 1:
                    root(NORMS[tag])

            def local(step):
                if step[0] == "rms":
                    act.wait_ge(norm_scaled, 4 * TT)
                    squares("x", x_in, tokens(0)[:, 1, :], [x_landed] * TT)
                elif step[0] == "angles":
                    for which in range(2):
                        act.wait_ge(ang_ready, which + 1)
                        did(act.activation(ropes[:, 2 * which + 1, :], rope_ang[which], ACT.Sin))
                        did(act.activation(rope_abs, rope_ang[which], ACT.Abs))
                        did.wait()
                        act.activation(ropes[:, 2 * which, :], rope_abs, ACT.Sin, scale=-1.0,
                                       bias=half_pi[:, 0:1]).then_inc(rope_ready, 1)
                        act.wait_ge(rope_ready, which + 1)
                elif step[0] == "s5_params":
                    act.wait_ge(s5_raw_landed, 16)
                    if step[1] == 0:
                        act.activation(s5_dt, s5_raw[:, 2, :], ACT.Exp).then_inc(s5_ready, 1)
                    if step[1] != 2:
                        return
                    act.wait_ge(s5_ready, 2)
                    did(act.activation(s5_sin, s5_thr, ACT.Sin))
                    act.activation(s5_sin2, s5_thr, ACT.Sin, scale=0.5).then_inc(trig_done, 1)

            def exps(a, src, dst, scale):
                at = 16 + 8 * (a % 2)
                did(act.activation(dst[:, 0, :], src[:, 0, :], ACT.Exp, bias=stat[:, at + 2:at + 3], scale=scale,
                                   accum_out=stat[:, at + 4:at + 5]))
                return act.activation(dst[:, 1, :], src[:, 1, :], ACT.Exp, bias=stat[:, at + 3:at + 4], scale=scale,
                                      accum_out=stat[:, at + 5:at + 6])

            def copy_bank(phase, b, dst, func=ACT.Copy):
                act.activation(dst, stream_bank(B0[phase] + b), func).then_inc(evacuated[(B0[phase] + b) % 4], 1)

            T_DST = {"mk": mkT, "mq": mqT, "su": uT, "sz": zT[1], "nq": qT}
            N_DST = {"mv": mv, "av": av, "rv": rv}

            def cut(g, i=None, per=0):
                if g >= UNITS or ORDER[g][0] == "mod" or ORDER[g][1] == "cw":
                    return
                for h in range(2):
                    value = 16 * (g // RING + 1)
                    act.wait_ge(landed[(2 * g + h) % (2 * RING)], value if i is None else i * (per // RING * 16) + value)
                    if g >= RING:
                        value = 2 * (g - RING) + h + 1
                        act.wait_ge(units_done, value if i is None else i * (2 * per) + value)
                    cols = slice(h * HALF, (h + 1) * HALF)
                    act.activation(r32(hi[:, g % RING, cols]), ring[:, g % RING, cols], ACT.Copy).then_inc(hi_made, 1)

            def square(phase, c, t):
                n = (phase == "fo1") * 4 * TT + TT * c + t
                if n:
                    act.wait_ge(res_squares, n)
                at = 32 + 4 * t + c
                act.activation(work[:, TMP[0], :], y[:, t, c * CHUNK:(c + 1) * CHUNK], ACT.Square,
                               accum_out=stat[:, at:at + 1]).then_inc(res_squares, 1)

            def unit(phase, u):
                if phase in T_DST and u % 2:
                    act.wait_ge(*multiplied(phase, u))
                    copy_bank(phase, u // 2, both(T_DST[phase], u // 2), ACT.Silu if phase == "sz" else ACT.Copy)
                elif ("rope", phase, u // 2) in ROPE and (u % 2 or phase == "ik"):
                    r = ROPE[("rope", phase, u // 2)]
                    act.wait_ge(*multiplied(phase, u))
                    if r >= 2:
                        act.wait_ge(roped, r - 1)
                    width = S if phase == "ik" else 2 * S
                    b = B0[phase] + u // 2
                    act.activation(work[:, TMP[r % 2], 0:width], stream_bank(b)[:, 0:width],
                                   ACT.Copy).then_inc(evacuated[b % 4], 1)
                elif phase in N_DST and u % 4 == 3:
                    act.wait_ge(*multiplied(phase, u))
                    c = u // 4
                    for t in range(TT):
                        copy_bank(phase, 2 * c + t, N_DST[phase][:, t, c * CHUNK:(c + 1) * CHUNK])
                elif phase == "rg" and u % 4 == 3:
                    act.wait_ge(*multiplied(phase, u))
                    c = u // 4
                    if c:
                        act.wait_ge(ret_gated, TT * c)
                    for t in range(TT):
                        copy_bank(phase, 2 * c + t, work[:, TMP[t], :], ACT.Silu)
                elif phase == "wo" and u % 4 == 3:
                    c = u // 4
                    act.wait_ge(*multiplied(phase, u))
                    for t in range(TT):
                        copy_bank(phase, 2 * c + t, y[:, t, c * CHUNK:(c + 1) * CHUNK])
                        act.wait_ge(*emptied(B0[phase] + 2 * c + t))
                        square(phase, c, t)
                elif phase == "fo0" and (u + 1) % (FF_PARTS[0] // KG) == 0:
                    act.wait_ge(*multiplied(phase, u))
                    c = u // (FF_PARTS[0] // KG)
                    for t in range(TT):
                        copy_bank(phase, 2 * c + t, y[:, t, c * CHUNK:(c + 1) * CHUNK])
                elif phase == "fo1" and (u + 1) % (FF_PARTS[1] // KG) == 0:
                    c = u // (FF_PARTS[1] // KG)
                    for t in range(TT):
                        act.wait_ge(*emptied(B0[phase] + 2 * c + t))
                        square(phase, c, t)
                elif phase == "glu" and u % 2:
                    act.wait_ge(*multiplied(phase, u))
                    b = u // 2
                    for c in range(2):
                        ins = act.activation(work[:, b % 4, c * S:(c + 1) * S], stream_bank(B0["glu"] + b)[:, c * S:(c + 1) * S],
                                             ACT.Sigmoid, bias=vecs[:, V["b_glu"], 2 * b + c:2 * b + c + 1])
                    ins.then_inc(glu_gate, 1)
                elif phase == "kvt" and u % 2 and u >= 8:
                    act.wait_ge(*multiplied(phase, u))
                    copy_bank(phase, u // 2, both(ksT if u < 12 else kwT, (u // 2) % 2))
                elif phase == "kvn" and u % 4 == 3:
                    act.wait_ge(*multiplied(phase, u))
                    for t in range(TT):
                        copy_bank(phase, u // 4 * 2 + t, (vs if u < 4 else vw)[:, t, :])
                elif phase in ("so", "no") and u and (u % 4 == 0 or u == 15):
                    squares_of_sum("x3" if phase == "so" else "out", (u - 1) // 4)
                elif phase == "nz" and u % 4 == 3:
                    c = u // 4
                    act.wait_ge(*multiplied(phase, u))
                    if c >= 2:
                        act.wait_ge(o_added, O_AFTER[c - 2])
                    for t in range(TT):
                        copy_bank(phase, 2 * c + t, zs[:, c % 2, t, :], ACT.Silu)

            def side(step):
                kind, n = step[0], SIDE[step]
                done = side_read[n % 4]
                if kind == "norm":
                    tag, j = step[1:]
                    if tag in ("x2", "x3") and j == 0:
                        act.wait_ge(mod_gain, 1 if tag == "x2" else 2)
                    act.wait_ge(*written(n))
                    dst, gain, shift = NORM_TO[tag]
                    for c in range(2):
                        k = 2 * j + c
                        part = side_bank(n)[:, c * S:(c + 1) * S]
                        ins = act.activation(r32(dst[0][:, k, :]), part, ACT.Identity, scale=gain[:, k:k + 1],
                                             bias=0.0 if shift is None else shift[:, k:k + 1])
                        if tag == "x3":
                            gain2, shift2 = gains[:, 2, k:k + 1], modv[:, PIECES.index("nsa_shift"), k:k + 1]
                            ins = act.activation(hnT[1][:, k, :], part, ACT.Identity, scale=gain2, bias=shift2)
                    ins.then_inc(rounded, 1)
                elif kind == "idx":
                    h = step[1]
                    act.wait_ge(*written(n))
                    if h >= 2:
                        act.wait_ge(idx_added, h - 1)
                    act.activation(work[:, prob[h % 2], :], side_bank(n), ACT.Relu).then_inc(done, 1)
                elif kind == "mem_logits":
                    a = HEADS[step]
                    act.wait_ge(head_max, a + 1)
                    if a >= 2:
                        act.wait_ge(*written(SIDE[TURNS[a - 2]]))
                    exps(a, halves_of(side_bank(n)), halves(prob[a % 2]), 0.0625).then_inc(done, 1)
                elif kind in ("att_logits", "sel_logits", "win_logits"):
                    a = HEADS[step]
                    act.wait_ge(head_max, a + 1)
                    exps(a, halves(prob[a % 2]), halves(prob[a % 2]), HD ** -0.5).then_inc(head_exp, 1)
                elif kind == "cmp_logits":
                    a = HEADS[step]
                    act.wait_ge(head_max, a + 1)
                    p4 = p_cmp.rearrange("p (a n) -> p a n", n=CMP_PAD)[:, :, 0:N_CMP]
                    act.activation(p4, p4, ACT.Exp, scale=HD ** -0.5).then_inc(head_exp, 1)
                elif kind.endswith("_turn") and kind != "mod_turn":
                    a = HEADS[(kind[:3] + "_logits", step[1])]
                    act.wait_ge(*written(n))
                    if a >= 2:
                        act.wait_ge(*written(SIDE[VALUES[a - 2]]))
                    width = 2 * P if kind == "cmp_turn" else 2 * S
                    act.activation(work[:, probT[a % 2], 0:width], side_bank(n)[:, 0:width], ACT.Copy).then_inc(done, 1)
                elif kind in ("mem_values", "att_values", "turn_y", "turn_mix", "turn_o"):
                    j = step[1]
                    act.wait_ge(*written(n))
                    dst = {"mem_values": o_cT, "att_values": o_aT, "turn_y": o_bT, "turn_mix": mixT, "turn_o": oT}[kind][0]
                    if kind == "att_values":
                        act.activation(r32(dst[:, j, :]), side_bank(n)[:, 0:S], ACT.Copy).then_inc(rounded, 1)
                    else:
                        act.activation(r32(both(dst, j)), side_bank(n), ACT.Copy).then_inc(rounded, 1)
                    if kind == "mem_values" and j == N_MEM - 1:
                        act.dma_start(decay, A["decay"].rearrange("p (h t) -> p h t", h=N_RET)).then_inc(decay_landed, 16)
                elif kind == "ret_values" and step[1] == N_RET - 1:
                    act.wait_ge(ret_var, 1)
                    act.activation(stat[:, 48:64], stat[:, 48:64], ACT.Sqrt).then_inc(ret_root, 1)
                elif kind == "gate":
                    act.wait_ge(*written(n))
                    to = row if step[1] == "s5" else nsa_row
                    act.activation(to[:, step[2] * CHUNK:(step[2] + 1) * CHUNK], side_bank(n), ACT.Copy).then_inc(done, 1)
                elif kind == "cmp_hidden":
                    act.wait_ge(*written(n))
                    act.activation(hid[:, step[1], :], side_bank(n)[:, 0:NKV * N_CMP], ACT.Gelu_apprx_tanh).then_inc(done, 1)
                elif kind == "cmp_out" and step[1] == 1:
                    for q in range(4):
                        act.activation(r32(hnT[0][:, 4 * q:4 * q + 4, :]), hnT[1][:, 4 * q:4 * q + 4, :],
                                       ACT.Copy).then_inc(hn_hi, 1)
                elif kind == "cmp_out" and step[1] == 0:
                    act.wait_ge(*written(n))
                    act.activation(kcT, side_bank(n)[:, 0:NKV * N_CMP], ACT.Identity, bias=b2_col).then_inc(done, 1)
                elif kind in ("idx_w", "ngate"):
                    act.wait_ge(*written(n))
                    m = N_IDX if kind == "idx_w" else 3 * NQ
                    act.activation(few[kind][0:m, :], side_bank(n)[0:m, 0:S], ACT.Copy).then_inc(done, 1)
                elif kind == "ngate_back":
                    act.wait_ge(*written(n))
                    act.activation(gates.rearrange("p t n -> p (t n)"), side_bank(n)[:, 0:TT * 3 * NQ],
                                   ACT.Sigmoid).then_inc(done, 1)

            def steps(todo):
                for step in todo:
                    for x in visited(step):
                        cut(POS[x] + LEAD)
                    if step[0] == "unit":
                        unit(step[1], step[2])
                    elif step[0] in LOCAL:
                        if step[0] != "mod":
                            local(step)
                    else:
                        side(step)

            def branch_root(n):
                act.wait_ge(res_mean, n + 1)
                act.activation(stat[:, 40:42], stat[:, 40:42], ACT.Sqrt).then_inc(res_root, 1)

            squares("mem", mem_in, tokens(0)[:, 0, :], mem_landed)
            act.wait_ge(consts_landed, 32)
            act.activation(c_act[:, :], vecs[:, V["c"], :], ACT.Silu).then_inc(act_ready, 1)
            act.dma_start(x_in, A["x"].rearrange("(t p) n -> p t n", p=P)).then_inc(x_landed, 16)
            act.dma_start(pos_i, A["positions"].broadcast_to([P, S])).then_inc(pos_landed, 16)
            act.dma_start(s5_raw, A["s5_raw"]).then_inc(s5_raw_landed, 16)
            cut(0)
            steps(MIXER[:KT // 2])
            cut(1)
            steps(MIXER[KT // 2:])
            with act.Fori(0, MIX_LOOPS) as i:
                for step in MIX_BODY:
                    cut(POS[step] + LEAD, i, MIX_TURN)
                    if step[0] != "unit" or step[2] + 1 not in MIX_GATES:
                        continue
                    m = MIX_GATES.index(step[2] + 1)
                    b = B0["mix"] + 4 * m
                    act.wait_ge(units_done, i * (2 * MIX_TURN) + (2 * POS[step] + 2))
                    for t in range(TT):
                        old = b + t + 2 - 8
                        act.wait_ge(evacuated[old % 4], i * 6 + (old // 4 + 1))
                        act.activation(work[:, (m % 2) * 2 + t, :], stream_bank(b + t),
                                       ACT.Sigmoid).then_inc(evacuated[(b + t) % 4], 1)
            steps(AFTER_MIX)
            act.dma_start(xr, A["x"].rearrange("(t p) n -> p t n", p=P)).then_inc(x_again_landed, 16)
            act.dma_start(row, A["g_post_mix"].broadcast_to([P, D])).then_inc(rows_landed, 16)
            steps(OUT)
            branch_root(0)
            for c in range(NORM_PARTS["x1"]):
                squares_of_sum("x1", c)
            act.dma_start(row, A["g_post_ffn"].broadcast_to([P, D])).then_inc(rows_landed, 16)
            steps(BEFORE_FFN)
            for part, tiles in enumerate(FF_PARTS):
                ff = f"ff{part}"
                with act.Fori(0, tiles // 4) as i:
                    for u in range(8):
                        g = POS[("unit", ff, u)]
                        cut(g + LEAD, i, 8)
                        if u % 2:
                            act.wait_ge(units_done, i * 16 + (2 * g + 2))
                            act.activation(work[:, u // 2, 0:S], stream_bank(B0[ff] + u // 2)[:, 0:S],
                                           ACT.Silu).then_inc(ff_gate, 1)
                steps(FFN_OUT[part])
            branch_root(1)
            for c in range(NORM_PARTS["x2"]):
                squares_of_sum("x2", c)
            act.dma_start(x_kept.rearrange("(t p) n -> p t n", p=P), xr).then_inc(x_stored, 16)
            steps(BEFORE_S5)

            def wholes(value, buf):
                act.wait_ge(ssm_turns, value)
                did(act.activation(whole_t[buf], frac_t, ACT.Identity, bias=round_up[:, 0:1]))
                did.wait()
                act.activation(whole_t[buf], whole_t[buf], ACT.Identity, bias=round_back[:, 0:1]).then_inc(ssm_whole, 1)

            def tables(value, buf):
                act.wait_ge(ssm_frac, value)
                did(act.activation(abs_t, frac_t, ACT.Abs))
                did(act.activation(sin_t[buf], frac_t, ACT.Sin, scale=TURN_F))
                did.wait()
                act.activation(cos_t[buf], abs_t, ACT.Sin, scale=-TURN_F, bias=half_pi[:, 0:1]).then_inc(ssm_trig, 1)

            act.dma_start(ssm_in[:, 0, :], A["ssm_bc"][0]).then_inc(ssm_landed[0], 16)
            act.wait_ge(x_stored, 16)
            wholes(1, 0)
            tables(1, 0)
            act.nop().then_inc(ssm_gelu, SSM_GELU0)
            with act.Fori(0, SSM_CHUNKS // SSM_BODY) as i:
                did.enter(i, 3 * SSM_BODY)
                def gelu(cc):
                    b = B0["sz"] + 2 * cc + 1
                    act.wait_ge(evacuated[b % 4], i * 2 + (b // 4 + 1))
                    act.activation(uT[:, bass.ds(i * SSM_BODY + cc, 1), :].rearrange("p a t -> p (a t)"),
                                   work[:, TMP[cc % 2], 0:S], ACT.Gelu_apprx_tanh).then_inc(ssm_gelu, 1)

                for cc in range(SSM_BODY):
                    buf = (cc + 1) % 2
                    act.wait_ge(ssm_y, i * (SSM_BODY * PAIRS) + PAIRS * cc + SSM_AHEAD)
                    act.dma_start(ssm_in[:, buf, :], A["ssm_bc"][bass.ds(i * SSM_BODY + (cc + 1), 1)]
                                  .rearrange("a p n -> p (a n)")).then_inc(ssm_landed[buf], 16)
                    wholes(i * SSM_BODY + (cc + 2), buf)
                    g = POS[("unit", "sz", cc)]
                    b = B0["sz"] + 2 * cc
                    act.wait_ge(units_done, i * (2 * SSM_BODY) + (2 * g + 2))
                    act.activation(zT[1][:, bass.ds(i * SSM_BODY + cc, 1), :].rearrange("p a t -> p (a t)"),
                                   stream_bank(b)[:, 0:S], ACT.Silu).then_inc(evacuated[b % 4], 1)
                    if cc:
                        gelu(cc - 1)
                    tables(i * SSM_BODY + (cc + 2), buf)
                    cut(g + LEAD, i, SSM_BODY)
                gelu(SSM_BODY - 1)
                did.leave(SSM_CHUNKS // SSM_BODY)
            act.wait_ge(ssm_landed[0], 16 * (SSM_CHUNKS // 2 + 1))
            act.wait_ge(ssm_gelu, SSM_CHUNKS + SSM_GELU0)
            act.wait_ge(ssm_trig, SSM_CHUNKS + 1)
            act.wait_ge(ssm_turns, SSM_CHUNKS + 2)
            act.dma_start(xr, x_kept.rearrange("(t p) n -> p t n", p=P)).then_inc(x_again_landed, 16)
            for q in range(4):
                act.activation(r32(yT[0][:, 4 * q:4 * q + 4, :]), uT[:, 4 * q:4 * q + 4, :], ACT.Copy).then_inc(y_hi, 1)
            steps(S5_GLU + S5_OUT)
            act.dma_start(early[:, 0:LATE], A["late"]).then_inc(late_landed, 16)
            steps(NSA)
            act.dma_start(final_row, A["final_norm_g"].broadcast_to([P, D])).then_inc(final_row_landed, 16)
            steps(NSA_OUT)

        @block.vector
        def _(dve):
            did = Steps(dve, dve_steps)

            def then(ins):
                did(ins)
                did.wait()

            def rms_scale(tag):
                n_norm, parts = NORMS[tag], NORM_PARTS[tag]
                dve.wait_ge(norm_squares, SQUARES[tag])
                then(dve.tensor_reduce(stat[:, 0:2], stat[:, 32:40].rearrange("p (t c) -> p t c", t=TT)[:, :, 0:parts], AX, ALU.add))
                dve.tensor_scalar(stat[:, 2:4], stat[:, 0:2], 1.0 / D, EPS, ALU.mult, ALU.add).then_inc(norm_mean, 1)
                dve.wait_ge(norm_root, n_norm + 1)
                then(dve.reciprocal(stat[:, 4:6], stat[:, 2:4]))

            def rms(tag, src, dst):
                rms_scale(tag)
                for c in range(D // CHUNK):
                    for t in range(TT):
                        cols = slice(c * CHUNK, (c + 1) * CHUNK)
                        dve.tensor_scalar(dst[:, t, cols], src[:, t, cols], stat[:, 4 + t:5 + t], None,
                                          ALU.mult).then_inc(norm_scaled, 1)

            def angles():
                dve.wait_ge(pos_landed, 16)
                then(dve.tensor_copy(rope_pos, pos_i))
                for w in range(2):
                    r, k = rope_ang[w], rope_k
                    then(dve.tensor_scalar(r, rope_pos, freq[:, w:w + 1], None, ALU.mult))
                    then(dve.tensor_scalar(k, r, 1.0 / TURN, ROUND, ALU.mult, ALU.add))
                    then(dve.tensor_scalar(k, k, -ROUND, None, ALU.add))
                    then(dve.scalar_tensor_tensor(out=r, in0=k, scalar=-TURN_HI, in1=r, op0=ALU.mult, op1=ALU.add))
                    then(dve.scalar_tensor_tensor(out=r, in0=k, scalar=-TURN_LO, in1=r, op0=ALU.mult, op1=ALU.add))
                    dve.tensor_scalar(r, r, -PI, PI, ALU.max, ALU.min).then_inc(ang_ready, 1)
                    dve.wait_ge(ang_ready, w + 1)

            def s5_states():
                lr, li, dt, w_, e_, a_, b_, c_ = (s5_raw[:, 0, :], s5_raw[:, 1, :], s5_dt, s5_tmp[0], s5_tmp[1], s5_tmp[2],
                                                 s5_tmp[3], s5_tmp[4])
                mag, turn, kre, kim, nkim = (s5[:, r, 0:SSM_CHUNKS * PAIRS] for r in range(5))
                yield
                dve.wait_ge(s5_raw_landed, 16)
                dve.wait_ge(s5_ready, 1)
                then(dve.tensor_tensor(w_, lr, dt, ALU.mult))
                then(dve.tensor_scalar(w_, w_, -20.0, 1.0 / 32, ALU.max, ALU.mult))
                then(dve.tensor_scalar(e_, w_, 1.0 / 8, 1.0, ALU.mult, ALU.add))
                for m in range(7, 1, -1):
                    then(dve.tensor_tensor(e_, e_, w_, ALU.mult))
                    then(dve.tensor_scalar(e_, e_, 1.0 / m, 1.0, ALU.mult, ALU.add))
                yield
                then(dve.tensor_tensor(e_, e_, w_, ALU.mult))
                for _ in range(5):
                    then(dve.scalar_tensor_tensor(out=e_, in0=e_, scalar=2.0, in1=e_, op0=ALU.add, op1=ALU.mult))
                then(dve.tensor_scalar(mag, e_, 1.0, None, ALU.add))
                yield
                then(dve.tensor_tensor(a_, li, dt, ALU.mult))
                then(dve.tensor_scalar(b_, a_, 1.0 / TURN, ROUND, ALU.mult, ALU.add))
                then(dve.tensor_scalar(b_, b_, -ROUND, None, ALU.add))
                then(dve.scalar_tensor_tensor(out=a_, in0=b_, scalar=-TURN_HI, in1=a_, op0=ALU.mult, op1=ALU.add))
                then(dve.scalar_tensor_tensor(out=a_, in0=b_, scalar=-TURN_LO, in1=a_, op0=ALU.mult, op1=ALU.add))
                then(dve.tensor_scalar(turn, a_, 1.0 / TURN, None, ALU.mult))
                dve.tensor_scalar(s5_thr, a_, -PI, PI, ALU.max, ALU.min).then_inc(s5_ready, 1)
                yield
                dve.wait_ge(trig_done, 1)
                then(dve.tensor_tensor(a_, s5_sin, mag, ALU.mult))
                then(dve.tensor_tensor(b_, s5_sin2, s5_sin2, ALU.mult))
                then(dve.tensor_tensor(b_, b_, mag, ALU.mult))
                then(dve.scalar_tensor_tensor(out=e_, in0=b_, scalar=-2.0, in1=e_, op0=ALU.mult, op1=ALU.add))
                then(dve.tensor_tensor(b_, lr, lr, ALU.mult))
                then(dve.tensor_tensor(c_, li, li, ALU.mult))
                then(dve.tensor_tensor(b_, b_, c_, ALU.add))
                then(dve.reciprocal(b_, b_))
                yield
                then(dve.tensor_tensor(c_, e_, lr, ALU.mult))
                then(dve.tensor_tensor(w_, a_, li, ALU.mult))
                then(dve.tensor_tensor(c_, c_, w_, ALU.add))
                then(dve.tensor_tensor(kre, c_, b_, ALU.mult))
                then(dve.tensor_tensor(c_, a_, lr, ALU.mult))
                then(dve.tensor_tensor(w_, e_, li, ALU.mult))
                then(dve.tensor_tensor(c_, c_, w_, ALU.subtract))
                then(dve.tensor_tensor(kim, c_, b_, ALU.mult))
                dve.tensor_scalar(nkim, kim, -1.0, None, ALU.mult).then_inc(s5_params, 1)
                dve.wait_ge(s5_params, 1)
                yield

            states_parts = s5_states()
            next(states_parts)

            def softmax_tail(a, n, p, masked):
                at = 16 + 8 * (a % 2)
                if masked:
                    dve.wait_ge(head_exp, MASKED[a] + 1)
                else:
                    dve.wait_ge(*read(n))
                then(dve.reciprocal(stat[:, at + 6:at + 8], stat[:, at + 4:at + 6]))
                dve.tensor_tensor(p, p, stat[:, at + 6:at + 8].unsqueeze(2).broadcast_to([P, TT, S]),
                                  ALU.mult).then_inc(head_prob, 1)

            def maximum(a, src, scale):
                at = 16 + 8 * (a % 2)
                then(dve.tensor_reduce(stat[:, at:at + 2], src, AX, ALU.max))
                dve.tensor_scalar(stat[:, at + 2:at + 4], stat[:, at:at + 2], -scale, None, ALU.mult).then_inc(head_max, 1)

            def top_k(step):
                if step[0] == "topk":
                    t, part = step[1:]
                    if (t, part) == (0, 0):
                        dve.wait_ge(idx_added, N_IDX)
                    if part == 0:
                        then(dve.tensor_tensor(top[:, t, :], score[:, t, :], causal[:, t, :], ALU.add))
                    for _ in range(2):
                        then(dve.max(stat[:, 8:16], top[:, t, :]))
                        then(dve.match_replace(out=top[:, t, :], in_to_replace=stat[:, 8:16], in_values=top[:, t, :],
                                               imm_value=TAKEN))
                else:
                    then(dve.tensor_scalar(top, top, TAKEN, None, ALU.is_equal))
                    then(dve.tensor_scalar(top, top, -1.0, -NEG, ALU.add, ALU.mult))
                    dve.tensor_tensor(selbias, top, causal, ALU.add).then_inc(sel_ready, 1)
                    dve.wait_ge(sel_ready, 1)

            def local(step):
                if step[0] == "rms":
                    dve.wait_ge(x_landed, 16)
                    rms("x", x_in, x_in)
                elif step[0] == "angles":
                    angles()
                elif step[0] == "s5_params":
                    next(states_parts)
                else:
                    top_k(step)

            def flat2(ap):
                return ap.rearrange("p (t s) -> p t s", t=TT)

            def side(step):
                kind, n = step[0], SIDE[step]
                done = side_read[n % 4]
                if kind == "norm":
                    tag, j = step[1:]
                    dst, gain, shift = NORM_TO[tag]
                    dve.wait_ge(rounded, ROUNDED[step] + 1)
                    for c in range(2):
                        k = 2 * j + c
                        part, hi_k, lo_k = side_bank(n)[:, c * S:(c + 1) * S], dst[0][:, k, :], dst[1][:, k, :]
                        if shift is None:
                            ins = dve.scalar_tensor_tensor(out=r32(lo_k), in0=part, scalar=gain[:, k:k + 1], in1=as32(hi_k),
                                                           op0=ALU.mult, op1=ALU.subtract)
                        else:
                            did(dve.tensor_scalar(lo_k, part, gain[:, k:k + 1], shift[:, k:k + 1], ALU.mult, ALU.add))
                    if shift is not None:
                        did.wait()
                        ins = dve.tensor_tensor(r32(both(dst[1], j)), both(dst[1], j), as32(both(dst[0], j)), ALU.subtract)
                    ins.then_inc(done, 1)
                elif kind in ("mem_values", "att_values", "turn_y", "turn_mix", "turn_o"):
                    j = step[1]
                    dst = {"mem_values": o_cT, "att_values": o_aT, "turn_y": o_bT, "turn_mix": mixT, "turn_o": oT}[kind]
                    dve.wait_ge(rounded, ROUNDED[step] + 1)
                    if kind == "att_values":
                        dve.tensor_tensor(r32(dst[1][:, j, :]), side_bank(n)[:, 0:S], as32(dst[0][:, j, :]),
                                          ALU.subtract).then_inc(done, 1)
                    else:
                        dve.tensor_tensor(r32(both(dst[1], j)), side_bank(n), as32(both(dst[0], j)), ALU.subtract).then_inc(done, 1)
                elif kind == "mod_turn":
                    mod_vec(step[1], step[2], n)
                elif kind == "rope":
                    r = ROPE[step]
                    phase, b = step[1:]
                    w = 1 if phase in ("ik", "iq") else 0
                    heads = 1 if phase == "ik" else 2
                    raw = work[:, TMP[r % 2], 0:heads * S].rearrange("p (h t) -> p h t", h=heads)
                    swapped = work[:, TMP[2], 0:heads * S].rearrange("p (h t) -> p h t", h=heads)
                    cos, sin = (ropes[:, 2 * w + k, :].unsqueeze(1).broadcast_to([P, heads, S]) for k in range(2))
                    if r == 0:
                        dve.wait_ge(rope_ready, 2)
                    else:
                        dve.wait_ge(roped, r)
                    dve.wait_ge(*written(n))
                    did(dve.tensor_tensor(raw, raw, cos, ALU.mult))
                    dve.tensor_tensor(swapped, side_bank(n)[:, 0:heads * S].rearrange("p (h t) -> p h t", h=heads), sin,
                                      ALU.mult).then_inc(done, 1)
                    did.wait()
                    dve.wait_ge(*read(n))
                    if phase == "ik":
                        did(dve.tensor_tensor(ikT[0:64, 0, :], raw[0:64, 0, :], swapped[0:64, 0, :], ALU.add))
                        dve.tensor_tensor(ikT[64:128, 1, :], raw[64:128, 0, :], swapped[64:128, 0, :],
                                          ALU.add).then_inc(roped, 1)
                    else:
                        dst = {"iq": iqT, "aq": aqT, "ak": akT, "rq": rqT, "rk": rkT}[phase]
                        dve.tensor_tensor(dst[:, 2 * b:2 * b + 2, :], raw, swapped, ALU.add).then_inc(roped, 1)
                elif kind == "idx_w_back":
                    dve.wait_ge(*written(n))
                    dve.tensor_scalar(iw[:, :, :], side_bank(n)[:, 0:TT * N_IDX].rearrange("p (t h) -> p t h", t=TT),
                                      64 ** -0.5 * N_IDX ** -0.5, None, ALU.mult).then_inc(done, 1)
                    then(dve.memset(score, 0.0))
                    dve.wait_ge(*read(n))
                elif kind == "idx":
                    h = step[1]
                    dve.wait_ge(*read(n))
                    if h:
                        dve.wait_ge(idx_added, h)
                    for t in range(TT):
                        ins = dve.scalar_tensor_tensor(out=score[:, t, :], in0=halves(prob[h % 2])[:, t, :],
                                                       scalar=iw[:, t, h:h + 1], in1=score[:, t, :], op0=ALU.mult,
                                                       op1=ALU.add)
                    ins.then_inc(idx_added, 1)
                elif kind == "mem_logits":
                    a = HEADS[step]
                    dve.wait_ge(*written(n))
                    maximum(a, flat2(side_bank(n)), 0.0625)
                    softmax_tail(a, n, halves(prob[a % 2]), False)
                elif kind in ("att_logits", "sel_logits", "win_logits"):
                    a = HEADS[step]
                    p = halves(prob[a % 2])
                    dve.wait_ge(*written(n))
                    dve.wait_ge(*written(SIDE[TURNS[a - 2]]))
                    dve.tensor_tensor(p, flat2(side_bank(n)), selbias if kind == "att_logits" else causal,
                                      ALU.add).then_inc(done, 1)
                    dve.wait_ge(*read(n))
                    maximum(a, p, HD ** -0.5)
                    softmax_tail(a, n, p, True)
                elif kind == "ret_scores":
                    h = step[1]
                    if h == 0:
                        dve.wait_ge(decay_landed, 16)
                    dve.wait_ge(*written(n))
                    if h >= 2:
                        dve.wait_ge(*written(SIDE[("ret_values", h - 2)]))
                    sd = work[:, prob[h % 2], :]
                    dve.tensor_tensor(sd[:, 0:S], side_bank(n)[:, 0:S], decay[:, h, :], ALU.mult)
                    dve.tensor_tensor(sd[:, S:S + P], side_bank(n)[:, S:S + P], decay[:, h, 0:P],
                                      ALU.mult).then_inc(done, 1)
                elif kind == "ret_values":
                    h = step[1]
                    dve.wait_ge(*written(n))
                    if h:
                        did.wait()
                    for t in range(TT):
                        did(dve.bn_stats(bn[:, t, :], side_bank(n)[:, t * RETV:(t + 1) * RETV]))
                    did.wait()
                    for t in range(TT):
                        k = TT * h + t
                        did(dve.bn_aggr(ret_stat[:, k, :], bn[:, t, :]))
                    dve.tensor_copy(rv[:, :, h * RETV:(h + 1) * RETV], flat2(side_bank(n))).then_inc(done, 1)
                    if h == N_RET - 1:
                        dve.wait_ge(*read(n))
                        did.wait()
                        dve.tensor_scalar(stat[:, 48:64], ret_stat[:, :, 1], EPS, None, ALU.add).then_inc(ret_var, 1)
                        dve.wait_ge(ret_root, 1)
                        then(dve.reciprocal(stat[:, 48:64], stat[:, 48:64]))
                        for hh in range(N_RET):
                            for t in range(TT):
                                k = TT * hh + t
                                yh = rv[:, t, hh * RETV:(hh + 1) * RETV]
                                did(dve.tensor_scalar(yh, yh, ret_stat[:, k, 0:1], stat[:, 48 + k:49 + k],
                                                      ALU.subtract, ALU.mult))
                        did.wait()
                elif kind == "gate":
                    tag, j = step[1:]
                    piece = PIECES.index(tag + "_gate")
                    g = GATES[step]
                    if tag == "nsa" and j == 0:
                        dve.wait_ge(o_added, O_ADDS)
                    if j >= 2:
                        dve.wait_ge(*written(SIDE[(kind, tag, j - 2)]))
                    for c in range(4):
                        k = 4 * j + c
                        ins = dve.tensor_scalar(work[:, TMP[j % 2], c * P:(c + 1) * P], ident, modv[:, piece, k:k + 1],
                                                None, ALU.mult)
                    ins.then_inc(diag_ready, 1)
                elif kind == "cmp_hidden" and step[1] == 0:
                    then(dve.memset(p_cmp, 0.0))
                elif kind == "cmp_out" and step[1] == 1:
                    dve.wait_ge(*written(n))
                    dve.tensor_tensor(v_tmp[0:N_CMP, :, :],
                                      side_bank(n)[0:N_CMP, :].rearrange("p (g d) -> p g d", g=NKV),
                                      b2_row[0:N_CMP, :].unsqueeze(1).broadcast_to([N_CMP, NKV, P]),
                                      ALU.add).then_inc(done, 1)
                    dve.wait_ge(*read(n))
                    dve.wait_ge(v_zero, 1)
                    for h in range(HPG):
                        ins = dve.tensor_copy(v_blocks[32 * h:32 * h + N_CMP, :, h * P:(h + 1) * P], v_tmp[0:N_CMP, :, :])
                    ins.then_inc(cmp_vblock, 1)
                    for q in range(4):
                        dve.wait_ge(hn_hi, q + 1)
                        whole, top_part = (x[:, 4 * q:4 * q + 4, :] for x in (hnT[1], hnT[0]))
                        dve.tensor_tensor(r32(whole), whole, as32(top_part), ALU.subtract).then_inc(hn_cut, 1)
                elif kind == "cmp_logits":
                    a, g = HEADS[step], step[1]
                    p4 = p_cmp.rearrange("p (t h n) -> p t h n", t=TT, h=HPG)[:, :, :, 0:N_CMP]
                    p3 = p_cmp.rearrange("p (a n) -> p a n", n=CMP_PAD)[:, :, 0:N_CMP]
                    add, keep = (m.unsqueeze(2).broadcast_to([P, TT, HPG, N_CMP]) for m in (cmp_add, cmp_keep))
                    logit4 = side_bank(n)[:, 0:2 * P].rearrange("p (t h n) -> p t h n", t=TT, h=HPG)[:, :, :, 0:N_CMP]
                    st = stat[:, 8:16]

                    def row_of(x):
                        return x.unsqueeze(2).broadcast_to([P, TT * HPG, N_CMP])

                    dve.wait_ge(*written(n))
                    if g:
                        dve.wait_ge(*written(SIDE[("cmp_turn", g - 1)]))
                    dve.tensor_tensor(p4, logit4, add, ALU.add).then_inc(done, 1)
                    dve.wait_ge(*read(n))
                    then(dve.tensor_reduce(st, p3, AX, ALU.max))
                    dve.tensor_tensor(p3, p3, row_of(st), ALU.subtract).then_inc(head_max, 1)
                    dve.wait_ge(head_exp, MASKED[a] + 1)
                    then(dve.tensor_reduce(st, p3, AX, ALU.add))
                    then(dve.reciprocal(st, st))
                    then(dve.tensor_tensor(p4, p4, keep, ALU.mult))
                    dve.tensor_tensor(p3, p3, row_of(st), ALU.mult).then_inc(head_prob, 1)
                elif kind in ("cmp_values", "sel_values", "win_values"):
                    br = ("cmp", "sel", "win").index(kind[:3])
                    g = step[1] if br == 0 else step[1] // HPG
                    c = 3 * g + br
                    k = O_INDEX[step]
                    dve.wait_ge(*written(n))
                    if k == 0:
                        dve.wait_ge(*read(SIDE[("ngate_back", 0)]))
                    else:
                        dve.wait_ge(o_added, k)
                    for w in (emptied(B0["nz"] + 2 * c), emptied(B0["nz"] + 2 * c + 1)):
                        dve.wait_ge(*w)
                    if br == 0:
                        t = step[2]
                        head = gates[:, t, HPG * g:HPG * (g + 1)].unsqueeze(2).broadcast_to([P, HPG, P])
                        part = work[:, TMP[1], :]
                        dve.tensor_tensor(part.rearrange("p (h d) -> p h d", h=HPG),
                                          side_bank(n).rearrange("p (h d) -> p h d", h=HPG), head, ALU.mult).then_inc(done, 1)
                        dve.wait_ge(*read(n))
                        dve.tensor_tensor(o_tok[:, t, g * CHUNK:(g + 1) * CHUNK], part, zs[:, c % 2, t, :],
                                          ALU.mult).then_inc(o_added, 1)
                    else:
                        h = step[1]
                        part = work[:, TMP[1], 0:2 * P].rearrange("p (t d) -> p t d", t=TT)
                        gate = gates[:, :, br * NQ + h:br * NQ + h + 1].broadcast_to([P, TT, P])
                        at, o = (h % HPG) * P, o_tok[:, :, h * P:(h + 1) * P]
                        dve.tensor_tensor(part, side_bank(n)[:, 0:2 * P].rearrange("p (t d) -> p t d", t=TT), gate,
                                          ALU.mult).then_inc(done, 1)
                        dve.wait_ge(*read(n))
                        then(dve.tensor_tensor(part, part, zs[:, c % 2, :, at:at + P], ALU.mult))
                        dve.tensor_tensor(o, o, part, ALU.add).then_inc(o_added, 1)

            def unit(phase, u):
                if phase == "kvt" and u % 2 and u < 8:
                    j, b = u // 4, B0["kvt"] + u // 2
                    dve.wait_ge(*multiplied(phase, u))
                    g0 = 2 * (u // 2 % 2)
                    for half in range(2):
                        pe_ = cmp_pe[:, j, half * CMP_STRIDE:(half + 1) * CMP_STRIDE]
                        ins = dve.tensor_tensor(
                            cin[:, j, half, g0:g0 + 2, :].rearrange("p g (n r) -> p (g n) r", r=CMP_STRIDE),
                            stream_bank(b).rearrange("p (m r) -> p m r", r=CMP_STRIDE),
                            pe_.unsqueeze(1).broadcast_to([P, 2 * S // CMP_STRIDE, CMP_STRIDE]), ALU.add)
                    ins.then_inc(evacuated[b % 4], 1)
                elif phase == "rg" and u % 4 == 3:
                    c = u // 4
                    for t in range(TT):
                        dve.wait_ge(*emptied(B0[phase] + 2 * c + t))
                        yc = rv[:, t, c * CHUNK:(c + 1) * CHUNK]
                        dve.tensor_tensor(yc, yc, work[:, TMP[t], :], ALU.mult).then_inc(ret_gated, 1)
                elif phase == "fo1" and (u + 1) % (FF_PARTS[1] // KG) == 0:
                    dve.wait_ge(*multiplied(phase, u))
                    c = u // (FF_PARTS[1] // KG)
                    for t in range(TT):
                        b = B0[phase] + 2 * c + t
                        yc = y[:, t, c * CHUNK:(c + 1) * CHUNK]
                        dve.wait_ge(*emptied(B0["fo0"] + 2 * c + t))
                        dve.tensor_tensor(yc, stream_bank(b), yc, ALU.add).then_inc(evacuated[b % 4], 1)
                    for t in range(TT):
                        times_gain(1, c, t)
                elif phase == "wo" and u % 4 == 3:
                    for t in range(TT):
                        times_gain(0, u // 4, t)
                elif phase == "glu" and u % 2:
                    b = u // 2
                    sig = work[:, b % 4, :]
                    top_part, whole = both(zT[0], b), both(zT[1], b)
                    dve.wait_ge(glu_gate, b + 1)
                    then(dve.tensor_tensor(sig, sig, both(uT, b), ALU.mult))
                    then(dve.tensor_tensor(whole, whole, sig, ALU.mult))
                    then(dve.tensor_scalar(r32(top_part), whole, 1.0, None, ALU.mult))
                    dve.tensor_tensor(r32(whole), whole, as32(top_part), ALU.subtract).then_inc(evacuated[(B0["glu"] + b) % 4], 1)
                elif phase in ("so", "no") and u % 4 == 3:
                    add_gated(2 if phase == "so" else 3, phase, u // 4)

            def cut(g, i=None, per=0, per_hi=0):
                if g >= UNITS:
                    return
                if ORDER[g][1] == "cw":
                    dve.wait_ge(cut_done, 2 * g)
                    dve.nop().then_inc(cut_done, 2)
                    return
                for h in range(2):
                    cols = slice(h * HALF, (h + 1) * HALF)
                    slot = ring[:, g % RING, cols]
                    if ORDER[g][0] == "unit":
                        value = 2 * HI[g] - 1 + h
                        dve.wait_ge(hi_made, value if i is None else i * (2 * per_hi) + value)
                        dve.tensor_tensor(r32(slot), slot, as32(hi[:, g % RING, cols]), ALU.subtract).then_inc(cut_done, 1)
                        continue
                    _, piece, k = ORDER[g]
                    sums = sums_of(piece)[:, cols]
                    value = 16 * (g // RING + 1)
                    dve.wait_ge(landed[(2 * g + h) % (2 * RING)], value if i is None else i * (per // RING * 16) + value)
                    if k == 0 and i is not None:
                        dve.wait_ge(side_done, i * 4 + SIDE[("mod_turn", MIX_PIECE, 0)])
                    elif k == 0 and ("mod_turn", piece - 1, 3) in SIDE:
                        dve.wait_ge(*written(SIDE[("mod_turn", piece - 1, 3)]))
                    if k == 0 and piece in (5, 6):
                        dve.wait_ge(act_cut, sum(FF_PARTS[:piece - 4]))
                    dve.wait_ge(cut_done, 2 * g if i is None else i * (2 * per) + 2 * g)
                    if k == 0:
                        ins = dve.tensor_scalar(sums, slot, c_act[:, k:k + 1], None, ALU.mult)
                    else:
                        ins = dve.scalar_tensor_tensor(out=sums, in0=slot, scalar=c_act[:, k:k + 1], in1=sums,
                                                       op0=ALU.mult, op1=ALU.add)
                    ins.then_inc(cut_done, 1)

            def mod_vec(piece, c, n, i=None):
                k = slice(4 * c, 4 * c + 4)
                if i is None:
                    dve.wait_ge(*written(n))
                    dst, bias = modv[:, piece, k], vecs[:, V[PIECES[piece]], k]
                else:
                    dve.wait_ge(side_done, i * 4 + (n + 1))
                    dst = modv[:, bass.ds(i + piece, 1), k].rearrange("p a k -> p (a k)")
                    bias = vecs[:, bass.ds(i + V[PIECES[piece]], 1), k].rearrange("p a k -> p (a k)")
                dve.tensor_tensor(dst, side_bank(n)[:, 0:4], bias, ALU.add).then_inc(side_read[n % 4], 1)

            def steps(todo):
                for step in todo:
                    for x in visited(step):
                        cut(POS[x] + LEAD)
                    if step[0] == "unit":
                        unit(step[1], step[2])
                    elif step[0] in LOCAL:
                        if step[0] != "mod":
                            local(step)
                    else:
                        side(step)

            def times_gain(n, c, t):
                cols = slice(c * CHUNK, (c + 1) * CHUNK)
                dve.wait_ge(rows_landed, 16 * (n + 1))
                dve.wait_ge(res_squares, TT * (4 * n + c) + t + 1)
                did(dve.tensor_tensor(y[:, t, cols], y[:, t, cols], row[:, cols], ALU.mult))

            def add_branch(n):
                did.wait()
                then(dve.tensor_reduce(stat[:, 40:42], stat[:, 32:40].rearrange("p (t c) -> p t c", t=TT), AX, ALU.add))
                dve.tensor_scalar(stat[:, 40:42], stat[:, 40:42], 1.0 / D, EPS, ALU.mult, ALU.add).then_inc(res_mean, 1)
                dve.wait_ge(res_root, n + 1)
                then(dve.reciprocal(stat[:, 42:44], stat[:, 40:42]))
                if n == 0:
                    dve.wait_ge(x_again_landed, 16)
                for c in range(2):
                    cols = slice(c * (D // 2), (c + 1) * (D // 2))
                    for t in range(TT):
                        dve.scalar_tensor_tensor(out=xr[:, t, cols], in0=y[:, t, cols], scalar=stat[:, 42 + t:43 + t],
                                                 in1=xr[:, t, cols], op0=ALU.mult, op1=ALU.add).then_inc(res_added, 1)

            def add_gated(n, phase, c):
                tag = "s5" if phase == "so" else "nsa"
                gate = row if phase == "so" else nsa_row
                if c == 0:
                    if phase == "so":
                        dve.wait_ge(x_again_landed, 32)
                    for w in last_reads([SIDE[("gate", tag, j)] for j in range(4)]):
                        dve.wait_ge(*w)
                    for j in range(2):
                        dve.wait_ge(*written(SIDE[("gate", tag, 2 + j)]))
                dve.wait_ge(*multiplied(phase, 4 * c + 3))
                for t in range(TT):
                    b = B0[phase] + 2 * c + t
                    part, x = work[:, TMP[t], :], xr[:, t, c * CHUNK:(c + 1) * CHUNK]
                    if c:
                        dve.wait_ge(res_added, RES_ADDED["x2" if phase == "so" else "x3"] + TT * (c - 1) + t + 1)
                    dve.tensor_tensor(part, stream_bank(b), gate[:, c * CHUNK:(c + 1) * CHUNK],
                                      ALU.mult).then_inc(evacuated[b % 4], 1)
                    dve.wait_ge(*emptied(b))
                    dve.tensor_tensor(x, x, part, ALU.add).then_inc(res_added, 1)
                if phase == "no":
                    dve.wait_ge(final_row_landed, 16)
                    cols = slice(c * CHUNK, (c + 1) * CHUNK)
                    for t in range(TT):
                        dve.wait_ge(res_added, RES_ADDED["x3"] + TT * c + t + 1)
                        did(dve.tensor_tensor(y_out[:, t, cols], xr[:, t, cols], final_row[:, cols], ALU.mult))

            dve.wait_ge(consts_landed, 32)
            dve.wait_ge(consts_made, CONSTS_MADE)
            for t in range(TT):
                dve.wait_ge(mem_landed[t], 16)
            rms("mem", mem_in, mem_in)
            dve.wait_ge(act_ready, 1)
            cut(0)
            steps(MIXER[:KT // 2])
            cut(1)
            steps(MIXER[KT // 2:])
            with dve.Fori(0, MIX_LOOPS) as i:
                for step in MIX_BODY:
                    cut(POS[step] + LEAD, i, MIX_TURN, 80 // MIX_LOOPS)
                    if step[0] != "unit" or step[2] + 1 not in MIX_ENDS:
                        continue
                    m = MIX_ENDS.index(step[2] + 1)
                    c, br = divmod(m, 3)
                    b = B0["mix"] + 4 * m + 2
                    dve.wait_ge(units_done, i * (2 * MIX_TURN) + (2 * POS[step] + 2))
                    for t in range(TT):
                        dst = mixed[:, t, bass.ds((i * 2 + c) * CHUNK, CHUNK)]
                        gate = work[:, (m % 2) * 2 + t, :]
                        dve.wait_ge(evacuated[(b - 2 + t) % 4], i * 6 + ((b - 2 + t) // 4 + 1))
                        if br == 0:
                            dve.tensor_tensor(dst, stream_bank(b + t), gate, ALU.mult).then_inc(evacuated[(b + t) % 4], 1)
                        else:
                            dve.tensor_tensor(gate, stream_bank(b + t), gate, ALU.mult).then_inc(mix_part, 1)
                            dve.wait_ge(mix_part, i * 8 + (c * 4 + (br - 1) * 2 + t + 1))
                            dve.wait_ge(evacuated[(b - 4 + t) % 4], i * 6 + ((b - 4 + t) // 4 + 1))
                            dve.tensor_tensor(dst, dst, gate, ALU.add).then_inc(evacuated[(b + t) % 4], 1)
                for _, piece, c in MIX_TURNS:
                    mod_vec(piece, c, SIDE[("mod_turn", piece, c)], i)
            for w in last_banks("mix"):
                dve.wait_ge(*w)
            dve.nop().then_inc(mix_done, 1)
            steps(AFTER_MIX + OUT)
            for w in last_banks("wo"):
                dve.wait_ge(*w)
            add_branch(0)
            rms("x1", xr, xn)
            steps(BEFORE_FFN)
            tile0 = 0
            for part, tiles in enumerate(FF_PARTS):
                ff = f"ff{part}"
                with dve.Fori(0, tiles // 4) as i:
                    for u in range(8):
                        g = POS[("unit", ff, u)]
                        cut(g + LEAD, i, 8, 8)
                        if u % 2 == 0:
                            continue
                        k = u // 2
                        b = B0[ff] + k
                        top_part, low_part = (x[:, bass.ds(i * 4 + k, 1), :].rearrange("p a t -> p (a t)") for x in actT)
                        whole = work[:, k, S:2 * S]
                        dve.wait_ge(ff_gate, i * 4 + (tile0 + k + 1))
                        dve.tensor_tensor(whole, stream_bank(b)[:, S:2 * S], work[:, k, 0:S],
                                          ALU.mult).then_inc(evacuated[b % 4], 1)
                        dve.wait_ge(evacuated[b % 4], i + (b // 4 + 1))
                        dve.tensor_scalar(r32(top_part), whole, 1.0, None, ALU.mult).then_inc(act_hi, 1)
                        dve.wait_ge(act_hi, i * 4 + (tile0 + k + 1))
                        dve.tensor_tensor(r32(low_part), whole, as32(top_part), ALU.subtract).then_inc(act_cut, 1)
                tile0 += tiles
                steps(FFN_OUT[part])
            def modulation(row_, gain, scale, n):
                ins = dve.scalar_tensor_tensor(out=gains[:, row_, :], in0=modv[:, PIECES.index(scale), :], scalar=1.0,
                                               in1=vecs[:, V[gain], :], op0=ALU.add, op1=ALU.mult)
                ins.then_inc(mod_gain, 1) if n else did(ins)

            modulation(0, "norm0", "s5_scale", 1)
            add_branch(1)
            rms("x2", xr, xn)
            steps(BEFORE_S5)
            modulation(1, "kv_norm", "kv_scale", 0)
            modulation(2, "norm1", "nsa_scale", 1)
            n_pairs = SSM_BODY * PAIRS
            dve.nop().then_inc(ssm_prod, SSM_AHEAD)
            with dve.Fori(0, SSM_CHUNKS // SSM_BODY) as i:
                did.enter(i, n_pairs * 2)

                def table(t, cc, q):
                    return t[cc % 2][:, q * S:(q + 1) * S].unsqueeze(1).broadcast_to([P, 2, S])

                def products(cc, q):
                    p = cc * PAIRS + q
                    bank = flat2(side_bank(SSM_SIDE0 + p))
                    dve.wait_ge(side_done, i * n_pairs + (SSM_SIDE0 + p + 1))
                    dve.wait_ge(ssm_y, i * n_pairs + (p + 1))
                    did(dve.tensor_tensor(flat2(ssm_buf[q][0]), bank, table(cos_t, cc, q), ALU.mult))
                    dve.tensor_tensor(flat2(ssm_buf[q][1]), bank, table(sin_t, cc, q), ALU.mult).then_inc(ssm_prod, 1)

                def scans(cc, q):
                    p = cc * PAIRS + q
                    dve.wait_ge(ssm_rot, i * n_pairs + (p + 1))
                    col = s5[:, S_MAG, bass.ds(i * n_pairs + p, 1)]
                    for part in range(2):
                        z = ssm_buf[q][0][:, part * S:(part + 1) * S]
                        ins = dve.tensor_tensor_scan(z, col.broadcast_to([P, S]), z, 0.0, ALU.mult, ALU.add)
                    ins.then_inc(ssm_state, 1)

                def back(cc, q):
                    p = cc * PAIRS + q
                    dve.wait_ge(ssm_state, i * n_pairs + (p + 1))
                    did(dve.tensor_tensor(flat2(ssm_buf[q][1]), flat2(ssm_buf[q][0]), table(cos_t, cc, q), ALU.mult))
                    dve.tensor_tensor(flat2(ssm_buf[q][2]), flat2(ssm_buf[q][0]), table(sin_t, cc, q),
                                      ALU.mult).then_inc(ssm_back, 1)

                def skip(cc):
                    b = B0["sz"] + 2 * cc + 1
                    dve.wait_ge(ssm_y, i * n_pairs + (PAIRS * (cc + 1) + SSM_AHEAD))
                    dve.wait_ge(ssm_gelu, i * SSM_BODY + max(cc - 1 + SSM_GELU0, 1))
                    d_col = vecs[:, V["d_skip"], bass.ds(i * SSM_BODY + cc, 1)]
                    dve.scalar_tensor_tensor(out=work[:, TMP[cc % 2], 0:S],
                                             in0=uT[:, bass.ds(i * SSM_BODY + cc, 1), :].rearrange("p a t -> p (a t)"),
                                             scalar=d_col, in1=stream_bank(b)[:, 0:S], op0=ALU.mult,
                                             op1=ALU.add).then_inc(evacuated[b % 4], 1)

                for cc in range(SSM_BODY):
                    dve.wait_ge(ssm_trig, i * SSM_BODY + (cc + 1))
                    products(cc, 0)
                    products(cc, 1)
                    if cc:
                        skip(cc - 1)
                    for q in range(PAIRS):
                        scans(cc, q)
                        if q + 2 < PAIRS:
                            products(cc, q + 2)
                        back(cc, q)
                    cut(POS[("unit", "sz", cc)] + LEAD, i, SSM_BODY, SSM_BODY)
                skip(SSM_BODY - 1)
                did.leave(SSM_CHUNKS // SSM_BODY)
            dve.wait_ge(ssm_back, SSM_CHUNKS * PAIRS)
            dve.wait_ge(*written(SSM_SIDE0 + (SSM_CHUNKS + 1) * PAIRS - 1))
            for b in range(4):
                dve.nop().then_inc(side_read[b], SSM_CHUNKS + 1)
            for q in range(4):
                dve.wait_ge(y_hi, q + 1)
                dve.tensor_tensor(r32(yT[1][:, 4 * q:4 * q + 4, :]), uT[:, 4 * q:4 * q + 4, :], as32(yT[0][:, 4 * q:4 * q + 4, :]),
                                  ALU.subtract).then_inc(y_cut, 1)
            steps(S5_GLU + S5_OUT)
            rms("x3", xr, xn)
            dve.wait_ge(late_landed, 16)
            steps(NSA)
            steps(NSA_OUT)
            rms_scale("out")
            for t in range(TT):
                for half in range(2):
                    z = y_out[:, t, half * (D // 2):(half + 1) * (D // 2)]
                    dve.tensor_scalar(z, z, stat[:, 4 + t:5 + t], None, ALU.mult).then_inc(out_ready, 1)

        @block.gpsimd
        def _(pool):
            did = Steps(pool, pool_steps)

            pool.memset(ones[:, :], 1.0).then_inc(consts_made, 1)
            pool.memset(half_pi[:, :], float(np.pi / 2)).then_inc(consts_made, 1)
            pool.memset(round_up[:, :], ROUND).then_inc(consts_made, 1)
            pool.memset(round_back[:, :], -ROUND).then_inc(consts_made, 1)
            pool.memset(ikT, 0.0).then_inc(consts_made, 1)
            pool.memset(s5[:, :, :], 0.0).then_inc(consts_made, 1)

            f4 = frac_t.rearrange("p (q t) -> p q t", q=PAIRS)
            times = time_row.unsqueeze(1).broadcast_to([P, PAIRS, S])

            pool.wait_ge(s5_params, 1)
            for w in last_banks("su"):
                pool.wait_ge(*w)
            pool.tensor_tensor(f4, times, s5[:, S_TURN, 0:PAIRS].unsqueeze(2).broadcast_to([P, PAIRS, S]),
                               ALU.mult).then_inc(ssm_turns, 1)
            pool.wait_ge(ssm_whole, 1)
            pool.tensor_tensor(frac_t, frac_t, whole_t[0], ALU.subtract).then_inc(ssm_frac, 1)
            pool.wait_ge(ssm_trig, 1)
            pool.tensor_tensor(f4, times, s5[:, S_TURN, PAIRS:2 * PAIRS].unsqueeze(2).broadcast_to([P, PAIRS, S]),
                               ALU.mult).then_inc(ssm_turns, 1)
            n_pairs = SSM_BODY * PAIRS

            def c_times_factor(buf, states, count):
                c_re, c_im = (ssm_in[:, buf, SSM_B + k * P:SSM_B + (k + 1) * P].rearrange("p (q c) -> p q c", q=PAIRS)
                              for k in range(2))
                f_re, f_im, f_neg = (s5[:, r, states].unsqueeze(2).broadcast_to([P, PAIRS, 32])
                                     for r in (S_KRE, S_KIM, S_NKIM))
                k0, k1, k2 = (ssm_c[:, buf, k, :, :] for k in range(3))
                t0, t1 = (ssm_tmp[:, k * P:(k + 1) * P].rearrange("p (q c) -> p q c", q=PAIRS) for k in range(2))
                did(pool.tensor_tensor(t0, c_re, f_re, ALU.mult))
                did(pool.tensor_tensor(t1, c_im, f_im, ALU.mult))
                did.wait()
                did(pool.tensor_tensor(k0, t0, t1, ALU.subtract))
                did(pool.tensor_tensor(k1, t1, t0, ALU.subtract))
                did.wait()
                did(pool.tensor_tensor(t0, c_re, f_neg, ALU.mult))
                did(pool.tensor_tensor(t1, c_im, f_re, ALU.mult))
                did.wait()
                pool.tensor_tensor(k2, t0, t1, ALU.subtract).then_inc(ssm_cmul, 1)
                pool.wait_ge(ssm_cmul, count)

            pool.wait_ge(ssm_landed[0], 16)
            c_times_factor(0, slice(0, PAIRS), 1)
            with pool.Fori(0, SSM_CHUNKS // SSM_BODY) as i:
                did.enter(i, SSM_BODY * (6 + PAIRS))
                for cc in range(SSM_BODY):
                    for q in range(PAIRS):
                        p = cc * PAIRS + q
                        one, two = ssm_buf[q][0:2]
                        pool.wait_ge(ssm_prod, i * n_pairs + (p + 1 + SSM_AHEAD))
                        did(pool.tensor_tensor(one[:, 0:S], one[:, 0:S], two[:, S:2 * S], ALU.add))
                        pool.tensor_tensor(one[:, S:2 * S], one[:, S:2 * S], two[:, 0:S], ALU.subtract).then_inc(ssm_rot, 1)
                        if q == 1:
                            pool.wait_ge(ssm_whole, i * SSM_BODY + (cc + 2))
                            pool.tensor_tensor(frac_t, frac_t, whole_t[(cc + 1) % 2], ALU.subtract).then_inc(ssm_frac, 1)
                    pool.wait_ge(ssm_landed[(cc + 1) % 2], i * 32 + 16 * ((cc + 1) // 2 + 1))
                    c_times_factor((cc + 1) % 2, bass.ds(i * n_pairs + (cc + 1) * PAIRS, PAIRS), i * SSM_BODY + (cc + 2))
                    turn = s5[:, S_TURN, bass.ds(i * n_pairs + (cc + 2) * PAIRS, PAIRS)]
                    pool.wait_ge(ssm_trig, i * SSM_BODY + (cc + 2))
                    pool.tensor_tensor(f4, times, turn.unsqueeze(2).broadcast_to([P, PAIRS, S]),
                                       ALU.mult).then_inc(ssm_turns, 1)
                did.leave(SSM_CHUNKS // SSM_BODY)
            pool.wait_ge(*written(SIDE[("cmp_hidden", 1)]))
            pool.memset(v_blocks, 0.0).then_inc(v_zero, 1)



def t_units(w):
    k, n = w.shape
    return w.reshape(k // P, P, n // P, P).transpose(2, 1, 0, 3).reshape(n // P, P, -1)


def n_units(w):
    k, n = w.shape
    return w.reshape(k // (KG * P), KG, P, n // CHUNK, CHUNK).transpose(3, 0, 2, 1, 4).reshape(-1, P, UNIT)


def kernel(**inputs):
    import concourse.bacc as bacc
    from concourse.bass_utils import run_bass_kernel_spmd

    x = {n: np.asarray(a) for n, a in inputs.items()}
    f = np.float32

    w = x["w_in"][0]
    cols, at = {}, 0
    for name, n in (("aq", 1024), ("ak", 1024), ("av", 1024), ("iq", 1024), ("ik", 64), ("iw", 16), ("rq", 1024),
                    ("rk", 1024), ("rv", 2048), ("rg", 2048), ("mq", 1024), ("ga", D), ("gb", D), ("gc", D)):
        cols[name] = w[:, at:at + n]
        at += n
    mem_kv, kv = x["w_mem_kv"][0], x["w_kv_2"]
    qg = x["nsa_w_qg_2"][0]
    s_in = x["ssm_w_in_2"][0]
    ff = x["w_ffn_in"][0]
    mix = [n_units(cols["ga"]).reshape(4, 4, P, UNIT), n_units(x["w_branch_a"][0]).reshape(4, 2, P, UNIT),
           n_units(cols["gb"]).reshape(4, 4, P, UNIT), n_units(x["w_branch_b"][0]).reshape(4, 4, P, UNIT),
           n_units(cols["gc"]).reshape(4, 4, P, UNIT), n_units(x["w_branch_c"][0]).reshape(4, 2, P, UNIT)]
    gate_up = np.stack([t_units(ff[:, :FF_T * P]), t_units(ff[:, FF_T * P:])], 1).reshape(2 * FF_T, P, UNIT)
    kv_cols = kv.reshape(D, 6, NKV * HD)
    cw = x["cmp_w1_2"].reshape(2, 2, CMP_STRIDE, HD, HD).transpose(0, 1, 3, 2, 4).reshape(4, P, UNIT)
    z = qg[:, NQ * HD + 3 * NQ:].reshape(D, 3, NKV, HPG * HD).transpose(0, 2, 1, 3).reshape(D, 3 * NQ * HD)
    mod_w, kvm = x["mod_w_2"], x["kv_mod_w_2"]
    m = [a.reshape(KT, P, D) for a in (mod_w[0][:, D:2 * D], mod_w[0][:, :D], mod_w[0][:, 2 * D:], kvm[:, :D], kvm[:, D:],
                                       mod_w[1][:, :D], mod_w[1][:, D:2 * D], mod_w[1][:, 2 * D:])]
    fo = x["w_ffn_out"][0]
    split = FF_PARTS[0]
    phases = {
        "mk": t_units(mem_kv[:, :1024]), "mv": n_units(mem_kv[:, 1024:]), "mq": t_units(cols["mq"]),
        "ik": t_units(np.concatenate([cols["ik"], cols["ik"]], 1)), "iq": t_units(cols["iq"]), "aq": t_units(cols["aq"]),
        "av": n_units(cols["av"]), "ak": t_units(cols["ak"]), "rq": t_units(cols["rq"]), "rk": t_units(cols["rk"]),
        "rv": n_units(cols["rv"]), "rg": n_units(cols["rg"]), "mix": np.concatenate(mix, 1).reshape(-1, P, UNIT),
        "wo": n_units(x["w_out"][0]), "ff0": gate_up[:2 * split], "ff1": gate_up[2 * split:],
        "fo0": n_units(fo[:split * P]), "fo1": n_units(fo[split * P:]),
        "su": t_units(s_in[:, :D]), "sz": t_units(s_in[:, D:]), "glu": t_units(x["ssm_w_glu_2"][0]),
        "so": n_units(x["ssm_w_out_2"][0]), "kvt": t_units(kv_cols[:, [0, 1, 2, 4]].reshape(D, -1)), "cw": cw,
        "kvn": n_units(kv_cols[:, [3, 5]].reshape(D, -1)), "nq": t_units(qg[:, :NQ * HD]), "nz": n_units(z),
        "no": n_units(x["nsa_w_o_2"][0]),
    }
    stream = np.zeros((STREAM_UNITS, P, UNIT), f)
    for g, (kind, name, u) in enumerate(ORDER):
        stream[g] = phases[name][u] if kind == "unit" else m[name][u]
    mod_b, kvb = x["mod_b_2"], x["kv_mod_b_2"]
    biases = [mod_b[0][D:2 * D], mod_b[0][:D], mod_b[0][2 * D:], kvb[:D], kvb[D:], mod_b[1][:D], mod_b[1][D:2 * D],
              mod_b[1][2 * D:]]

    def on_partitions(v):
        return v.reshape(-1, P).T

    vec_rows = [x["g_pre_mix"][0], x["g_mem"][0], x["g_pre_ffn"][0], x["norm_g_2"][0], x["norm_g_2"][1],
                x["kv_norm_g_2"], x["c_2"][0], x["ssm_b_glu_2"][0], x["ssm_d_2"][0], *biases]

    pos = np.arange(S)
    tok = pos.reshape(TT, P).T
    causal = np.where(pos[None, None] <= tok[:, :, None], 0.0, NEG).astype(f)
    perms = np.zeros((P, 2, P), f)
    freq = np.zeros((P, 2), f)
    for k, d in enumerate((HD, 64)):
        for m in range(P):
            head, r = divmod(m, d)
            perms[head * d + (r + d // 2) % d, k, m] = -1.0 if r < d // 2 else 1.0
        fr = np.power(f(10000.0), (-np.arange(0, d, 2, dtype=f) / f(d)).astype(f)).astype(f)
        freq[:, k] = np.tile(np.concatenate([fr, fr]), P // d)
    log_gamma = np.log1p(-np.exp2(-5.0 - np.arange(N_RET)))
    gap = pos[None, :] - np.arange(P)[:, None]
    decay = np.where(gap[:, None] >= 0, np.exp(np.maximum(gap, 0)[:, None] * log_gamma[None, :, None]), 0.0) * HD ** -0.5
    ends = np.arange(N_CMP) * CMP_STRIDE + CMP_LEN - 1
    keep = (ends[None, None] <= tok[:, :, None])

    cst = np.concatenate([np.eye(P, dtype=f), causal.reshape(P, -1), np.broadcast_to(pos.astype(f), (P, S)),
                          np.concatenate([on_partitions(v) for v in vec_rows], 1), freq], 1)
    w_iw = cols["iw"].reshape(KT, P, N_IDX).transpose(1, 0, 2).reshape(P, -1)
    w_ng = qg[:, NQ * HD:NQ * HD + 3 * NQ].reshape(KT, P, 3 * NQ).transpose(1, 0, 2).reshape(P, -1)
    b1 = np.zeros((P, 2, HD), f)
    b1[0] = x["cmp_b1_2"]
    late = np.concatenate([
        w_ng, x["cmp_w2_2"].transpose(1, 0, 2).reshape(P, -1), b1.reshape(P, -1),
        np.broadcast_to(x["cmp_b2_2"][1], (P, HD)), x["cmp_pe_2"].transpose(2, 0, 1).reshape(P, -1),
        np.where(keep, 0.0, NEG).reshape(P, -1), keep.reshape(P, -1).astype(f), x["cmp_b2_2"][0][:, None]], 1)

    def states(a):
        return a.reshape(-1, P).T
    step = np.repeat(x["ssm_log_step_2"][0][:, None], 64, 1)
    s5_raw = np.stack([states(x["ssm_lam_re_2"][0]), states(x["ssm_lam_im_2"][0]), states(step)], 1)
    bc = np.zeros((SSM_CHUNKS + 1, P, SSM_COLS), f)
    bmat = bc[:SSM_CHUNKS, :, :SSM_B].reshape(SSM_CHUNKS, PAIRS, 2, 16, PAIRS, 2, 2, 64)
    cmat = np.zeros((SSM_CHUNKS, 2, 64, 2, PAIRS, 2, 16), f)
    for part, name in enumerate(("ssm_b_re_2", "ssm_b_im_2")):
        b = x[name][0].reshape(SSM_CHUNKS, PAIRS, 2, 64, 16)
        for q in range(PAIRS):
            for g in range(2):
                bmat[:, q, g, :, q, part, g, :] = b[:, q, g].transpose(0, 2, 1)
    bc[:SSM_CHUNKS, :, :SSM_B] = bmat.reshape(SSM_CHUNKS, P, SSM_B)
    for part, name in enumerate(("ssm_c_re_2", "ssm_c_im_2")):
        c = x[name][0].reshape(SSM_CHUNKS, PAIRS, 2, 16, 64)
        for g in range(2):
            cmat[:, g, :, part, :, g, :] = c[:, :, g].transpose(0, 3, 1, 2)
    bc[:SSM_CHUNKS, :, SSM_B:] = cmat.reshape(SSM_CHUNKS, P, SSM_C)

    arrays = {
        "stream": stream.reshape(-1, P, 2, HALF).transpose(0, 2, 1, 3).reshape(-1, P, HALF), "x": x["x"][0], "mem": x["mem"][0], "positions": x["positions"], "cst": cst,
        "early": np.concatenate([perms.reshape(P, -1), w_iw], 1), "late": late, "decay": decay.reshape(P, -1),
        "s5_raw": s5_raw, "ssm_bc": bc, "g_post_mix": x["g_post_mix"], "g_post_ffn": x["g_post_ffn"],
        "final_norm_g": x["final_norm_g_2"][None],
    }
    arrays = {n: np.ascontiguousarray(a if a.dtype.kind in "iu" else a.astype(f, copy=False)) for n, a in arrays.items()}
    nc = bacc.Bacc("TRN2", target_bir_lowering=False, num_devices=1)
    A = {n: nc.dram_tensor("in_" + n, a.shape, mybir.dt.from_np(a.dtype), kind="ExternalInput").ap() for n, a in arrays.items()}
    out = nc.dram_tensor("out_0", (S, D), F32, kind="ExternalOutput").ap()
    x_kept = nc.dram_tensor("x_kept", (S, D), F32, kind="Internal").ap()
    program(nc, A, out, x_kept)
    r = run_bass_kernel_spmd(nc, [{"in_" + n: a for n, a in arrays.items()}], core_ids=[0])
    return r.results[0]["out_0"].reshape(1, S, D)
```
